# Optimizing a Trainium2 kernel written in Bass

```python
import jax, jax.numpy as jnp
from jax import lax
import numpy as np

D_MODEL = 2048
BATCH = 1
SEQ = 256
DEPTH = 1

CHUNK = 64

D_MIX = D_MODEL
D_LRU = D_MIX // 2
D_POOL = D_MIX - D_LRU
LRU_HEADS = 16
LRU_HEAD_DIM = D_LRU // LRU_HEADS
CONV_WIDTH = 4
LRU_C = 8.0
POOL_WINDOWS = (2, 4, 8, 16)
POOL_GROUPS = len(POOL_WINDOWS)
POOL_GROUP_DIM = D_POOL // POOL_GROUPS
D_FF = ((8 * D_MODEL + 3 * 256 - 1) // (3 * 256)) * 256
N_MOD = 6
EPS = 1e-6


def rmsnorm(x, g):
    xf = x.astype(jnp.float32)
    y = xf * lax.rsqrt(jnp.mean(xf * xf, axis=-1, keepdims=True) + EPS)
    return (y * g.astype(jnp.float32)).astype(x.dtype)

def modulate(h, shift, scale):
    return h * (1 + scale[:, None, :]) + shift[:, None, :]

def causal_dwconv(x, w, b):
    y = lax.conv_general_dilated(
        x, w[:, None, :].astype(x.dtype), window_strides=(1,),
        padding=[(CONV_WIDTH - 1, 0)],
        dimension_numbers=("NWC", "WIO", "NWC"),
        feature_group_count=x.shape[-1])
    return y + b.astype(x.dtype)

def rg_lru(x, w_a, b_a, w_i, b_i, lam):
    bsz, seq, _ = x.shape
    xf = x.astype(jnp.float32)
    xh = xf.reshape(bsz, seq, LRU_HEADS, LRU_HEAD_DIM)
    r = jax.nn.sigmoid(jnp.einsum("bshi,hij->bshj", xh, w_a.astype(jnp.float32)).reshape(bsz, seq, D_LRU)
                       + b_a.astype(jnp.float32))
    i = jax.nn.sigmoid(jnp.einsum("bshi,hij->bshj", xh, w_i.astype(jnp.float32)).reshape(bsz, seq, D_LRU)
                       + b_i.astype(jnp.float32))
    log_a = LRU_C * r * jax.nn.log_sigmoid(lam.astype(jnp.float32))
    a = jnp.exp(log_a)
    mult = jnp.sqrt(-jnp.expm1(2.0 * log_a))
    u = mult * (i * xf)

    def combine(left, right):
        a1, b1 = left
        a2, b2 = right
        return a1 * a2, a2 * b1 + b2

    _, h = lax.associative_scan(combine, (a, u), axis=1)
    return h

def pool_mixer(x, w_pool, ls_pool):
    bsz, seq, _ = x.shape
    xf = x.astype(jnp.float32)
    cs0 = jnp.concatenate([jnp.zeros((bsz, 1, D_POOL), jnp.float32), jnp.cumsum(xf, axis=1)], axis=1)
    pos1 = jnp.arange(1, seq + 1, dtype=jnp.float32)
    outs = []
    for g, w in enumerate(POOL_WINDOWS):
        sl = slice(g * POOL_GROUP_DIM, (g + 1) * POOL_GROUP_DIM)
        c0 = cs0[..., sl]
        upper = c0[:, 1:]
        lower = jnp.concatenate([jnp.zeros((bsz, w - 1, POOL_GROUP_DIM), jnp.float32),
                                 c0[:, :seq - w + 1]], axis=1)
        count = jnp.minimum(pos1, float(w))[None, :, None]
        outs.append((upper - lower) / count - xf[..., sl])
    pooled = jnp.stack(outs, axis=2)
    y = jnp.einsum("bsgc,gcd->bsgd", pooled, w_pool.astype(jnp.float32)) * ls_pool.astype(jnp.float32)
    return y.reshape(bsz, seq, D_POOL)

def first_inputs(seed: int = 0) -> dict:
    key = jax.random.key(seed)
    ks = jax.random.split(key, 24)
    f32 = jnp.float32
    nrm = lambda k, shape, s: jax.random.normal(k, shape, f32) * s
    a0 = jax.random.uniform(ks[12], (DEPTH, D_LRU), f32, 0.9, 0.999)
    s0 = a0 ** (1.0 / LRU_C)
    lam = jnp.log(s0) - jnp.log1p(-s0)
    return {
        "x": nrm(ks[0], (BATCH, SEQ, D_MODEL), 1.0),
        "c": nrm(ks[1], (BATCH, D_MODEL), 1.0),
        "w_ada": nrm(ks[2], (DEPTH, D_MODEL, N_MOD * D_MODEL), 0.5 * D_MODEL ** -0.5),
        "b_ada": nrm(ks[3], (DEPTH, N_MOD * D_MODEL), 0.02),
        "g_norm_mix": 1.0 + nrm(ks[4], (DEPTH, D_MODEL), 0.05),
        "w_in": nrm(ks[5], (DEPTH, D_MODEL, 2 * D_LRU + D_POOL), D_MODEL ** -0.5),
        "w_conv": nrm(ks[6], (DEPTH, CONV_WIDTH, D_LRU), CONV_WIDTH ** -0.5),
        "b_conv": nrm(ks[7], (DEPTH, D_LRU), 0.02),
        "w_rg_a": nrm(ks[8], (DEPTH, LRU_HEADS, LRU_HEAD_DIM, LRU_HEAD_DIM), LRU_HEAD_DIM ** -0.5),
        "b_rg_a": nrm(ks[9], (DEPTH, D_LRU), 0.02),
        "w_rg_i": nrm(ks[10], (DEPTH, LRU_HEADS, LRU_HEAD_DIM, LRU_HEAD_DIM), LRU_HEAD_DIM ** -0.5),
        "b_rg_i": nrm(ks[11], (DEPTH, D_LRU), 0.02),
        "lru_lambda": lam,
        "w_pool": nrm(ks[13], (DEPTH, POOL_GROUPS, POOL_GROUP_DIM, POOL_GROUP_DIM), POOL_GROUP_DIM ** -0.5),
        "ls_pool": 1.0 + nrm(ks[14], (DEPTH, POOL_GROUPS, POOL_GROUP_DIM), 0.1),
        "w_out": nrm(ks[15], (DEPTH, D_MIX, D_MODEL), D_MIX ** -0.5),
        "g_norm_ffn": 1.0 + nrm(ks[16], (DEPTH, D_MODEL), 0.05),
        "w_ffn_gate": nrm(ks[17], (DEPTH, D_MODEL, D_FF), D_MODEL ** -0.5),
        "w_ffn_up": nrm(ks[18], (DEPTH, D_MODEL, D_FF), D_MODEL ** -0.5),
        "w_ffn_down": nrm(ks[19], (DEPTH, D_FF, D_MODEL), D_FF ** -0.5),
        "g_norm_final": 1.0 + nrm(ks[20], (D_MODEL,), 0.05),
    }

def first_block(x, c, w_ada, b_ada, g_norm_mix, w_in, w_conv, b_conv, w_rg_a, b_rg_a,
              w_rg_i, b_rg_i, lru_lambda, w_pool, ls_pool, w_out, g_norm_ffn,
              w_ffn_gate, w_ffn_up, w_ffn_down, g_norm_final):
    dt = x.dtype
    c_act = jax.nn.silu(c)
    for l in range(DEPTH):
        mod = c_act @ w_ada[l] + b_ada[l]
        sh1, sc1, gt1, sh2, sc2, gt2 = jnp.split(mod, N_MOD, axis=-1)

        h = modulate(rmsnorm(x, g_norm_mix[l]), sh1, sc1)
        proj = h @ w_in[l]
        xr = proj[..., :D_LRU]
        gr = proj[..., D_LRU:2 * D_LRU]
        xp = proj[..., 2 * D_LRU:]
        xr = causal_dwconv(xr, w_conv[l], b_conv[l])
        hr = rg_lru(xr, w_rg_a[l], b_rg_a[l], w_rg_i[l], b_rg_i[l], lru_lambda[l])
        y_lru = (hr * jax.nn.gelu(gr.astype(jnp.float32))).astype(dt)
        y_pool = pool_mixer(xp, w_pool[l], ls_pool[l]).astype(dt)
        y = jnp.concatenate([y_lru, y_pool], axis=-1) @ w_out[l]
        x = x + gt1[:, None, :] * y

        h = modulate(rmsnorm(x, g_norm_ffn[l]), sh2, sc2)
        f = (jax.nn.silu(h @ w_ffn_gate[l]) * (h @ w_ffn_up[l])) @ w_ffn_down[l]
        x = x + gt2[:, None, :] * f
    return rmsnorm(x, g_norm_final)


PLE_DIM = 256

SSM_HEAD_DIM = 64
SSM_INNER = D_MODEL
SSM_HEADS = SSM_INNER // SSM_HEAD_DIM
SSM_GROUPS = 4
SSM_STATE = 128
SSM_CONV = 4
SSM_CHUNK = 128
SSM_HPG = SSM_HEADS // SSM_GROUPS
SSM_CONV_CH = SSM_INNER + 2 * SSM_GROUPS * SSM_STATE

ATT_HEAD_DIM = 64
ATT_HEADS = D_MODEL // ATT_HEAD_DIM
ATT_KV_HEADS = ATT_HEADS // 4
ATT_REP = ATT_HEADS // ATT_KV_HEADS
ATT_INNER = ATT_HEADS * ATT_HEAD_DIM
ATT_KV_DIM = ATT_KV_HEADS * ATT_HEAD_DIM
WINDOW = 128
ROPE_THETA = 500000.0
ROPE_DIM = ATT_HEAD_DIM // 4

MIX_WIDTH = SSM_INNER + ATT_INNER
IN_WIDTH = SSM_INNER + SSM_CONV_CH + SSM_HEADS + ATT_INNER + 2 * ATT_KV_DIM

D_FF_2 = 256 * ((8 * D_MODEL // 3 + 255) // 256)
FFN_CONV = 3


def _rmsnorm(x, g):
    xf = x.astype(jnp.float32)
    y = xf * lax.rsqrt(jnp.mean(xf * xf, axis=-1, keepdims=True) + EPS)
    return (y * g.astype(jnp.float32)).astype(x.dtype)

def _causal_dwconv(x, w, b):
    k = w.shape[0]
    y = lax.conv_general_dilated(x, w[:, None, :].astype(x.dtype), window_strides=(1,),
                                 padding=[(k - 1, 0)],
                                 dimension_numbers=('NWC', 'WIO', 'NWC'),
                                 feature_group_count=x.shape[-1])
    return y + b.astype(x.dtype)

def _ssd(xs, dt, a, bm, cm):
    b, s = xs.shape[0], xs.shape[1]
    nc, L = s // SSM_CHUNK, SSM_CHUNK
    G, E, P, N = SSM_GROUPS, SSM_HPG, SSM_HEAD_DIM, SSM_STATE
    X = (xs.astype(jnp.float32) * dt[..., None]).reshape(b, nc, L, G, E, P)
    a_dt = (dt * a).reshape(b, nc, L, G, E).transpose(0, 3, 4, 1, 2)
    Bc = bm.astype(jnp.float32).reshape(b, nc, L, G, N)
    Cc = cm.astype(jnp.float32).reshape(b, nc, L, G, N)
    a_cs = jnp.cumsum(a_dt, axis=-1)
    tril = jnp.tril(jnp.ones((L, L), dtype=bool))
    seg = a_cs[..., :, None] - a_cs[..., None, :]
    decay_in = jnp.exp(jnp.where(tril, seg, -jnp.inf))
    cb = jnp.einsum('bclgn,bcsgn->bgcls', Cc, Bc)
    y_diag = jnp.einsum('bgecls,bcsgep->bclgep', cb[:, :, None] * decay_in, X)
    decay_states = jnp.exp(a_cs[..., -1:] - a_cs)
    states = jnp.einsum('bclgn,bgecl,bclgep->bcgepn', Bc, decay_states, X)
    chunk_decay = jnp.exp(a_cs[..., -1])

    def step(h, inp):
        st, d = inp
        return h * d[..., None, None] + st, h

    h0 = jnp.zeros((b, G, E, P, N), jnp.float32)
    _, prev = lax.scan(step, h0, (jnp.moveaxis(states, 1, 0), jnp.moveaxis(chunk_decay, -1, 0)))
    prev = jnp.moveaxis(prev, 0, 1)
    y_off = jnp.einsum('bclgn,bcgepn,bgecl->bclgep', Cc, prev, jnp.exp(a_cs))
    return (y_diag + y_off).reshape(b, s, SSM_HEADS, P)

def _partial_rope(t, cos, sin):
    half = ROPE_DIM // 2
    t1, t2 = t[..., :half], t[..., half:ROPE_DIM]
    return jnp.concatenate([t1 * cos - t2 * sin, t2 * cos + t1 * sin, t[..., ROPE_DIM:]], axis=-1)

def _swa_sinks(q, k, v, sinks):
    b, s = q.shape[0], q.shape[1]
    blk = WINDOW
    nb = s // blk
    scale = ATT_HEAD_DIM ** -0.5
    qb = q.astype(jnp.float32).reshape(b, nb, blk, ATT_KV_HEADS, ATT_REP, ATT_HEAD_DIM)

    def band(t):
        tp = jnp.pad(t.astype(jnp.float32), ((0, 0), (blk, 0), (0, 0), (0, 0)))
        tp = tp.reshape(b, nb + 1, blk, ATT_KV_HEADS, ATT_HEAD_DIM)
        return jnp.concatenate([tp[:, :-1], tp[:, 1:]], axis=2)

    kb, vb = band(k), band(v)
    sc = jnp.einsum('bnqhrd,bnkhd->bnhrqk', qb, kb) * scale
    qi = jnp.arange(blk)[:, None]
    kj = jnp.arange(2 * blk)[None, :]
    diff = qi + blk - kj
    in_band = (diff >= 0) & (diff < WINDOW)
    valid = (jnp.arange(nb)[:, None] * blk + kj - blk) >= 0
    mask = in_band[None] & valid[:, None, :]
    sc = jnp.where(mask[None, :, None, None], sc, -jnp.inf)
    sink = sinks.astype(jnp.float32).reshape(ATT_KV_HEADS, ATT_REP)[None, None, :, :, None, None]
    m = jnp.maximum(jnp.max(sc, axis=-1, keepdims=True), sink)
    e = jnp.exp(sc - m)
    pr = e / (jnp.sum(e, axis=-1, keepdims=True) + jnp.exp(sink - m))
    o = jnp.einsum('bnhrqk,bnkhd->bnqhrd', pr, vb)
    return o.reshape(b, s, ATT_INNER).astype(q.dtype)

def second_inputs(seed: int = 0) -> dict:
    key = jax.random.key(seed)
    ks = jax.random.split(key, 24)
    f32 = jnp.float32
    nrm = lambda k, shape, sc: jax.random.normal(k, shape, f32) * sc
    gain = lambda k, shape: 1.0 + 0.02 * jax.random.normal(k, shape, f32)
    dt0 = jnp.exp(jax.random.uniform(ks[5], (DEPTH, SSM_HEADS), f32) * (np.log(0.1) - np.log(0.001)) + np.log(0.001))
    return {
        'x': nrm(ks[0], (BATCH, SEQ, D_MODEL), 1.0),
        'p': nrm(ks[1], (DEPTH, BATCH, SEQ, PLE_DIM), 1.0),
        'positions': jnp.broadcast_to(jnp.arange(SEQ, dtype=jnp.int32)[None, :], (BATCH, SEQ)),
        'attn_norm_g': gain(ks[2], (DEPTH, D_MODEL)),
        'w_in': nrm(ks[3], (DEPTH, D_MODEL, IN_WIDTH), D_MODEL ** -0.5),
        'conv_w': nrm(ks[4], (DEPTH, SSM_CONV, SSM_CONV_CH), SSM_CONV ** -0.5),
        'conv_b': nrm(ks[6], (DEPTH, SSM_CONV_CH), 0.02),
        'dt_bias': dt0 + jnp.log(-jnp.expm1(-dt0)),
        'a_log': jnp.log(jax.random.uniform(ks[7], (DEPTH, SSM_HEADS), f32, 1.0, 16.0)),
        'd_skip': gain(ks[8], (DEPTH, SSM_HEADS)),
        'ssm_norm_g': gain(ks[9], (DEPTH, SSM_INNER)),
        'q_norm_g': gain(ks[10], (DEPTH, ATT_HEAD_DIM)),
        'k_norm_g': gain(ks[11], (DEPTH, ATT_HEAD_DIM)),
        'sinks': nrm(ks[12], (DEPTH, ATT_HEADS), 0.5),
        'w_out': nrm(ks[13], (DEPTH, MIX_WIDTH, D_MODEL), MIX_WIDTH ** -0.5),
        'ffn_norm_g': gain(ks[14], (DEPTH, D_MODEL)),
        'w_up': nrm(ks[15], (DEPTH, D_MODEL, 2 * D_FF_2), D_MODEL ** -0.5),
        'ffn_conv_w': nrm(ks[16], (DEPTH, FFN_CONV, 2 * D_FF_2), FFN_CONV ** -0.5),
        'ffn_conv_b': nrm(ks[17], (DEPTH, 2 * D_FF_2), 0.02),
        'w_down': nrm(ks[18], (DEPTH, D_FF_2, D_MODEL), D_FF_2 ** -0.5),
        'ple_norm_g': gain(ks[19], (DEPTH, D_MODEL)),
        'w_ple_gate': nrm(ks[20], (DEPTH, D_MODEL, D_MODEL), D_MODEL ** -0.5),
        'w_ple_proj': nrm(ks[21], (DEPTH, PLE_DIM, D_MODEL), PLE_DIM ** -0.5),
        'ple_post_g': gain(ks[22], (DEPTH, D_MODEL)),
    }

def second_block(x, p, positions, attn_norm_g, w_in, conv_w, conv_b, dt_bias, a_log, d_skip,
              ssm_norm_g, q_norm_g, k_norm_g, sinks, w_out, ffn_norm_g, w_up, ffn_conv_w,
              ffn_conv_b, w_down, ple_norm_g, w_ple_gate, w_ple_proj, ple_post_g):
    b, s = x.shape[0], x.shape[1]
    inv_freq = ROPE_THETA ** (-jnp.arange(0, ROPE_DIM, 2, dtype=jnp.float32) / ROPE_DIM)
    ang = positions.astype(jnp.float32)[..., None] * inv_freq
    cos = jnp.cos(ang)[:, :, None, :].astype(x.dtype)
    sin = jnp.sin(ang)[:, :, None, :].astype(x.dtype)
    o1 = SSM_INNER
    o2 = o1 + SSM_CONV_CH
    o3 = o2 + SSM_HEADS
    o4 = o3 + ATT_INNER
    o5 = o4 + ATT_KV_DIM
    h = x
    for i in range(DEPTH):
        a_in = _rmsnorm(h, attn_norm_g[i])
        proj = a_in @ w_in[i]
        z, xbc, dt_raw, q, k, v = jnp.split(proj, [o1, o2, o3, o4, o5], axis=-1)
        xbc = jax.nn.silu(_causal_dwconv(xbc, conv_w[i], conv_b[i]))
        xs, bm, cm = jnp.split(xbc, [SSM_INNER, SSM_INNER + SSM_GROUPS * SSM_STATE], axis=-1)
        dt = jax.nn.softplus(dt_raw.astype(jnp.float32) + dt_bias[i].astype(jnp.float32))
        a_neg = -jnp.exp(a_log[i].astype(jnp.float32))
        xs_h = xs.reshape(b, s, SSM_HEADS, SSM_HEAD_DIM)
        y = _ssd(xs_h, dt, a_neg, bm.reshape(b, s, SSM_GROUPS, SSM_STATE),
                 cm.reshape(b, s, SSM_GROUPS, SSM_STATE))
        y = y + d_skip[i].astype(jnp.float32)[:, None] * xs_h.astype(jnp.float32)
        y = y.reshape(b, s, SSM_INNER) * jax.nn.silu(z.astype(jnp.float32))
        y_ssm = _rmsnorm(y.reshape(b, s, SSM_GROUPS, SSM_INNER // SSM_GROUPS),
                         ssm_norm_g[i].reshape(SSM_GROUPS, SSM_INNER // SSM_GROUPS))
        y_ssm = y_ssm.reshape(b, s, SSM_INNER).astype(h.dtype)
        qh = _rmsnorm(q.reshape(b, s, ATT_HEADS, ATT_HEAD_DIM), q_norm_g[i])
        kh = _rmsnorm(k.reshape(b, s, ATT_KV_HEADS, ATT_HEAD_DIM), k_norm_g[i])
        qh = _partial_rope(qh, cos, sin)
        kh = _partial_rope(kh, cos, sin)
        vh = v.reshape(b, s, ATT_KV_HEADS, ATT_HEAD_DIM)
        y_att = _swa_sinks(qh, kh, vh, sinks[i])
        h = h + jnp.concatenate([y_ssm, y_att], axis=-1) @ w_out[i]
        u = _rmsnorm(h, ffn_norm_g[i]) @ w_up[i]
        u = _causal_dwconv(u, ffn_conv_w[i], ffn_conv_b[i])
        g_ff, u_ff = jnp.split(u, [D_FF_2], axis=-1)
        h = h + (jax.nn.silu(g_ff) * u_ff) @ w_down[i]
        gate = jax.nn.sigmoid(_rmsnorm(h, ple_norm_g[i]) @ w_ple_gate[i])
        pe = _rmsnorm(p[i] @ w_ple_proj[i], ple_post_g[i])
        h = h + gate * pe
    return h


def setup_inputs(seed=0):
    out = dict(first_inputs(seed))
    for name, value in second_inputs(seed + 1).items():
        if name != "x":
            out[name + "_2"] = value
    return out


def reference(
    x, c, w_ada, b_ada, g_norm_mix, w_in, w_conv, b_conv, w_rg_a, b_rg_a, w_rg_i, b_rg_i,
    lru_lambda, w_pool, ls_pool, w_out, g_norm_ffn, w_ffn_gate, w_ffn_up, w_ffn_down,
    g_norm_final, p_2, positions_2, attn_norm_g_2, w_in_2, conv_w_2, conv_b_2, dt_bias_2,
    a_log_2, d_skip_2, ssm_norm_g_2, q_norm_g_2, k_norm_g_2, sinks_2, w_out_2, ffn_norm_g_2,
    w_up_2, ffn_conv_w_2, ffn_conv_b_2, w_down_2, ple_norm_g_2, w_ple_gate_2, w_ple_proj_2,
    ple_post_g_2,
):
    x = first_block(
        x, c, w_ada, b_ada, g_norm_mix, w_in, w_conv, b_conv, w_rg_a, b_rg_a, w_rg_i, b_rg_i,
        lru_lambda, w_pool, ls_pool, w_out, g_norm_ffn, w_ffn_gate, w_ffn_up, w_ffn_down,
        g_norm_final,
    )
    return second_block(
        x, p_2, positions_2, attn_norm_g_2, w_in_2, conv_w_2, conv_b_2, dt_bias_2, a_log_2,
        d_skip_2, ssm_norm_g_2, q_norm_g_2, k_norm_g_2, sinks_2, w_out_2, ffn_norm_g_2, w_up_2,
        ffn_conv_w_2, ffn_conv_b_2, w_down_2, ple_norm_g_2, w_ple_gate_2, w_ple_proj_2,
        ple_post_g_2,
    )


_drawn_inputs = setup_inputs


def setup_inputs(seed=0):
    import zlib

    import numpy as np

    out = dict(_drawn_inputs(seed))
    spreads = {}
    factors = {'g_norm_mix': 3.171,
     'b_conv': 3.867,
     'b_rg_a': 8.0,
     'b_rg_i': 8.0,
     'g_norm_ffn': 3.202,
     'attn_norm_g_2': 3.17,
     'conv_b_2': 3.569,
     'd_skip_2': 54.536,
     'ssm_norm_g_2': 4.747,
     'q_norm_g_2': 8.0,
     'k_norm_g_2': 8.0,
     'sinks_2': 53.798,
     'ffn_norm_g_2': 4.731,
     'ffn_conv_b_2': 4.805,
     'ple_norm_g_2': 64.0,
     'ple_post_g_2': 61.712}
    for name, (base, spread) in spreads.items():
        noise = np.random.default_rng([zlib.crc32(name.encode()), seed]).standard_normal(out[name].shape)
        drawn = base * np.exp(spread * noise) if base else spread * noise
        out[name] = __import__('jax').numpy.asarray(drawn.astype(out[name].dtype))
    for name, factor in factors.items():
        out[name] = (out[name] * factor).astype(out[name].dtype)
    return out
```

```python
from contextlib import ExitStack

import numpy as np

import concourse.bass as bass
from concourse import mybir

F32 = mybir.dt.float32
F32R = mybir.dt.float32r
I32 = mybir.dt.int32
ALU = mybir.AluOpType
ACT = mybir.ActivationFunctionType
AX = mybir.AxisListType

P = 128
KB = 1024
EPS = 1e-6
COLS = 512
RAW_SLOTS = 4
HALF_SLOTS = 4
LEAD = 4
CONV = 4
FFN_CONV = 3
LRU_C = 8.0
POOL_WINDOWS = (2, 4, 8, 16)
ROPE_THETA = 500000.0
HALF_ROPE = 8
MASKED = -1e30
ROUND = 12582912.0
TWO_PI_1 = 6.28125
TWO_PI_2 = float(np.float32(np.round((2 * np.pi - TWO_PI_1) * 2.0**20) / 2.0**20))
TWO_PI_3 = float(np.float32(2 * np.pi - TWO_PI_1 - TWO_PI_2))


class Phase:

    def __init__(self, before, blocks, rows, dmas=1, landed0=0):
        self.blocks, self.rows = blocks, rows
        self.tiles, self.halves = len(rows), 2 * len(rows)
        self.tile0 = before.tile0 + before.blocks * before.tiles if before else 0
        self.landed0 = before.landed1 if before else landed0
        self.unit = 16 * dmas
        self.landed1 = self.landed0 + self.unit * blocks * self.tiles // RAW_SLOTS
        assert self.tiles % RAW_SLOTS == 0 and blocks % 2 == 0
        self.row0 = [sum(rows[:j]) for j in range(self.tiles)]

    def half(self, b):
        return b * self.halves + 2 * self.tile0

    def end(self, b):
        return b * self.halves + (2 * self.tile0 + self.halves)

    def tile(self, b):
        return b * self.tiles + self.tile0

    def landed(self, b, j):
        return b * (self.unit * self.tiles // RAW_SLOTS) + (self.landed0 + self.unit * (j // RAW_SLOTS + 1))

    def half_rows(self, h):
        rows = self.rows[h // 2]
        first = (rows + 1) // 2
        return (0, self.row0[h // 2], first) if h % 2 == 0 else (first, self.row0[h // 2] + first, rows - first)


def two_blocks(nc, d, out):
    S, D = d["x"].shape[1:]
    T, KC = S // P, D // P
    HC = d["w_ffn_gate"].shape[2] // P
    RC = d["w_conv"].shape[2] // P
    MODS = d["w_ada"].shape[2] // D
    G = d["w_pool"].shape[1]
    HEADS, HD = d["sinks_2"].shape[1], d["q_norm_g_2"].shape[1]
    KV = HEADS // 4
    SH, SG = d["dt_bias_2"].shape[1], 4
    SP = D // SH
    XBC = d["conv_b_2"].shape[1] // P
    PLE = d["p_2"].shape[3]
    O_XBC = D
    O_DT = O_XBC + XBC * P
    O_Q = O_DT + SH
    O_K = O_Q + D
    O_V = O_K + KV * HD
    assert T == 2 and HEADS == SH == 32 and HD == SP == 64 and RC == 8 and G == 4 and KV == 8

    four = [4] * 4
    down_rows = [4] * 8 + [3] * 4
    assert sum(down_rows) == HC and sum(four) == KC
    MOD_BLOCKS = MODS * D // COLS
    MOD_TILES = MOD_BLOCKS * 4
    w_in = Phase(None, 6, four, landed0=16 * MOD_TILES // RAW_SLOTS)
    w_out = Phase(w_in, 4, four)
    up1 = Phase(w_out, HC // 2, four, dmas=2)
    down1 = Phase(up1, 4, down_rows)
    w_in2 = Phase(down1, 16, four)
    w_out2 = Phase(w_in2, 4, [4] * 8)
    up2 = Phase(w_out2, HC // 2, four, dmas=2)
    down2 = Phase(up2, 4, down_rows)
    ple_gate = Phase(down2, 4, four)
    w_in_cols = [0, COLS, 2 * RC * P, 2 * RC * P + COLS, RC * P, RC * P + COLS]
    w_in2_cols = [O_Q + COLS * j for j in range(4)] + [O_K, O_V] + [O_XBC + COLS * j for j in range(6)] \
        + [COLS * j for j in range(4)]
    B_K, B_V, B_XBC, B_Z = 4, 5, 6, 12

    with ExitStack() as ctx:
        size = 222 * KB
        base = -(-nc.sbuf_base // 64) * 64
        ctx.enter_context(nc.sbuf_tensor("arena", [P, size // 4], F32, align_bytes=64))
        assert nc.sbuf_base == base + size

        def at(name, kb, shape, dtype=F32):
            assert kb * KB + 4 * int(np.prod(shape[1:])) <= size, name
            return nc.alloc_sbuf_tensor_at(name, shape, dtype, offset=base + int(kb * KB))

        def sem(name):
            return ctx.enter_context(nc.semaphore(name))

        raw = at("raw", 0, [P, RAW_SLOTS, 4, COLS])
        w_hi = at("w_hi", 32, [P, HALF_SLOTS, 2, COLS], F32R)
        w_lo = at("w_lo", 48, [P, HALF_SLOTS, 2, COLS], F32R)
        x = at("x_res", 64, [P, T, D])
        a_hi = at("a_hi", 80, [P, KC, S], F32R)
        a_lo = at("a_lo", 96, [P, KC, S], F32R)
        R = 112
        row = at("row", R, [P, D])
        lru_den = at("lru_den", R, [P, RC, S])
        page = at("page", R, [P, D])
        state = at("state", R, [P, SH, SP])
        C = 120
        ident = at("ident", C, [P, P])
        ones = at("ones", C + 0.5, [P, P])
        upper = at("upper", C + 1, [P, P])
        a_mask = at("a_mask", C + 1.5, [P, 3 * P])
        vec = at("vec", C + 3, [P, 7, P])
        mod = at("mod", C + 6.5, [P, MODS * KC])
        pos_i = at("pos_i", C + 6.9375, [P, T], I32)
        rows = at("rows", C + 7, [P, 256])
        keep = at("keep", C + 8, [P, 512])
        F = 130
        xn = at("xn", F, [P, T, D])
        hf = at("hf", F + 16, [P, KC, S])
        vec_rows = at("vec_rows", F + 52, [P, 7, P])
        mod_acc = at("mod_acc", F + 56, [P, 2, 4, COLS])
        xc = at("xc", F, [P, RC, S])
        lru_a = at("lru_a", F + 8, [P, RC, S])
        lru_u = at("lru_u", F + 16, [P, RC, S])
        y_mix = at("y_mix", F + 24, [P, 2 * RC, S])
        lru_m = at("lru_m", F + 40, [P, RC, S])
        xp = at("xp", F + 48, [P, RC, S])
        gates_w = at("gates_w", F + 56, [P, 2, RC, P])
        pool_w = at("pool_w", F + 64, [P, 2 * G, 2 * P])
        pool_a = at("pool_a", F + 72, [P, RC, S])
        pool_b = at("pool_b", F + 80, [P, RC, S])
        res_tmp = at("res_tmp", F + 88, [P, T, COLS])
        hid_hi = at("hid_hi", F, [P, HC, S], F32R)
        hid_lo = at("hid_lo", F + 44, [P, HC, S], F32R)
        ff_g = at("ff_g", F + 88, [P, 2, S])
        ff_u = at("ff_u", F + 90, [P, 2, S])
        k_t = at("k_t", F, [P, T, KV, HD])
        v_t = at("v_t", F + 4, [P, T, KV, HD])
        k_two = at("k_two", F + 8, [P, T, KV, 2, HD])
        p_tr = at("p_tr", F + 8, [P, 2, 2, 3 * P])
        q_tr = at("q_tr", F + 16, [P, KC, S])
        k_tr = at("k_tr", F + 32, [P, KV, S])
        q_sq = at("q_sq", F + 40, [P, T, HEADS, HD])
        k_sq = at("k_sq", F + 56, [P, T, KV, HD])
        rope = at("rope", F + 56, [P, 4, T, HEADS, HALF_ROPE])
        scores = at("scores", F + 40, [P, HEADS // 2, 3 * P])
        w_dt = at("w_dt", F + 64, [P, KC, SH])
        w_dt_hi = at("w_dt_hi", F + 66, [P, KC, SH], F32R)
        w_dt_lo = at("w_dt_lo", F + 68, [P, KC, SH], F32R)
        q_t = at("q_t", F + 72, [P, T, HEADS, HD])
        o_t = at("o_t", F + 72, [P, T, HEADS, HD])
        xbc = at("xbc", F, [P, XBC, S])
        decay = at("decay", F, [P, SH, P])
        xs_t = at("xs_t", F + 24, [P, T, SH, SP])
        xdt = at("xdt", F + 40, [P, T, SH, SP])
        y_t = at("y_t", F + 40, [P, T, SH, SP])
        z_t = at("z_t", F + 56, [P, T, D])
        b_tok = at("b_tok", F + 88, [P, SG, P])
        cb = at("cb", F + 90, [P, SG, P])
        s_hi = at("s_hi", F, [P, KC, S], F32R)
        s_lo = at("s_lo", F + 16, [P, KC, S], F32R)
        s_f = at("s_f", F + 56, [P, KC, S])
        pe_t = at("pe_t", F + 32, [P, T, D])
        p_t = at("p_t", F + 48, [P, T, PLE])
        p_f = at("p_f", F + 50, [P, PLE // P, S])
        w_ple = at("w_ple", F + 52, [P, PLE // P, D])
        sig = at("sig", F + 68, [P, T, COLS])
        pe_sq = at("pe_sq", F + 72, [P, D])

        pair = ctx.enter_context(nc.psum_tensor("pair", [P, 2, 2, COLS], F32))
        misc = ctx.enter_context(nc.psum_tensor("misc", [P, 4, COLS], F32))

        b_ada, g_mix, g_ffn = vec[:, 0, 0:96], vec[:, 0, 96:112], vec[:, 0, 112:128]
        cw1, cb1 = vec[:, 1, 0:32], vec[:, 1, 32:40]
        b_ra, b_ri, lam, ls_pool = (vec[:, 1, 40 + 8 * n:48 + 8 * n] for n in range(4))
        g_att, g_fin, g_ssm = (vec[:, 1, 72 + 16 * n:88 + 16 * n] for n in range(3))
        cw2, g_ffn2, g_ple = vec[:, 2, 0:96], vec[:, 2, 96:112], vec[:, 2, 112:128]
        cb2, cb3, g_post = vec[:, 3, 0:24], vec[:, 3, 24:112], vec[:, 3, 112:128]
        c_col = vec[:, 4, 2 * HC:2 * HC + KC]

        def by_chunk(a):
            return a.rearrange("(n p) -> n p", p=P)

        vec_loads = [
            (0, 0, by_chunk(d["b_ada"][0])), (0, 96, by_chunk(d["g_norm_mix"][0])), (0, 112, by_chunk(d["g_norm_ffn"][0])),
            *[(1, RC * j, by_chunk(d["w_conv"][0, j])) for j in range(CONV)],
            (1, 32, by_chunk(d["b_conv"][0])), (1, 40, by_chunk(d["b_rg_a"][0])), (1, 48, by_chunk(d["b_rg_i"][0])),
            (1, 56, by_chunk(d["lru_lambda"][0])), (1, 64, d["ls_pool"][0].rearrange("g (n p) -> (g n) p", p=P)),
            (1, 72, by_chunk(d["attn_norm_g_2"][0])), (1, 88, by_chunk(d["g_norm_final"])),
            (1, 104, by_chunk(d["ssm_norm_g_2"][0])),
            *[(2, XBC * j, by_chunk(d["conv_w_2"][0, j])) for j in range(CONV)],
            (2, 96, by_chunk(d["ffn_norm_g_2"][0])), (2, 112, by_chunk(d["ple_norm_g_2"][0])),
            (3, 0, by_chunk(d["conv_b_2"][0])), (3, 24, by_chunk(d["ffn_conv_b_2"][0])), (3, 112, by_chunk(d["ple_post_g_2"][0])),
            *[(4 + j, 0, by_chunk(d["ffn_conv_w_2"][0, j])) for j in range(FFN_CONV)],
            (4, 2 * HC, by_chunk(d["c"][0])),
        ]
        dt_bias, a_log, d_skip, sinks = (rows[:, 32 * n:32 * n + 32] for n in range(4))
        q_g, k_g = rows[:, 128:192], rows[:, 192:256]
        row_loads = [(dt_bias, d["dt_bias_2"]), (a_log, d["a_log_2"]), (d_skip, d["d_skip_2"]), (sinks, d["sinks_2"]),
                     (q_g, d["q_norm_g_2"]), (k_g, d["k_norm_g_2"])]

        def columns(tile, widths):
            ends = np.cumsum(widths)
            assert ends[-1] <= tile.shape[1]
            return [tile[:, int(e) - w:int(e)] for e, w in zip(ends, widths)]

        ssq, var, std, rstd, c_silu, g_mod, ls8, nls8, window_inv = columns(keep, [T, T, T, T, KC, KC, RC, RC, 16])
        dt, a_dt, a_cs, a_neg, to_last, from_start, a_last, cos_t, sin_t = columns(
            keep[:, 96:512], [T * SH, T * SH, T * SH, SH, SH, SH, SH, T * HALF_ROPE, T * HALF_ROPE])
        g_ssq, g_var, g_std, g_rstd = columns(keep[:, 450:512], [T * SG] * 4)
        l_abs, l_exp, l_den, l_s, l_s2, l_p, l_max = columns(page, [RC] * 7)
        freq, pos_f, ang, turns, ang_r, half_sin = columns(page[:, 64:512], [HALF_ROPE, T] + [T * HALF_ROPE] * 4)
        hn_ssq, hn_var, hn_std, hn_r = columns(page[:, 512:1024], [T * (HEADS + KV)] * 4)
        d_x, d_abs, d_exp, d_den, d_s, d_s2, d_p, d_max = columns(page[:, 1024:1536], [T * SH] * 8)
        m_max, m_all, m_neg, m_sink, e_sink, e_sum, e_den, e_inv = columns(page[:, 1536:2048], [2 * HEADS] * 8)

        landed = [sem(f"raw_landed{n}") for n in range(RAW_SLOTS)]
        hi_ready, lo_ready, w_used = sem("hi_ready"), sem("lo_ready"), sem("w_used")
        x_landed, vec_landed, rows_landed, mixw_landed = (sem(n) for n in ("x_landed", "vec_landed", "rows_landed", "mixw_landed"))
        dt_landed, ple_landed, stored = sem("dt_landed"), sem("ple_landed"), sem("stored")
        vec_zero, gates_zero, consts = sem("vec_zero"), sem("gates_zero"), sem("consts")
        pool_step, act_step, dve_step = sem("pool_step"), sem("act_step"), sem("dve_step")
        vec_turned, vec_ready, c_ready = sem("vec_turned"), sem("vec_ready"), sem("c_ready")
        prep_in, prep_exp = sem("prep_in"), sem("prep_exp")
        mod_step, mod_mm, mod_ready = sem("mod_step"), sem("mod_mm"), sem("mod_ready")
        n_ssq, n_var, n_std, n_xn, n_turned, n_f, n_hi, n_lo = (
            sem("norm_" + n) for n in ("ssq", "var", "std", "xn", "turned", "f", "hi", "lo"))
        x_new = sem("x_new")
        c1_bias, c1_tap, gate_mm, gate_ev, xp_ev, ge_ev = (sem(n) for n in ("c1_bias", "c1_tap", "gate_mm", "gate_ev", "xp_ev", "ge_ev"))
        lru_t, lru_e, lru_q, lru_r, pooled, pool_mm, pool_ev, y_hi, y_lo = (
            sem(n) for n in ("lru_t", "lru_e", "lru_q", "lru_r", "pooled", "pool_mm", "pool_ev", "y_hi", "y_lo"))
        row_mm, row_ready, fin_mm, fin_ssq, fin_var, fin_std, fin_x = (
            sem(n) for n in ("row_mm", "row_ready", "fin_mm", "fin_ssq", "fin_var", "fin_std", "fin_x"))
        ff_sig, ff_prod, h_hi, h_lo, c3_bias, c3_tap = (sem(n) for n in ("ff_sig", "ff_prod", "h_hi", "h_lo", "c3_bias", "c3_tap"))
        qkv_ev, dt_hi, dt_lo, dt_mm, dt_x, dt_exp, hn_v, hn_s, k_ready, q_ready, qk_turned, qk_ev = (
            sem(n) for n in ("qkv_ev", "dt_hi", "dt_lo", "dt_mm", "dt_x", "dt_exp", "hn_v", "hn_s", "k_ready", "q_ready",
                             "qk_turned", "qk_ev"))
        sc_mm, sc_ev, sc_max, sink_exp, sc_exp, p_turned, p_ev, pv_mm, o_ev = (
            sem(n) for n in ("sc_mm", "sc_ev", "sc_max", "sink_exp", "sc_exp", "p_turned", "p_ev", "pv_mm", "o_ev"))
        c2_bias, c2_tap, xbc_ev, z_ev, a_ready, cs_mm, cs_ev, end_ev, xs_turned, xs_ev, b_turned, b_ev = (
            sem(n) for n in ("c2_bias", "c2_tap", "xbc_ev", "z_ev", "a_ready", "cs_mm", "cs_ev", "end_ev", "xs_turned", "xs_ev",
                             "b_turned", "b_ev"))
        xdt_ready, cb_mm, cb_ev, seg_mm, seg_ev, seg_min, seg_exp, decay_ready, yd_mm, yd_ev, st_in, st_mm, st_ev, yo_mm, yo_ev = (
            sem(n) for n in ("xdt_ready", "cb_mm", "cb_ev", "seg_mm", "seg_ev", "seg_min", "seg_exp", "decay_ready", "yd_mm", "yd_ev",
                             "st_in", "st_mm", "st_ev", "yo_mm", "yo_ev"))
        g_v, g_s, ys_ready, ys_turned, ys_f, ys_hi, ys_lo, yo_turned, ya_hi, ya_lo = (
            sem(n) for n in ("g_v", "g_s", "ys_ready", "ys_turned", "ys_f", "ys_hi", "ys_lo", "yo_turned", "ya_hi", "ya_lo"))
        pt_turned, pt_ev, pe_mm, pe_ev, pe_ssq, pe_v, pe_s, post_mm, pe_ready, gate_sig, x_out = (
            sem(n) for n in ("pt_turned", "pt_ev", "pe_mm", "pe_ev", "pe_ssq", "pe_v", "pe_s", "post_mm", "pe_ready", "gate_sig",
                             "x_out"))

        class Steps:

            def __init__(self, eng, steps):
                self.eng, self.steps, self.n = eng, steps, 0

            def __call__(self, ins):
                ins.then_inc(self.steps, 1)
                self.n += 1
                return self.n

            def wait(self, n=None):
                self.eng.wait_ge(self.steps, self.n if n is None else n)

        def flat(a):
            return a.rearrange("p a b -> p (a b)")

        def flat3(a):
            return a.rearrange("p a b c -> p (a b c)")

        def by_block(a):
            return a.rearrange("p (b h) -> p b h", b=2)

        end_in, dt_raw, res_ready = sem("end_in"), sem("dt_raw"), sem("res_ready")
        block = ctx.enter_context(nc.Block())

        @block.gpsimd
        def _(pool):
            done = Steps(pool, pool_step)
            pool.memset(vec_rows[:], 0.0).then_inc(vec_zero, 1)
            done(pool.memset(ident[:], 0.0))
            done(pool.memset(upper[:], 1.0))
            done(pool.memset(a_mask[:], 0.0))
            pool.memset(ones[:], 1.0).then_inc(consts, 1)
            done.wait()
            pool.affine_select(out=ident[:], in_=ident[:], compare_op=ALU.not_equal, fill=1.0, base=0,
                               pattern=[[-1, P]], channel_multiplier=1).then_inc(consts, 1)
            pool.affine_select(out=upper[:], in_=upper[:], compare_op=ALU.is_ge, fill=0.0, base=0,
                               pattern=[[1, P]], channel_multiplier=-1).then_inc(consts, 1)
            done(pool.affine_select(out=a_mask[:, 0:S], in_=a_mask[:, 0:S], compare_op=ALU.is_ge, fill=MASKED, base=-1,
                                    pattern=[[1, S]], channel_multiplier=-1))
            done.wait()
            pool.affine_select(out=a_mask[:, 0:S], in_=a_mask[:, 0:S], compare_op=ALU.is_ge, fill=MASKED, base=P,
                               pattern=[[-1, S]], channel_multiplier=1).then_inc(consts, 1)
            pool.affine_select(out=a_mask[:, S:3 * P], in_=a_mask[:, S:3 * P], compare_op=ALU.is_ge, fill=MASKED, base=0,
                               pattern=[[-1, P]], channel_multiplier=1).then_inc(consts, 1)
            pool.iota(window_inv, [[1, 16]], base=1, channel_multiplier=0,
                      allow_small_or_imprecise_dtypes=True).then_inc(consts, 1)
            for n in range(HALF_ROPE):
                pool.memset(freq[:, n:n + 1], float(np.float32(ROPE_THETA) ** np.float32(-n / HALF_ROPE))).then_inc(consts, 1)
            pool.wait_ge(mod_mm, MOD_BLOCKS)
            pool.memset(gates_w[:], 0.0).then_inc(gates_zero, 1)

        CONSTS = 6 + HALF_ROPE

        @block.sync
        def _(sp):
            for t in range(T):
                sp.dma_start(x[:, t, :], d["x"][0, t * P:(t + 1) * P, :]).then_inc(x_landed, 16)
            sp.wait_ge(vec_zero, 1)
            for n, r0, src in vec_loads:
                sp.dma_start(vec_rows[r0:r0 + src.shape[0], n, :], src).then_inc(vec_landed, 16)
            for dst, src in row_loads:
                sp.dma_start(dst, src.partition_broadcast(P) if len(src.shape) == 1 else src.to_broadcast([P, src.shape[1]])).then_inc(rows_landed, 16)
            sp.dma_start(pos_i[:], d["positions_2"][0].rearrange("(t p) -> p t", p=P),
                         allow_slow_non_contiguous=True).then_inc(rows_landed, 16)

            ada = d["w_ada"][0].rearrange("(k p) n -> p k n", p=P)

            def load_mod(b, first):
                for j in range(4):
                    if not first:
                        sp.wait_ge(mod_step, b * 16 + 4 * (j + 1 - 4))
                    sp.dma_start(raw[:, j], ada[:, 4 * j:4 * j + 4, bass.ds(b * COLS, COLS)]).then_inc(landed[j], 16)

            def load_mod_next(b):
                for j in range(4):
                    sp.wait_ge(mod_step, b * 16 + 4 * (j + 1) - 16)
                    sp.dma_start(raw[:, j], ada[:, 4 * j:4 * j + 4, bass.ds(b * COLS, COLS)]).then_inc(landed[j], 16)

            load_mod(0, True)
            with sp.Fori(1, MOD_BLOCKS) as b:
                load_mod_next(b)

            def load(ph, b, sources):
                for j in range(ph.tiles):
                    if not isinstance(b, int) or ph.tile(b) + j >= RAW_SLOTS:
                        sp.wait_ge(lo_ready, 2 * ph.tile(b) + (2 * j - 2 * RAW_SLOTS + 2))
                    else:
                        sp.wait_ge(mod_step, 4 * (MOD_TILES - RAW_SLOTS + j + 1))
                    k0, n = ph.row0[j], ph.rows[j]
                    for c0, src in sources(k0, k0 + n):
                        sp.dma_start(raw[:, j % RAW_SLOTS, 0:n, c0:c0 + src.shape[2]], src).then_inc(landed[j % RAW_SLOTS], 16)

            def plain(w, cols):
                w = w.rearrange("(k p) n -> p k n", p=P)
                return lambda k0, k1: [(0, w[:, k0:k1, cols])]

            def twin(w, col, v, col2):
                w, v = (a.rearrange("(k p) n -> p k n", p=P) for a in (w, v))
                return lambda k0, k1: [(0, w[:, k0:k1, bass.ds(col, COLS // 2)]), (COLS // 2, v[:, k0:k1, bass.ds(col2, COLS // 2)])]

            def load_all(ph, w):
                with sp.Fori(0, ph.blocks) as b:
                    load(ph, b, plain(w, bass.ds(b * COLS, COLS)))

            load(w_in, 0, plain(d["w_in"][0], bass.ds(w_in_cols[0], COLS)))
            sp.wait_ge(gates_zero, 1)
            for n, w in enumerate((d["w_rg_a"][0], d["w_rg_i"][0])):
                for e in range(2):
                    sp.dma_start(gates_w[64 * e:64 * e + 64, n, :, 64 * e:64 * e + 64],
                                 w.rearrange("(m e) i j -> e i m j", e=2)[e]).then_inc(mixw_landed, 16)
            sp.dma_start(pool_w[:], d["w_pool"][0].rearrange("g (k p) n -> p (g k) n", p=P)).then_inc(mixw_landed, 16)
            for b in range(1, w_in.blocks):
                load(w_in, b, plain(d["w_in"][0], bass.ds(w_in_cols[b], COLS)))
            load_all(w_out, d["w_out"][0])
            with sp.Fori(0, up1.blocks) as b:
                load(up1, b, twin(d["w_ffn_gate"][0], b * (COLS // 2), d["w_ffn_up"][0], b * (COLS // 2)))
            load_all(down1, d["w_ffn_down"][0])
            load(w_in2, 0, plain(d["w_in_2"][0], bass.ds(w_in2_cols[0], COLS)))
            sp.wait_ge(w_used, down1.end(down1.blocks - 1))
            sp.dma_start(w_dt[:], d["w_in_2"][0].rearrange("(k p) n -> p k n", p=P)[:, :, O_DT:O_DT + SH]).then_inc(dt_landed, 16)
            for b in range(1, w_in2.blocks):
                load(w_in2, b, plain(d["w_in_2"][0], bass.ds(w_in2_cols[b], COLS)))
            load_all(w_out2, d["w_out_2"][0])
            with sp.Fori(0, up2.blocks) as b:
                load(up2, b, twin(d["w_up_2"][0], b * (COLS // 2), d["w_up_2"][0], b * (COLS // 2) + HC * P))
            load_all(down2, d["w_down_2"][0])
            load(ple_gate, 0, plain(d["w_ple_gate_2"][0], bass.ds(0, COLS)))
            sp.wait_ge(w_used, down2.end(down2.blocks - 1))
            sp.dma_start(p_t[:], d["p_2"][0, 0].rearrange("(t p) n -> p t n", p=P)).then_inc(ple_landed, 16)
            sp.dma_start(w_ple[:], d["w_ple_proj_2"][0].rearrange("(k p) n -> p k n", p=P)).then_inc(ple_landed, 16)
            for b in range(1, ple_gate.blocks):
                load(ple_gate, b, plain(d["w_ple_gate_2"][0], bass.ds(b * COLS, COLS)))
            result = out[0].rearrange("(t p) n -> p t n", p=P)
            for b in range(ple_gate.blocks):
                sp.wait_ge(x_out, b + 1)
                sp.dma_start(result[:, :, b * COLS:(b + 1) * COLS], x[:, :, b * COLS:(b + 1) * COLS]).then_inc(stored, 16)
            sp.wait_ge(stored, 16 * ple_gate.blocks)

        @block.scalar
        def _(act):
            done = Steps(act, act_step)
            run = nc.scalar.activation

            def split_hi(ph, b, halves):
                for h in halves:
                    at0, _, n = ph.half_rows(h)
                    if h % 2 == 0:
                        act.wait_ge(landed[h // 2 % RAW_SLOTS], ph.landed(b, h // 2))
                    if not isinstance(b, int) or ph.half(b) + h >= HALF_SLOTS:
                        act.wait_ge(w_used, ph.half(b) + (h - HALF_SLOTS + 1))
                    run(w_hi[:, h % HALF_SLOTS, 0:n, :], raw[:, h // 2 % RAW_SLOTS, at0:at0 + n, :],
                        ACT.Copy).then_inc(hi_ready, 1)

            def stream(ph, finish, nxt, peel=0):
                def one(b, c, more):
                    split_hi(ph, b, range(LEAD, ph.halves))
                    if more:
                        split_hi(ph, b + 1, range(LEAD))
                    elif nxt:
                        split_hi(nxt, 0, range(LEAD))
                    act.wait_ge(w_used, ph.end(b))
                    finish(b, c)

                for b in range(2 * peel):
                    one(b, b % 2, True)
                with act.Fori(peel, ph.blocks // 2 - 1) as i:
                    one(i * 2, 0, True)
                    one(i * 2 + 1, 1, True)
                one(ph.blocks - 2, 0, True)
                one(ph.blocks - 1, 1, False)

            def norm_stats(n):
                for t in range(T):
                    run(xn[:, t, :], x[:, t, :], ACT.Square, accum_out=ssq[:, t:t + 1]).then_inc(n_ssq, 1)
                act.wait_ge(n_var, n + 1)
                run(std, var, ACT.Sqrt).then_inc(n_std, 1)

            def norm_features(n, scale, shift):
                for b in range(KC // 2):
                    act.wait_ge(n_turned, n * (KC // 2) + b + 1)
                    for e in range(2):
                        m = 2 * b + e
                        of = misc[:, b % 4, e * S:(e + 1) * S]
                        if shift is None:
                            run(hf[:, m, :], of, ACT.Copy, scale=scale[:, m:m + 1]).then_inc(n_f, 1)
                        else:
                            run(hf[:, m, :], of, ACT.Identity, scale=scale[:, m:m + 1], bias=shift[:, m:m + 1]).then_inc(n_f, 1)

            def conv_bias(c, m0, tap, bias, dst, signal):
                for m in range(4):
                    run(dst[:, m0 + m, :], pair[:, c, m // 2, (m % 2) * S:(m % 2 + 1) * S], ACT.Identity,
                        scale=tap[:, m0 + m:m0 + m + 1], bias=bias[:, m0 + m:m0 + m + 1]).then_inc(signal, 1)

            act.wait_ge(vec_turned, 1)
            run(flat(vec[:, 0:4, :]), misc[:, 0, :], ACT.Copy).then_inc(vec_ready, 1)
            run(flat(vec[:, 4:7, :]), misc[:, 1, 0:3 * P], ACT.Copy).then_inc(vec_ready, 1)
            act.wait_ge(vec_ready, 2)
            run(c_silu, c_col, ACT.Silu).then_inc(c_ready, 1)
            act.wait_ge(prep_in, 1)
            run(l_exp, l_abs, ACT.Exp, scale=-1.0).then_inc(prep_exp, 1)
            act.wait_ge(rows_landed, 16 * (len(row_loads) + 1))
            run(a_neg, a_log, ACT.Exp).then_inc(prep_exp, 1)
            act.wait_ge(prep_in, 2)
            run(half_sin, ang_r, ACT.Sin, scale=0.5).then_inc(prep_exp, 1)
            run(sin_t, ang_r, ACT.Sin).then_inc(prep_exp, 1)

            act.wait_ge(x_landed, 16 * T)
            norm_stats(0)
            split_hi(w_in, 0, range(LEAD))
            norm_features(0, g_mod, mod[:, 0:KC])

            def mixer(b):
                split_hi(w_in, b, range(LEAD, w_in.halves))
                if b + 1 < w_in.blocks:
                    split_hi(w_in, b + 1, range(LEAD))
                else:
                    split_hi(w_out, 0, range(LEAD))
                act.wait_ge(w_used, w_in.end(b))

            for b in range(2):
                mixer(b)
                conv_bias(b % 2, 4 * b, cw1[:, (CONV - 1) * RC:], cb1, xc, c1_bias)
            mixer(2)
            run(flat(xp[:, 0:4, :]), flat(pair[:, 0]), ACT.Copy).then_inc(xp_ev, 1)
            for m in range(RC):
                act.wait_ge(gate_mm, m + 1)
                run(lru_a[:, m, :], misc[:, m % 4, 0:S], ACT.Sigmoid, bias=b_ra[:, m:m + 1]).then_inc(gate_ev, 1)
                run(lru_u[:, m, :], misc[:, m % 4, S:2 * S], ACT.Sigmoid, bias=b_ri[:, m:m + 1]).then_inc(gate_ev, 1)
            mixer(3)
            run(flat(xp[:, 4:8, :]), flat(pair[:, 1]), ACT.Copy).then_inc(xp_ev, 1)
            act.wait_ge(gate_ev, 2 * RC)
            act.wait_ge(prep_in, 4)
            for m in range(RC):
                run(lru_m[:, m, :], lru_a[:, m, :], ACT.Tanh, scale=nls8[:, m:m + 1]).then_inc(lru_t, 1)
            for m in range(RC):
                run(lru_a[:, m, :], lru_a[:, m, :], ACT.Exp, scale=ls8[:, m:m + 1]).then_inc(lru_e, 1)
            mixer(4)
            run(flat(y_mix[:, 0:4, :]), flat(pair[:, 0]), ACT.Gelu_apprx_tanh).then_inc(ge_ev, 1)
            act.wait_ge(lru_q, 1)
            run(flat(lru_m[:]), flat(lru_m[:]), ACT.Sqrt, scale=2.0).then_inc(lru_r, 1)
            for m in range(2 * G):
                act.wait_ge(pool_mm, m // 2 * 2 + 2)
                run(y_mix[:, RC + m, :], misc[:, m // 2, (m % 2) * S:(m % 2 + 1) * S], ACT.Copy,
                    scale=ls_pool[:, m:m + 1]).then_inc(pool_ev, 1)
            mixer(5)
            run(flat(y_mix[:, 4:8, :]), flat(pair[:, 1]), ACT.Gelu_apprx_tanh).then_inc(ge_ev, 1)
            act.wait_ge(row_mm, 1)
            run(row[:], flat(misc[:]), ACT.Copy).then_inc(row_ready, 1)

            stream(w_out, lambda b, c: None, up1)
            act.wait_ge(x_new, w_out.blocks)
            norm_stats(1)
            norm_features(1, g_mod, mod[:, 3 * KC:4 * KC])
            act.wait_ge(row_mm, 2)
            run(row[:], flat(misc[:]), ACT.Copy).then_inc(row_ready, 1)

            def finish_up1(b, c):
                if not isinstance(b, int) or b:
                    act.wait_ge(ff_prod, b)
                run(flat(ff_g[:]), pair[:, c, 0, :], ACT.Silu).then_inc(ff_sig, 1)

            stream(up1, finish_up1, down1, peel=1)
            stream(down1, lambda b, c: None, w_in2)

            act.wait_ge(x_new, w_out.blocks + down1.blocks)
            for t in range(T):
                run(xn[:, t, :], x[:, t, :], ACT.Square, accum_out=ssq[:, t:t + 1]).then_inc(fin_ssq, 1)
            act.wait_ge(fin_var, 1)
            run(std, var, ACT.Sqrt).then_inc(fin_std, 1)
            act.wait_ge(fin_x, T)
            norm_stats(2)
            norm_features(2, g_att, None)
            act.wait_ge(dt_landed, 16)
            run(flat(w_dt_hi[:]), flat(w_dt[:]), ACT.Copy).then_inc(dt_hi, 1)

            def mixer2(b):
                split_hi(w_in2, b, range(LEAD, w_in2.halves))
                if b + 1 < w_in2.blocks:
                    split_hi(w_in2, b + 1, range(LEAD))
                else:
                    split_hi(w_out2, 0, range(LEAD))
                act.wait_ge(w_used, w_in2.end(b))

            for b in range(B_K):
                mixer2(b)
                run(q_t[:, :, 8 * b:8 * b + 8, :].rearrange("p t h e -> p t (h e)"), pair[:, b % 2], ACT.Copy).then_inc(qkv_ev, 1)
                if b == 2:
                    act.wait_ge(dt_x, 1)
                    run(d_exp, d_abs, ACT.Exp, scale=-1.0).then_inc(dt_exp, 1)
            for b, kv in ((B_K, k_t), (B_V, v_t)):
                mixer2(b)
                run(kv.rearrange("p t h e -> p t (h e)"), pair[:, b % 2], ACT.Copy).then_inc(qkv_ev, 1)

            act.wait_ge(hn_v, 1)
            run(hn_std, hn_var, ACT.Sqrt).then_inc(hn_s, 1)
            for f in range(KV // 2 + KC // 2):
                act.wait_ge(qk_turned, f + 1)
                dst = k_tr[:, 2 * f:2 * f + 2, :] if f < KV // 2 else q_tr[:, 2 * f - KV:2 * f - KV + 2, :]
                run(flat(dst), misc[:, f % 4, :], ACT.Copy).then_inc(qk_ev, 1)
            for g in range(2):
                act.wait_ge(sc_max, g + 1)
                run(by_block(e_sink)[:, :, 16 * g:16 * g + 16], by_block(m_sink)[:, :, 16 * g:16 * g + 16], ACT.Exp).then_inc(sink_exp, 1)
                for h in range(16):
                    for blk, keys in ((1, slice(0, S)), (0, slice(S, 3 * P))):
                        n = blk * HEADS + 16 * g + h
                        run(scores[:, h, keys], scores[:, h, keys], ACT.Exp, bias=m_neg[:, n:n + 1],
                            accum_out=e_sum[:, n:n + 1]).then_inc(sc_exp, 1)
                for i in range(8 * g, 8 * g + 8):
                    act.wait_ge(p_turned, i + 1)
                    if i >= 2:
                        act.wait_ge(pv_mm, i - 1)
                    bank = 2 * (i % 2)
                    run(p_tr[:, i % 2], misc[:, bank:bank + 2, 0:3 * P], ACT.Copy).then_inc(p_ev, 1)

            act.wait_ge(pv_mm, 16)
            for b in range(B_XBC, B_Z):
                j = b - B_XBC
                mixer2(b)
                conv_bias(b % 2, 4 * j, cw2[:, (CONV - 1) * XBC:], cb2, xbc, c2_bias)
                if j:
                    act.wait_ge(c2_tap, 12 * j)
                    run(flat(xbc[:, 4 * j - 4:4 * j, :]), flat(xbc[:, 4 * j - 4:4 * j, :]), ACT.Silu).then_inc(xbc_ev, 1)
            for b in range(B_Z, w_in2.blocks):
                j = b - B_Z
                mixer2(b)
                if j == 0:
                    act.wait_ge(c2_tap, 72)
                    run(flat(xbc[:, 20:24, :]), flat(xbc[:, 20:24, :]), ACT.Silu).then_inc(xbc_ev, 1)
                run(z_t[:, :, COLS * j:COLS * (j + 1)], pair[:, b % 2], ACT.Silu).then_inc(z_ev, 1)

            for i in range(2 * T * 2):
                act.wait_ge(xs_turned, i + 1)
                t, f = i // 4, i % 4
                run(xs_t[:, t, 8 * f:8 * f + 8, :].rearrange("p h e -> p (h e)"), misc[:, i % 4, :], ACT.Copy).then_inc(xs_ev, 1)
            act.wait_ge(b_turned, 1)
            run(flat(b_tok[:]), misc[:, 0, :], ACT.Copy).then_inc(b_ev, 1)
            act.wait_ge(cs_mm, 1)
            run(a_cs, misc[:, 1, 0:T * SH], ACT.Copy).then_inc(cs_ev, 1)
            run(a_last, misc[:, 1, T * SH:T * SH + SH], ACT.Copy).then_inc(cs_ev, 1)
            act.wait_ge(cs_ev, 2)
            run(from_start, a_cs[:, SH:2 * SH], ACT.Exp).then_inc(end_ev, 1)
            act.wait_ge(end_in, 1)
            run(to_last, to_last, ACT.Exp).then_inc(end_ev, 1)
            act.wait_ge(st_mm, 1)
            run(state.rearrange("p h e -> p (h e)"), flat(misc[:]), ACT.Copy).then_inc(st_ev, 1)
            for c in range(T):
                for g in range(SG):
                    act.wait_ge(seg_min, SG * c + g + 1)
                    run(flat(decay[:, 8 * g:8 * g + 8, :]), flat(decay[:, 8 * g:8 * g + 8, :]), ACT.Exp).then_inc(seg_exp, 1)
            act.wait_ge(g_v, 1)
            run(g_std, g_var, ACT.Sqrt).then_inc(g_s, 1)
            for f in range(KC // 2):
                act.wait_ge(yo_turned, f + 1)
                run(flat(a_hi[:, 2 * f:2 * f + 2, :]), misc[:, f % 4, :], ACT.Copy).then_inc(ya_hi, 1)
            for f in range(KC // 2):
                act.wait_ge(ys_turned, f + 1)
                for e in range(2):
                    m = 2 * f + e
                    run(s_f[:, m, :], misc[:, f % 4, e * S:(e + 1) * S], ACT.Copy, scale=g_ssm[:, m:m + 1]).then_inc(ys_f, 1)

            stream(w_out2, lambda b, c: None, up2)
            act.wait_ge(x_new, w_out.blocks + down1.blocks + w_out2.blocks)
            norm_stats(3)
            norm_features(3, g_ffn2, None)

            def finish_up2(b, c):
                act.wait_ge(h_lo, b + up1.blocks)
                for m in range(4):
                    dst, m0 = ((ff_g, 0), (ff_u, HC))[m // 2]
                    ch = bass.ds(b * 2 + (m0 + m % 2), 1)
                    run(dst[:, m % 2, :], pair[:, c, m // 2, (m % 2) * S:(m % 2 + 1) * S], ACT.Identity,
                        scale=vec[:, 4 + FFN_CONV - 1, ch], bias=vec[:, 3, bass.ds(b * 2 + (24 + m0 + m % 2), 1)]).then_inc(c3_bias, 1)
                act.wait_ge(c3_tap, b * 8 + 8)
                run(flat(ff_g[:]), flat(ff_g[:]), ACT.Silu).then_inc(ff_sig, 1)

            stream(up2, finish_up2, down2)
            stream(down2, lambda b, c: None, ple_gate)

            act.wait_ge(x_new, w_out.blocks + down1.blocks + w_out2.blocks + down2.blocks)
            norm_stats(4)
            norm_features(4, g_ple, None)
            act.wait_ge(pt_turned, 1)
            run(flat(p_f[:]), misc[:, 0, :], ACT.Copy).then_inc(pt_ev, 1)
            for t in range(T):
                act.wait_ge(pe_mm, t + 1)
                run(pe_t[:, t, :], flat(misc[:]), ACT.Copy).then_inc(pe_ev, 1)
                act.wait_ge(pe_ev, t + 1)
                run(pe_sq[:], pe_t[:, t, :], ACT.Square, accum_out=ssq[:, t:t + 1]).then_inc(pe_ssq, 1)
            act.wait_ge(pe_v, 1)
            run(std, var, ACT.Sqrt).then_inc(pe_s, 1)
            for b in range(ple_gate.blocks):
                split_hi(ple_gate, b, range(LEAD, ple_gate.halves))
                if b + 1 < ple_gate.blocks:
                    split_hi(ple_gate, b + 1, range(LEAD))
                act.wait_ge(w_used, ple_gate.end(b))
                act.wait_ge(x_out, b)
                run(flat(sig[:]), flat(pair[:, b % 2]), ACT.Sigmoid).then_inc(gate_sig, 1)

        @block.tensor
        def _(pe):
            def features(ph, b, c, hi, lo):
                for h in range(ph.halves):
                    pe.wait_ge(lo_ready, ph.half(b) + (h + 1))
                    slot = h % HALF_SLOTS
                    _, k0, n = ph.half_rows(h)
                    for kk in range(n):
                        k = k0 + kk
                        for m in range(4):
                            o = pair[:, c, m // 2, (m % 2) * S:(m % 2 + 1) * S]
                            wh, wl = (w[:, slot, kk, m * P:(m + 1) * P] for w in (w_hi, w_lo))
                            pe.matmul(o, wh, hi[:, k, :], start=(k == 0 and m % 2 == 0), stop=False, skip_group_check=True)
                            pe.matmul(o, wh, lo[:, k, :], start=False, stop=False, skip_group_check=True)
                            mm = pe.matmul(o, wl, hi[:, k, :], start=False, stop=(k == KC - 1), skip_group_check=True)
                    mm.then_inc(w_used, 1)

            def tokens(ph, b, c, operand, n_rows):
                for h in range(ph.halves):
                    pe.wait_ge(lo_ready, ph.half(b) + (h + 1))
                    slot = h % HALF_SLOTS
                    _, k0, n = ph.half_rows(h)
                    for kk in range(n):
                        k = k0 + kk
                        hi, lo = operand(k)
                        for t in range(T):
                            o, own = pair[:, c, t, :], slice(t * P, (t + 1) * P)
                            pe.matmul(o, hi[:, own], w_hi[:, slot, kk, :], start=(k == 0), stop=False)
                            pe.matmul(o, hi[:, own], w_lo[:, slot, kk, :], start=False, stop=False)
                            mm = pe.matmul(o, lo[:, own], w_hi[:, slot, kk, :], start=False, stop=(k == n_rows - 1))
                    mm.then_inc(w_used, 1)

            def normed(k):
                return a_hi[:, k, :], a_lo[:, k, :]

            def hidden(k):
                return hid_hi[:, k, :], hid_lo[:, k, :]

            def turn(n):
                pe.wait_ge(n_xn, T * (n + 1))
                for b in range(KC // 2):
                    if b >= 4:
                        pe.wait_ge(n_f, n * KC + 2 * (b - 4) + 2)
                    for e in range(2):
                        m = 2 * b + e
                        for t in range(T):
                            mm = pe.transpose(misc[:, b % 4, e * S + t * P:e * S + (t + 1) * P], xn[:, t, m * P:(m + 1) * P], ident[:])
                    mm.then_inc(n_turned, 1)

            def rows_of(col, signal):
                for m in range(KC):
                    mm = pe.matmul(misc[:, m // 4, (m % 4) * P:(m % 4 + 1) * P], col[:, m:m + 1].to_broadcast([P, P]), ident[:],
                                   start=True, stop=True, skip_group_check=True)
                mm.then_inc(signal, 1)

            pe.wait_ge(consts, CONSTS)
            pe.wait_ge(vec_landed, 16 * len(vec_loads))
            for n in range(7):
                mm = pe.transpose(misc[:, n // 4, (n % 4) * P:(n % 4 + 1) * P], vec_rows[:, n, :], ident[:])
            mm.then_inc(vec_turned, 1)

            def mod_sums(b, c):
                pe.wait_ge(mod_step, b * 16 + 16)
                for m in range(4):
                    for kk in range(4):
                        mm = pe.matmul(misc[:, 3, bass.ds(b * 4 + m, 1)], mod_acc[:, c, kk, m * P:(m + 1) * P], ones[:, 0:1],
                                       start=(kk == 0), stop=(kk == 3), skip_group_check=True)
                mm.then_inc(mod_mm, 1)

            with pe.Fori(0, MOD_BLOCKS // 2) as i:
                mod_sums(i * 2, 0)
                mod_sums(i * 2 + 1, 1)

            pe.wait_ge(mod_ready, 1)
            turn(0)
            pe.wait_ge(n_lo, KC // 2)
            for b in range(w_in.blocks):
                if 2 <= b < 4:
                    pe.wait_ge(c1_tap, 12 * (b - 1))
                elif b >= 4:
                    pe.wait_ge(xp_ev, b - 3)
                features(w_in, b, b % 2, a_hi, a_lo)
                if b == 2:
                    pe.wait_ge(c1_tap, 24)
                    pe.wait_ge(mixw_landed, 5 * 16)
                    for m in range(RC):
                        if m >= 4:
                            pe.wait_ge(gate_ev, 2 * (m - 4) + 2)
                        for n in range(2):
                            mm = pe.matmul(misc[:, m % 4, n * S:(n + 1) * S], gates_w[:, n, m, :], xc[:, m, :],
                                           start=True, stop=True, skip_group_check=True)
                        mm.then_inc(gate_mm, 1)
                if b == 4:
                    pe.wait_ge(pooled, 4)
                    pe.wait_ge(gate_ev, 2 * RC)
                    for m in range(2 * G):
                        g, e = m // 2, m % 2
                        for kk in range(2):
                            mm = pe.matmul(misc[:, g, e * S:(e + 1) * S], pool_w[:, 2 * g + kk, e * P:(e + 1) * P], xp[:, 2 * g + kk, :],
                                           start=(kk == 0), stop=(kk == 1), skip_group_check=True)
                        mm.then_inc(pool_mm, 1)
            pe.wait_ge(pool_ev, 2 * G)
            rows_of(mod[:, 2 * KC:3 * KC], row_mm)

            pe.wait_ge(y_lo, 2)
            for b in range(w_out.blocks):
                if b >= 2:
                    pe.wait_ge(x_new, b - 1)
                tokens(w_out, b, b % 2, normed, KC)

            pe.wait_ge(row_ready, 1)
            turn(1)
            pe.wait_ge(n_f, 2 * KC)
            rows_of(mod[:, 5 * KC:6 * KC], row_mm)
            pe.wait_ge(n_lo, 2 * (KC // 2))
            for b in range(2):
                features(up1, b, b, a_hi, a_lo)
            with pe.Fori(1, up1.blocks // 2) as i:
                for c in range(2):
                    pe.wait_ge(ff_prod, i * 2 + (c - 1))
                    features(up1, i * 2 + c, c, a_hi, a_lo)
            pe.wait_ge(row_ready, 2)
            rows_of(g_fin, fin_mm)
            pe.wait_ge(h_lo, up1.blocks)
            with pe.Fori(0, down1.blocks // 2) as i:
                for c in range(2):
                    pe.wait_ge(x_new, i * 2 + (w_out.blocks + c - 1))
                    tokens(down1, i * 2 + c, c, hidden, HC)

            turn(2)
            pe.wait_ge(n_lo, 3 * (KC // 2))

            def mixer2(b, product, *operands):
                product(w_in2, b, b % 2, *operands)

            for b in range(B_XBC):
                if b >= 2:
                    pe.wait_ge(qkv_ev, b - 1)
                tokens(w_in2, b, b % 2, normed, KC)
                if b == 0:
                    pe.wait_ge(dt_lo, 1)
                    pe.wait_ge(n_f, 3 * KC)
                    for t in range(T):
                        own = slice(t * P, (t + 1) * P)
                        for k in range(KC):
                            o = misc[:, 0, t * SH:(t + 1) * SH]
                            pe.matmul(o, a_hi[:, k, own], w_dt_hi[:, k, :], start=(k == 0), stop=False, skip_group_check=True)
                            pe.matmul(o, a_hi[:, k, own], w_dt_lo[:, k, :], start=False, stop=False, skip_group_check=True)
                            mm = pe.matmul(o, a_lo[:, k, own], w_dt_hi[:, k, :], start=False, stop=(k == KC - 1), skip_group_check=True)
                    mm.then_inc(dt_mm, 1)

            pe.wait_ge(dt_x, 1)
            for f in range(KV // 2 + KC // 2):
                if f == 0:
                    pe.wait_ge(k_ready, 1)
                if f == KV // 2:
                    pe.wait_ge(q_ready, 1)
                if f >= 4:
                    pe.wait_ge(qk_ev, f - 3)
                for e in range(2):
                    for t in range(T):
                        if f < KV // 2:
                            src = k_two[:, t, 2 * f + e].rearrange("p a b -> p (a b)")
                        else:
                            m = 2 * f - KV + e
                            src = q_t[:, t, 2 * m:2 * m + 2, :].rearrange("p a b -> p (a b)")
                        mm = pe.transpose(misc[:, f % 4, e * S + t * P:e * S + (t + 1) * P], src, ident[:])
                mm.then_inc(qk_turned, 1)
            pe.wait_ge(qk_ev, KV // 2 + KC // 2)
            for g in range(2):
                for i in range(8 * g, 8 * g + 8):
                    if i >= 2:
                        pe.wait_ge(sc_ev, i - 1)
                    if i == 8:
                        pe.wait_ge(p_ev, 8)
                        pe.wait_ge(o_ev, 8)
                    for e in range(2):
                        half = slice(HD * e, HD * e + HD)
                        bank = 2 * (i % 2) + e
                        pe.matmul(misc[:, bank, 0:S], q_tr[half, i, P:S], k_tr[half, i // 2, :], start=True, stop=True, skip_group_check=True)
                        mm = pe.matmul(misc[:, bank, S:3 * P], q_tr[half, i, 0:P], k_tr[half, i // 2, 0:P], start=True, stop=True, skip_group_check=True)
                    mm.then_inc(sc_mm, 1)

                def turn_probs(i):
                    pe.wait_ge(sc_exp, 32 * g + 4 * (i - 8 * g) + 4)
                    if i >= 2:
                        pe.wait_ge(p_ev, i - 1)
                        pe.wait_ge(o_ev, i - 1)
                    pe.wait_ge(sc_ev, 8 * g + 8)
                    for e in range(2):
                        for n in range(3):
                            mm = pe.transpose(misc[:, 2 * (i % 2) + e, n * P:(n + 1) * P],
                                              scores[:, 2 * (i - 8 * g) + e, n * P:(n + 1) * P], ident[:])
                    mm.then_inc(p_turned, 1)

                def values(i):
                    pe.wait_ge(p_ev, i + 1)
                    if i >= 2:
                        pe.wait_ge(o_ev, i - 1)
                    bank, n = 2 * (i % 2), i // 2
                    for e in range(2):
                        own = slice(3 * P + HD * e, 3 * P + HD * (e + 1))
                        pe.matmul(misc[:, bank, own], p_tr[:, i % 2, e, S:3 * P], v_t[:, 0, n, :], start=True, stop=True, skip_group_check=True)
                        pe.matmul(misc[:, bank + 1, own], p_tr[:, i % 2, e, 0:P], v_t[:, 0, n, :], start=True, stop=False, skip_group_check=True)
                        mm = pe.matmul(misc[:, bank + 1, own], p_tr[:, i % 2, e, P:S], v_t[:, 1, n, :], start=False, stop=True, skip_group_check=True)
                    mm.then_inc(pv_mm, 1)

                turn_probs(8 * g)
                for i in range(8 * g, 8 * g + 8):
                    if i + 1 < 8 * g + 8:
                        turn_probs(i + 1)
                    values(i)

            for b in range(B_XBC, B_Z):
                j = b - B_XBC
                if j < 2:
                    pe.wait_ge(qkv_ev, 5 + j)
                else:
                    pe.wait_ge(c2_tap, 12 * (j - 1))
                features(w_in2, b, b % 2, a_hi, a_lo)
            for b in range(B_Z, w_in2.blocks):
                j = b - B_Z
                if j < 2:
                    pe.wait_ge(c2_tap, 60 + 12 * j)
                else:
                    pe.wait_ge(z_ev, j - 1)
                tokens(w_in2, b, b % 2, normed, KC)

            pe.wait_ge(xbc_ev, 6)
            pe.wait_ge(o_ev, 16)
            for i in range(4 * T):
                t, f = i // 4, i % 4
                if i >= 4:
                    pe.wait_ge(xs_ev, i - 3)
                for e in range(4):
                    mm = pe.transpose(misc[:, i % 4, e * P:(e + 1) * P], xbc[:, 4 * f + e, t * P:(t + 1) * P], ident[:])
                mm.then_inc(xs_turned, 1)
            pe.wait_ge(xs_ev, 5)
            for g in range(SG):
                mm = pe.transpose(misc[:, 0, g * P:(g + 1) * P], xbc[:, KC + g, 0:P], ident[:])
            mm.then_inc(b_turned, 1)
            pe.wait_ge(xs_ev, 6)
            pe.wait_ge(a_ready, 1)
            for c in range(T):
                pe.matmul(misc[:, 1, c * SH:(c + 1) * SH], upper[:], a_dt[:, c * SH:(c + 1) * SH], start=True, stop=True, skip_group_check=True)
            pe.matmul(misc[:, 1, T * SH:T * SH + SH], ones[:], a_dt[:, 0:SH], start=True, stop=True, skip_group_check=True).then_inc(cs_mm, 1)
            pe.wait_ge(st_in, 1)
            pe.wait_ge(b_ev, 1)
            pe.wait_ge(cs_ev, 2)
            pe.wait_ge(xs_ev, 8)
            for g in range(SG):
                mm = pe.matmul(misc[:, g, :], b_tok[:, g, :], state[:, 8 * g:8 * g + 8, :].rearrange("p h e -> p (h e)"), start=True, stop=True)
            mm.then_inc(st_mm, 1)
            pe.wait_ge(st_ev, 1)
            for c in range(T):
                own = slice(c * P, (c + 1) * P)
                if c:
                    pe.wait_ge(yd_ev, c)
                for g in range(SG):
                    mm = pe.matmul(misc[:, 0, g * P:(g + 1) * P], xbc[:, KC + g, own], xbc[:, KC + SG + g, own], start=True, stop=True, skip_group_check=True)
                mm.then_inc(cb_mm, 1)
                for n in range(SH // 4):
                    bank = 1 + n % 3
                    if n >= 3:
                        pe.wait_ge(seg_ev, 8 * c + n - 2)
                    for e in range(4):
                        h = c * SH + 4 * n + e
                        mm = pe.matmul(misc[:, bank, e * P:(e + 1) * P], a_dt[:, h:h + 1].to_broadcast([P, P]), upper[:], start=True, stop=True, skip_group_check=True)
                    mm.then_inc(seg_mm, 1)
                pe.wait_ge(cb_ev, c + 1)
                pe.wait_ge(seg_ev, 8 * c + 8)
                for h in range(SH):
                    if h % 8 == 0:
                        pe.wait_ge(decay_ready, SG * c + h // 8 + 1)
                    mm = pe.matmul(misc[:, h // 8, (h % 8) * SP:(h % 8 + 1) * SP], decay[:, h, :], xdt[:, c, h, :], start=True, stop=True, skip_group_check=True)
                mm.then_inc(yd_mm, 1)
            pe.wait_ge(z_ev, 4)
            for g in range(SG):
                mm = pe.matmul(pair[:, g // 2, g % 2, :], xbc[:, KC + SG + g, P:S], state[:, 8 * g:8 * g + 8, :].rearrange("p h e -> p (h e)"), start=True, stop=True)
            mm.then_inc(yo_mm, 1)
            pe.wait_ge(yd_ev, 2)
            for f in range(KC // 2):
                if f >= 4:
                    pe.wait_ge(ya_lo, f - 3)
                for e in range(2):
                    m = 2 * f + e
                    for t in range(T):
                        mm = pe.transpose(misc[:, f % 4, e * S + t * P:e * S + (t + 1) * P],
                                          o_t[:, t, 2 * m:2 * m + 2, :].rearrange("p a b -> p (a b)"), ident[:])
                mm.then_inc(yo_turned, 1)
            pe.wait_ge(ys_ready, T)
            for f in range(KC // 2):
                if f < 4:
                    pe.wait_ge(ya_lo, f + 5)
                else:
                    pe.wait_ge(ys_f, 2 * (f - 4) + 2)
                for e in range(2):
                    m = 2 * f + e
                    for t in range(T):
                        mm = pe.transpose(misc[:, f % 4, e * S + t * P:e * S + (t + 1) * P],
                                          y_t[:, t, 2 * m:2 * m + 2, :].rearrange("p a b -> p (a b)"), ident[:])
                mm.then_inc(ys_turned, 1)
            pe.wait_ge(ys_lo, KC // 2)
            pe.wait_ge(yo_ev, 1)

            def mixed(k):
                return (s_hi[:, k, :], s_lo[:, k, :]) if k < KC else (a_hi[:, k - KC, :], a_lo[:, k - KC, :])

            x0 = w_out.blocks + down1.blocks
            with pe.Fori(0, w_out2.blocks // 2) as i:
                for c in range(2):
                    pe.wait_ge(x_new, i * 2 + (x0 + c - 1))
                    tokens(w_out2, i * 2 + c, c, mixed, 2 * KC)

            x0 += w_out2.blocks
            turn(3)
            pe.wait_ge(n_lo, 4 * (KC // 2))
            with pe.Fori(0, up2.blocks // 2) as i:
                for c in range(2):
                    pe.wait_ge(ff_prod, i * 2 + (up1.blocks + c - 1))
                    features(up2, i * 2 + c, c, a_hi, a_lo)
            pe.wait_ge(h_lo, up1.blocks + up2.blocks)
            with pe.Fori(0, down2.blocks // 2) as i:
                for c in range(2):
                    pe.wait_ge(x_new, i * 2 + (x0 + c - 1))
                    tokens(down2, i * 2 + c, c, hidden, HC)

            turn(4)
            pe.wait_ge(ple_landed, 32)
            pe.wait_ge(n_f, 5 * KC)
            for k in range(PLE // P):
                for t in range(T):
                    mm = pe.transpose(misc[:, 0, k * S + t * P:k * S + (t + 1) * P], p_t[:, t, k * P:(k + 1) * P], ident[:])
            mm.then_inc(pt_turned, 1)
            pe.wait_ge(pt_ev, 1)
            for t in range(T):
                if t:
                    pe.wait_ge(pe_ev, t)
                for j in range(D // COLS):
                    for k in range(PLE // P):
                        mm = pe.matmul(misc[:, j, :], p_f[:, k, t * P:(t + 1) * P], w_ple[:, k, j * COLS:(j + 1) * COLS],
                                       start=(k == 0), stop=(k == PLE // P - 1))
                mm.then_inc(pe_mm, 1)
            pe.wait_ge(pe_ev, T)
            rows_of(g_post, post_mm)
            pe.wait_ge(n_lo, 5 * (KC // 2))
            for b in range(ple_gate.blocks):
                if b >= 2:
                    pe.wait_ge(gate_sig, b - 1)
                tokens(ple_gate, b, b % 2, normed, KC)

        @block.vector
        def _(dve):
            done = Steps(dve, dve_step)

            def split_lo(ph, b, halves):
                for h in halves:
                    at0, _, n = ph.half_rows(h)
                    dve.wait_ge(hi_ready, ph.half(b) + (h + 1))
                    slot = h % HALF_SLOTS
                    dve.tensor_tensor(w_lo[:, slot, 0:n, :], raw[:, h // 2 % RAW_SLOTS, at0:at0 + n, :],
                                      w_hi[:, slot, 0:n, :].bitcast(F32), ALU.subtract).then_inc(lo_ready, 1)

            def stream(ph, finish, nxt):
                def one(b, c, more):
                    split_lo(ph, b, range(LEAD, ph.halves))
                    if more:
                        split_lo(ph, b + 1, range(LEAD))
                    elif nxt:
                        split_lo(nxt, 0, range(LEAD))
                    dve.wait_ge(w_used, ph.end(b))
                    finish(b, c)

                with dve.Fori(0, ph.blocks // 2 - 1) as i:
                    one(i * 2, 0, True)
                    one(i * 2 + 1, 1, True)
                one(ph.blocks - 2, 0, True)
                one(ph.blocks - 1, 1, False)

            def split(src, hi, lo, hi_signal, lo_signal, n_hi):
                dve.tensor_copy(hi, src).then_inc(hi_signal, 1)
                dve.wait_ge(hi_signal, n_hi)
                dve.tensor_tensor(lo, src, hi.bitcast(F32), ALU.subtract).then_inc(lo_signal, 1)

            def inverse_root(sums, squares, count, got_sums, var_signal, got_std, roots, out_):
                dve.wait_ge(*got_sums)
                dve.tensor_scalar(sums, squares, 1.0 / count, EPS, ALU.mult, ALU.add).then_inc(var_signal, 1)
                dve.wait_ge(*got_std)
                done(dve.reciprocal(out_, roots))
                done.wait()

            def norm(n, split_first=None):
                inverse_root(var, ssq, D, (n_ssq, T * (n + 1)), n_var, (n_std, n + 1), std, rstd)
                for t in range(T):
                    dve.tensor_scalar(xn[:, t, :], x[:, t, :], rstd[:, t:t + 1], None, ALU.mult).then_inc(n_xn, 1)
                if split_first:
                    split_lo(split_first, 0, range(LEAD))
                for b in range(KC // 2):
                    dve.wait_ge(n_f, n * KC + 2 * b + 2)
                    two = slice(2 * b, 2 * b + 2)
                    split(flat(hf[:, two, :]), flat(a_hi[:, two, :]), flat(a_lo[:, two, :]), n_hi, n_lo, n * (KC // 2) + b + 1)

            def log1p(e, den, s, s2, p):
                done(dve.tensor_scalar(den, e, 2.0, None, ALU.add))
                done.wait()
                done(dve.reciprocal(den, den))
                done.wait()
                done(dve.tensor_tensor(s, e, den, ALU.mult))
                done.wait()
                done(dve.tensor_tensor(s2, s, s, ALU.mult))
                done.wait()
                done(dve.tensor_scalar(p, s2, 1.0 / 19, None, ALU.mult))
                done.wait()
                for n in range(17, 1, -2):
                    done(dve.scalar_tensor_tensor(out=p, in0=p, scalar=1.0 / n, in1=s2, op0=ALU.add, op1=ALU.mult))
                    done.wait()
                done(dve.tensor_scalar(p, p, 1.0, 2.0, ALU.add, ALU.mult))
                done.wait()
                done(dve.tensor_tensor(p, p, s, ALU.mult))
                done.wait()

            def conv_taps(c, m0, taps, n_taps, width, dst, bias_signal, tap_signal, before):
                for j in range(1, n_taps):
                    for m in range(4):
                        if j == 1:
                            dve.wait_ge(bias_signal, m0 + m // 2 * 2 + 2)
                        else:
                            dve.wait_ge(tap_signal, before + 4 * (j - 2) + m + 1)
                        col = (n_taps - 1 - j) * width + m0 + m
                        dve.scalar_tensor_tensor(
                            out=dst[:, m0 + m, j:S], in0=pair[:, c, m // 2, (m % 2) * S:(m % 2 + 1) * S - j],
                            scalar=taps[:, col:col + 1], in1=dst[:, m0 + m, j:S], op0=ALU.mult, op1=ALU.add).then_inc(tap_signal, 1)

            dve.wait_ge(vec_ready, 2)
            dve.wait_ge(consts, CONSTS)
            dve.wait_ge(rows_landed, 16 * (len(row_loads) + 1))
            dve.scalar_tensor_tensor(out=l_abs, in0=lam, scalar=-1.0, in1=lam, op0=ALU.mult, op1=ALU.max).then_inc(prep_in, 1)
            done(dve.tensor_copy(pos_f, pos_i[:]))
            done.wait()
            for t in range(T):
                done(dve.tensor_scalar(ang[:, t * HALF_ROPE:(t + 1) * HALF_ROPE], freq, pos_f[:, t:t + 1], None, ALU.mult))
            done.wait()
            done(dve.tensor_scalar(turns, ang, float(1 / (2 * np.pi)), ROUND, ALU.mult, ALU.add))
            done.wait()
            done(dve.tensor_scalar(turns, turns, ROUND, None, ALU.subtract))
            done.wait()
            for n, part in enumerate((TWO_PI_1, TWO_PI_2, TWO_PI_3)):
                done(dve.scalar_tensor_tensor(out=ang_r, in0=turns, scalar=-part, in1=ang if n == 0 else ang_r, op0=ALU.mult, op1=ALU.add))
                done.wait()
            dve.tensor_scalar(ang_r, ang_r, 3.1415925, -3.1415925, ALU.min, ALU.max).then_inc(prep_in, 1)
            dve.wait_ge(prep_exp, 1)
            log1p(l_exp, l_den, l_s, l_s2, l_p)
            done(dve.tensor_scalar(l_max, lam, -1.0, 0.0, ALU.mult, ALU.max))
            done.wait()
            done(dve.tensor_tensor(l_p, l_p, l_max, ALU.add))
            done.wait()
            dve.tensor_scalar(ls8, l_p, -LRU_C, None, ALU.mult).then_inc(prep_in, 1)
            dve.tensor_scalar(nls8, l_p, LRU_C, None, ALU.mult).then_inc(prep_in, 1)
            dve.wait_ge(prep_exp, 4)
            done(dve.tensor_tensor(half_sin, half_sin, half_sin, ALU.mult))
            done.wait()
            done(dve.tensor_scalar(cos_t, half_sin, -2.0, 1.0, ALU.mult, ALU.add))
            done(dve.reciprocal(window_inv, window_inv))

            dve.wait_ge(c_ready, 1)

            def mod_products(b, c):
                for j in range(4):
                    dve.wait_ge(landed[j], b * 16 + 16)
                    for kk in range(4):
                        k = 4 * j + kk
                        if j == 0:
                            dve.tensor_scalar(mod_acc[:, c, kk, :], raw[:, j, kk, :], c_silu[:, k:k + 1], None, ALU.mult).then_inc(mod_step, 1)
                        else:
                            dve.wait_ge(mod_step, b * 16 + (k - 3))
                            dve.scalar_tensor_tensor(out=mod_acc[:, c, kk, :], in0=raw[:, j, kk, :], scalar=c_silu[:, k:k + 1],
                                                     in1=mod_acc[:, c, kk, :], op0=ALU.mult, op1=ALU.add).then_inc(mod_step, 1)

            mod_products(0, 0)
            mod_products(1, 1)
            with dve.Fori(1, MOD_BLOCKS // 2) as i:
                for c in range(2):
                    dve.wait_ge(mod_mm, i * 2 + (c - 1))
                    mod_products(i * 2 + c, c)
            dve.wait_ge(mod_mm, MOD_BLOCKS)
            dve.tensor_tensor(mod[:], misc[:, 3, 0:MODS * KC], b_ada, ALU.add).then_inc(mod_ready, 1)
            dve.wait_ge(mod_ready, 1)

            def modulated_gain(scale, g):
                done(dve.scalar_tensor_tensor(out=g_mod, in0=scale, scalar=1.0, in1=g, op0=ALU.add, op1=ALU.mult))
                done.wait()

            modulated_gain(mod[:, KC:2 * KC], g_mix)

            norm(0, w_in)

            def mixer(b):
                split_lo(w_in, b, range(LEAD, w_in.halves))
                if b + 1 < w_in.blocks:
                    split_lo(w_in, b + 1, range(LEAD))
                else:
                    split_lo(w_out, 0, range(LEAD))

            for b in range(2):
                mixer(b)
                conv_taps(b % 2, 4 * b, cw1, CONV, RC, xc, c1_bias, c1_tap, 12 * b)
            mixer(2)
            mixer(3)
            dve.wait_ge(gate_ev, 2 * RC)
            dve.wait_ge(c1_tap, 24)
            u_in = done(dve.tensor_tensor(flat(lru_u[:]), flat(lru_u[:]), flat(xc[:]), ALU.mult))
            dve.wait_ge(lru_t, RC)
            done(dve.tensor_scalar(flat(lru_den[:]), flat(lru_m[:]), 1.0, None, ALU.add))
            done.wait()
            done(dve.reciprocal(flat(lru_den[:]), flat(lru_den[:])))
            done.wait()
            dve.tensor_tensor(flat(lru_m[:]), flat(lru_m[:]), flat(lru_den[:]), ALU.mult).then_inc(lru_q, 1)
            dve.wait_ge(xp_ev, 2)
            src = xp
            for g, w in enumerate(POOL_WINDOWS):
                dst = (pool_a, pool_b)[g % 2]
                if g:
                    done.wait()
                done(dve.tensor_copy(dst[:, 2 * g:, 0:w // 2], src[:, 2 * g:, 0:w // 2]))
                done(dve.tensor_tensor(dst[:, 2 * g:, w // 2:], src[:, 2 * g:, w // 2:], src[:, 2 * g:, 0:S - w // 2], ALU.add))
                src = dst
            mixer(4)
            done.wait()
            for g, w in enumerate(POOL_WINDOWS):
                sums, two = (pool_a, pool_b)[g % 2], slice(2 * g, 2 * g + 2)
                done(dve.scalar_tensor_tensor(out=sums[:, two, 0:w - 1], in0=sums[:, two, 0:w - 1], scalar=float(w),
                                              in1=window_inv[:, None, 0:w - 1].to_broadcast([P, 2, w - 1]), op0=ALU.mult, op1=ALU.mult))
            done.wait()
            for g, w in enumerate(POOL_WINDOWS):
                sums, two = (pool_a, pool_b)[g % 2], slice(2 * g, 2 * g + 2)
                dve.scalar_tensor_tensor(out=xp[:, two, :], in0=sums[:, two, :], scalar=1.0 / w, in1=xp[:, two, :],
                                         op0=ALU.mult, op1=ALU.subtract).then_inc(pooled, 1)
            dve.wait_ge(lru_e, RC)
            dve.wait_ge(lru_r, 1)
            done(dve.tensor_tensor(flat(lru_u[:]), flat(lru_u[:]), flat(lru_m[:]), ALU.mult))
            done(dve.memset(lru_a[:, :, 0:1], 0.0))
            done.wait()
            h_done = done(dve.tensor_tensor_scan(flat(xc[:]), flat(lru_a[:]), flat(lru_u[:]), 0.0, ALU.mult, ALU.add))
            mixer(5)
            dve.wait_ge(w_used, w_in.end(w_in.blocks - 1))
            dve.wait_ge(pool_ev, 2 * G)
            split(flat(y_mix[:, RC:, :]), flat(a_hi[:, RC:, :]), flat(a_lo[:, RC:, :]), y_hi, y_lo, 1)
            dve.wait_ge(ge_ev, 2)
            done.wait(h_done)
            done(dve.tensor_tensor(flat(y_mix[:, 0:RC, :]), flat(y_mix[:, 0:RC, :]), flat(xc[:]), ALU.mult))
            done.wait()
            split(flat(y_mix[:, 0:RC, :]), flat(a_hi[:, 0:RC, :]), flat(a_lo[:, 0:RC, :]), y_hi, y_lo, 2)

            def add_gated(x0):
                def finish(b, c):
                    cols = bass.ds(b * COLS, COLS)
                    dve.tensor_tensor(res_tmp[:], pair[:, c], row[:, None, cols].to_broadcast([P, T, COLS]), ALU.mult).then_inc(res_ready, 1)
                    dve.wait_ge(res_ready, b + (x0 + 1))
                    dve.tensor_tensor(x[:, :, cols], x[:, :, cols], res_tmp[:], ALU.add).then_inc(x_new, 1)
                return finish

            def add_plain(b, c):
                cols = bass.ds(b * COLS, COLS)
                dve.tensor_tensor(x[:, :, cols], x[:, :, cols], pair[:, c], ALU.add).then_inc(x_new, 1)

            dve.wait_ge(row_ready, 1)
            stream(w_out, add_gated(0), up1)
            modulated_gain(mod[:, 4 * KC:5 * KC], g_ffn)
            norm(1)

            def hidden(b, c, source, blocks0):
                dve.wait_ge(ff_sig, b + (blocks0 + 1))
                dve.tensor_tensor(flat(ff_u[:]), flat(ff_g[:]), source, ALU.mult).then_inc(ff_prod, 1)
                dve.wait_ge(ff_prod, b + (blocks0 + 1))
                two = bass.ds(b * 2, 2)
                dve.tensor_copy(hid_hi[:, two, :], ff_u[:]).then_inc(h_hi, 1)
                dve.wait_ge(h_hi, b + (blocks0 + 1))
                dve.tensor_tensor(hid_lo[:, two, :], ff_u[:], hid_hi[:, two, :].bitcast(F32), ALU.subtract).then_inc(h_lo, 1)

            stream(up1, lambda b, c: hidden(b, c, pair[:, c, 1, :], 0), down1)
            dve.wait_ge(row_ready, 2)
            stream(down1, add_gated(w_out.blocks), w_in2)

            inverse_root(var, ssq, D, (fin_ssq, T), fin_var, (fin_std, 1), std, rstd)
            dve.wait_ge(fin_mm, 1)
            for t in range(T):
                dve.scalar_tensor_tensor(out=x[:, t, :], in0=x[:, t, :], scalar=rstd[:, t:t + 1], in1=flat(misc[:]),
                                         op0=ALU.mult, op1=ALU.mult).then_inc(fin_x, 1)
            dve.wait_ge(fin_x, T)
            norm(2)
            dve.wait_ge(dt_hi, 1)
            dve.tensor_tensor(flat(w_dt_lo[:]), flat(w_dt[:]), flat(w_dt_hi[:]).bitcast(F32), ALU.subtract).then_inc(dt_lo, 1)

            def mixer2(b):
                split_lo(w_in2, b, range(LEAD, w_in2.halves))
                if b + 1 < w_in2.blocks:
                    split_lo(w_in2, b + 1, range(LEAD))
                else:
                    split_lo(w_out2, 0, range(LEAD))

            def hn(a, t, h0, n):
                return a.rearrange("p (t h) -> p t h", t=T)[:, t, h0:h0 + n]

            def over_tiles(a):
                return a.rearrange("p (t h) -> p t h", t=T)

            for b in range(B_K):
                mixer2(b)
                dve.wait_ge(qkv_ev, b + 1)
                eight = slice(8 * b, 8 * b + 8)
                done(dve.tensor_tensor(q_sq[:, :, eight, :].rearrange("p t h e -> p t (h e)"), q_t[:, :, eight, :].rearrange("p t h e -> p t (h e)"),
                                       q_t[:, :, eight, :].rearrange("p t h e -> p t (h e)"), ALU.mult))
                done.wait()
                done(dve.tensor_reduce(over_tiles(hn_ssq)[:, :, eight], q_sq[:, :, eight, :], AX.X, ALU.add))
                if b == 1:
                    dve.wait_ge(dt_mm, 1)
                    dve.tensor_tensor(over_tiles(d_x), misc[:, 0, 0:T * SH].rearrange("p (t h) -> p t h", t=T),
                                      dt_bias[:, None, :].to_broadcast([P, T, SH]), ALU.add).then_inc(dt_raw, 1)
                    dve.wait_ge(dt_raw, 1)
                    dve.scalar_tensor_tensor(out=d_abs, in0=d_x, scalar=-1.0, in1=d_x, op0=ALU.mult, op1=ALU.max).then_inc(dt_x, 1)
            mixer2(B_K)
            dve.wait_ge(qkv_ev, B_K + 1)
            done(dve.tensor_tensor(flat3(k_sq[:]), flat3(k_t[:]), flat3(k_t[:]), ALU.mult))
            done.wait()
            done(dve.tensor_reduce(over_tiles(hn_ssq)[:, :, HEADS:], k_sq[:], AX.X, ALU.add))
            done.wait()
            dve.tensor_scalar(hn_var, hn_ssq, 1.0 / HD, EPS, ALU.mult, ALU.add).then_inc(hn_v, 1)
            mixer2(B_V)
            dve.wait_ge(dt_exp, 1)
            log1p(d_exp, d_den, d_s, d_s2, d_p)
            done(dve.tensor_scalar(d_max, d_x, 0.0, None, ALU.max))
            done.wait()
            done(dve.tensor_tensor(dt, d_p, d_max, ALU.add))
            done.wait()
            dve.scalar_tensor_tensor(out=over_tiles(a_dt), in0=over_tiles(dt), scalar=-1.0, in1=a_neg[:, None, :].to_broadcast([P, T, SH]),
                                     op0=ALU.mult, op1=ALU.mult).then_inc(a_ready, 1)

            dve.wait_ge(hn_s, 1)
            done(dve.reciprocal(hn_r, hn_std))
            done.wait()
            for a, h0, n, g in ((k_t, HEADS, KV, k_g), (q_t, 0, HEADS, q_g)):
                for t in range(T):
                    done(dve.tensor_tensor(a[:, t], a[:, t], hn(hn_r, t, h0, n)[:, :, None].to_broadcast([P, n, HD]), ALU.mult))
                done.wait()
                for t in range(T):
                    done(dve.tensor_tensor(a[:, t], a[:, t], g[:, None, :].to_broadcast([P, n, HD]), ALU.mult))
                done.wait()
                for t in range(T):
                    one, two = a[:, t, :, 0:HALF_ROPE], a[:, t, :, HALF_ROPE:2 * HALF_ROPE]
                    cos, sin = (v[:, None, t * HALF_ROPE:(t + 1) * HALF_ROPE].to_broadcast([P, n, HALF_ROPE]) for v in (cos_t, sin_t))
                    for i, (of, by) in enumerate(((one, cos), (two, sin), (two, cos), (one, sin))):
                        done(dve.tensor_tensor(rope[:, i, t, 0:n, :], of, by, ALU.mult))
                done.wait()
                for t in range(T):
                    done(dve.tensor_tensor(a[:, t, :, 0:HALF_ROPE], rope[:, 0, t, 0:n, :], rope[:, 1, t, 0:n, :], ALU.subtract))
                    last = dve.tensor_tensor(a[:, t, :, HALF_ROPE:2 * HALF_ROPE], rope[:, 2, t, 0:n, :], rope[:, 3, t, 0:n, :], ALU.add)
                    if a is q_t and t == T - 1:
                        last.then_inc(q_ready, 1)
                    else:
                        done(last)
                if a is k_t:
                    done.wait()
                    for t in range(T):
                        done(dve.tensor_copy(k_two[:, t, :, 0, :], k_t[:, t]))
                        last = dve.tensor_copy(k_two[:, t, :, 1, :], k_t[:, t])
                        if t == T - 1:
                            last.then_inc(k_ready, 1)
                        else:
                            done(last)

            def group(a, g):
                return by_block(a)[:, :, 16 * g:16 * g + 16]

            for g in range(2):
                if g:
                    dve.wait_ge(p_turned, 8)
                for i in range(8 * g, 8 * g + 8):
                    dve.wait_ge(sc_mm, i + 1)
                    bank = 2 * (i % 2)
                    dve.scalar_tensor_tensor(out=scores[:, 2 * (i - 8 * g):2 * (i - 8 * g) + 2, :], in0=misc[:, bank:bank + 2, 0:3 * P],
                                             scalar=float(HD) ** -0.5, in1=a_mask[:, None, :].to_broadcast([P, 2, 3 * P]),
                                             op0=ALU.mult, op1=ALU.add).then_inc(sc_ev, 1)
                dve.wait_ge(sc_ev, 8 * g + 8)
                done(dve.tensor_reduce(group(m_max, g)[:, 1], scores[:, :, 0:S], AX.X, ALU.max))
                done(dve.tensor_reduce(group(m_max, g)[:, 0], scores[:, :, S:3 * P], AX.X, ALU.max))
                done.wait()
                sink = sinks[:, None, 16 * g:16 * g + 16].to_broadcast([P, 2, 16])
                done(dve.tensor_tensor(group(m_all, g), group(m_max, g), sink, ALU.max))
                done.wait()
                done(dve.tensor_scalar(group(m_neg, g), group(m_all, g), -1.0, None, ALU.mult))
                done.wait()
                dve.tensor_tensor(group(m_sink, g), group(m_neg, g), sink, ALU.add).then_inc(sc_max, 1)
                dve.wait_ge(sink_exp, g + 1)
                dve.wait_ge(sc_exp, 32 * g + 32)
                done(dve.tensor_tensor(group(e_den, g), group(e_sum, g), group(e_sink, g), ALU.add))
                done.wait()
                done(dve.reciprocal(group(e_inv, g), group(e_den, g)))
                done.wait()
                for i in range(8 * g, 8 * g + 8):
                    dve.wait_ge(pv_mm, i + 1)
                    bank, two = 2 * (i % 2), slice(2 * i, 2 * i + 2)
                    for blk in range(2):
                        ins = dve.tensor_tensor(o_t[:, blk, two, :], misc[:, bank + blk, 3 * P:].rearrange("p (h e) -> p h e", h=2),
                                                by_block(e_inv)[:, blk, two][:, :, None].to_broadcast([P, 2, HD]), ALU.mult)
                        if blk:
                            ins.then_inc(o_ev, 1)

            for b in range(B_XBC, B_Z):
                j = b - B_XBC
                mixer2(b)
                conv_taps(b % 2, 4 * j, cw2, CONV, XBC, xbc, c2_bias, c2_tap, 12 * j)
            for b in range(B_Z, w_in2.blocks):
                mixer2(b)

            def heads(a, t):
                return a[:, t * SH:(t + 1) * SH][:, :, None].to_broadcast([P, SH, SP])

            dve.wait_ge(a_ready, 1)
            for t in range(T):
                dve.wait_ge(xs_ev, 4 * (t + 1))
                dve.tensor_tensor(xdt[:, t], xs_t[:, t], heads(dt, t), ALU.mult).then_inc(xdt_ready, 1)
            dve.wait_ge(cs_ev, 2)
            dve.tensor_tensor(to_last, a_last, a_cs[:, 0:SH], ALU.subtract).then_inc(end_in, 1)
            dve.wait_ge(end_ev, 2)
            dve.wait_ge(xdt_ready, 2)
            dve.tensor_tensor(state[:], xdt[:, 0], heads(to_last, 0), ALU.mult).then_inc(st_in, 1)
            for c in range(T):
                dve.wait_ge(cb_mm, c + 1)
                dve.tensor_tensor(cb[:], misc[:, 0, :].rearrange("p (g l) -> p g l", g=SG), upper[:, None, :].to_broadcast([P, SG, P]),
                                  ALU.mult).then_inc(cb_ev, 1)
                if c:
                    dve.wait_ge(yd_mm, c)
                for n in range(SH // 4):
                    dve.wait_ge(seg_mm, 8 * c + n + 1)
                    h = slice(c * SH + 4 * n, c * SH + 4 * n + 4)
                    dve.tensor_tensor(decay[:, 4 * n:4 * n + 4, :], misc[:, 1 + n % 3, :].rearrange("p (h l) -> p h l", h=4),
                                      a_cs[:, h][:, :, None].to_broadcast([P, 4, P]), ALU.subtract).then_inc(seg_ev, 1)
                    if n % 2:
                        g = n // 2
                        dve.wait_ge(seg_ev, 8 * c + n + 1)
                        part = flat(decay[:, 8 * g:8 * g + 8, :])
                        dve.tensor_scalar(part, part, 0.0, None, ALU.min).then_inc(seg_min, 1)
                dve.wait_ge(cb_ev, c + 1)
                for g in range(SG):
                    dve.wait_ge(seg_exp, SG * c + g + 1)
                    dve.tensor_tensor(decay[:, 8 * g:8 * g + 8, :], decay[:, 8 * g:8 * g + 8, :], cb[:, g:g + 1, :].to_broadcast([P, 8, P]),
                                      ALU.mult).then_inc(decay_ready, 1)
                done(dve.tensor_tensor(xs_t[:, c], xs_t[:, c], heads(d_skip, 0), ALU.mult))
                done.wait()
                dve.wait_ge(yd_mm, c + 1)
                dve.tensor_tensor(flat(y_t[:, c]), flat(xs_t[:, c]), flat(misc[:]), ALU.add).then_inc(yd_ev, 1)
            dve.wait_ge(yo_mm, 1)
            dve.wait_ge(yd_ev, 2)
            dve.tensor_tensor(xs_t[:, 1], pair.rearrange("p a b (h e) -> p (a b h) e", e=SP), heads(from_start, 0), ALU.mult).then_inc(yo_ev, 1)
            dve.wait_ge(yo_ev, 1)
            done(dve.tensor_tensor(flat(y_t[:, 1]), flat(y_t[:, 1]), flat(xs_t[:, 1]), ALU.add))
            done.wait()
            dve.wait_ge(z_ev, 4)
            for t in range(T):
                done(dve.tensor_tensor(flat(y_t[:, t]), flat(y_t[:, t]), z_t[:, t, :], ALU.mult))
            done.wait()
            for t in range(T):
                done(dve.tensor_tensor(flat(xs_t[:, t]), flat(y_t[:, t]), flat(y_t[:, t]), ALU.mult))
            done.wait()
            done(dve.tensor_reduce(g_ssq, xs_t.rearrange("p t (g h) e -> p (t g) (h e)", g=SG), AX.X, ALU.add))
            done.wait()
            dve.tensor_scalar(g_var, g_ssq, SG / D, EPS, ALU.mult, ALU.add).then_inc(g_v, 1)
            for f in range(KC // 2):
                two = slice(2 * f, 2 * f + 2)
                dve.wait_ge(ya_hi, f + 1)
                dve.tensor_tensor(flat(a_lo[:, two, :]), misc[:, f % 4, :], flat(a_hi[:, two, :]).bitcast(F32), ALU.subtract).then_inc(ya_lo, 1)
                if f == 1:
                    dve.wait_ge(g_s, 1)
                    done(dve.reciprocal(g_rstd, g_std))
                    done.wait()
                    for t in range(T):
                        dve.tensor_tensor(y_t[:, t].rearrange("p (g h) e -> p g (h e)", g=SG), y_t[:, t].rearrange("p (g h) e -> p g (h e)", g=SG),
                                          g_rstd[:, SG * t:SG * t + SG][:, :, None].to_broadcast([P, SG, D // SG]), ALU.mult).then_inc(ys_ready, 1)
            for f in range(KC // 2):
                two = slice(2 * f, 2 * f + 2)
                dve.wait_ge(ys_f, 2 * f + 2)
                split(flat(s_f[:, two, :]), flat(s_hi[:, two, :]), flat(s_lo[:, two, :]), ys_hi, ys_lo, f + 1)

            stream(w_out2, add_plain, up2)
            norm(3)

            def finish_up2(b, c):
                for j in range(1, FFN_CONV):
                    for m in range(4):
                        if j == 1:
                            dve.wait_ge(c3_bias, b * 4 + (m // 2 * 2 + 2))
                        else:
                            dve.wait_ge(c3_tap, b * 8 + (m + 1))
                        dst, m0 = ((ff_g, 0), (ff_u, HC))[m // 2]
                        dve.scalar_tensor_tensor(
                            out=dst[:, m % 2, j:S], in0=pair[:, c, m // 2, (m % 2) * S:(m % 2 + 1) * S - j],
                            scalar=vec[:, 4 + FFN_CONV - 1 - j, bass.ds(b * 2 + (m0 + m % 2), 1)], in1=dst[:, m % 2, j:S],
                            op0=ALU.mult, op1=ALU.add).then_inc(c3_tap, 1)
                hidden(b, c, flat(ff_u[:]), up1.blocks)

            stream(up2, finish_up2, down2)
            stream(down2, add_plain, ple_gate)

            norm(4)
            inverse_root(var, ssq, D, (pe_ssq, T), pe_v, (pe_s, 1), std, rstd)
            dve.wait_ge(post_mm, 1)
            for t in range(T):
                dve.scalar_tensor_tensor(out=pe_t[:, t, :], in0=pe_t[:, t, :], scalar=rstd[:, t:t + 1], in1=flat(misc[:]),
                                         op0=ALU.mult, op1=ALU.mult).then_inc(pe_ready, 1)
            dve.wait_ge(pe_ready, T)
            for b in range(ple_gate.blocks):
                split_lo(ple_gate, b, range(LEAD, ple_gate.halves))
                if b + 1 < ple_gate.blocks:
                    split_lo(ple_gate, b + 1, range(LEAD))
                cols = slice(b * COLS, (b + 1) * COLS)
                dve.wait_ge(gate_sig, b + 1)
                done(dve.tensor_tensor(sig[:], sig[:], pe_t[:, :, cols], ALU.mult))
                done.wait()
                dve.tensor_tensor(x[:, :, cols], x[:, :, cols], sig[:], ALU.add).then_inc(x_out, 1)


NAMES = ["x", "c", "w_ada", "b_ada", "g_norm_mix", "w_in", "w_conv", "b_conv", "w_rg_a", "b_rg_a", "w_rg_i", "b_rg_i",
         "lru_lambda", "w_pool", "ls_pool", "w_out", "g_norm_ffn", "w_ffn_gate", "w_ffn_up", "w_ffn_down",
         "g_norm_final", "p_2", "positions_2", "attn_norm_g_2", "w_in_2", "conv_w_2", "conv_b_2", "dt_bias_2",
         "a_log_2", "d_skip_2", "ssm_norm_g_2", "q_norm_g_2", "k_norm_g_2", "sinks_2", "w_out_2", "ffn_norm_g_2",
         "w_up_2", "ffn_conv_w_2", "ffn_conv_b_2", "w_down_2", "ple_norm_g_2", "w_ple_gate_2", "w_ple_proj_2",
         "ple_post_g_2"]


def kernel(**inputs):
    from concourse import bacc
    from concourse.bass_utils import run_bass_kernel_spmd

    nc = bacc.Bacc("TRN2", target_bir_lowering=False, num_devices=1, dynamic_dma_scratch_size=1024)
    arrays = {f"in_{name}": np.ascontiguousarray(inputs[name]) for name in NAMES}
    d = {name: nc.dram_tensor(f"in_{name}", a.shape, mybir.dt.from_np(a.dtype), kind="ExternalInput").ap()
         for name, a in zip(NAMES, arrays.values())}
    out = nc.dram_tensor("out", arrays["in_x"].shape, F32, kind="ExternalOutput").ap()
    two_blocks(nc, d, out)
    return run_bass_kernel_spmd(nc, [arrays], core_ids=[0]).results[0]["out"]
```

```python
from contextlib import ExitStack

import numpy as np

import concourse.bass as bass
from concourse import mybir

F32 = mybir.dt.float32
F32R = mybir.dt.float32r
I32 = mybir.dt.int32
ALU = mybir.AluOpType
ACT = mybir.ActivationFunctionType
AX = mybir.AxisListType

P = 128
KB = 1024
EPS = 1e-6
COLS = 512
RAW_SLOTS = 4
HALF_SLOTS = 4
LEAD = 3
CONV = 4
FFN_CONV = 3
LRU_C = 8.0
MOD_COLS = 1024
MOD_SLOTS = 4
POOL_WINDOWS = (2, 4, 8, 16)
ROPE_THETA = 500000.0
HALF_ROPE = 8
MASKED = -1e30
ROUND = 12582912.0
TWO_PI_1 = 6.28125
TWO_PI_2 = float(np.float32(np.round((2 * np.pi - TWO_PI_1) * 2.0**20) / 2.0**20))
TWO_PI_3 = float(np.float32(2 * np.pi - TWO_PI_1 - TWO_PI_2))


class Phase:

    def __init__(self, before, blocks, rows, dmas=1, first=0, lead=LEAD):
        self.blocks, self.rows = blocks, rows
        self.tiles, self.halves = len(rows), 2 * len(rows)
        self.tile0 = before.tile0 + before.blocks * before.tiles if before else 0
        self.landed0 = before.landed1 if before else 0
        self.unit, self.lead = 16 * dmas, lead
        self.landed1 = self.landed0 + self.unit * blocks * self.tiles // RAW_SLOTS
        assert self.tiles % RAW_SLOTS == 0 and blocks % 2 == 0
        self.row0 = [(first + sum(rows[:j])) % sum(rows) for j in range(self.tiles)]

    def half(self, b):
        return b * self.halves + 2 * self.tile0

    def end(self, b):
        return b * self.halves + (2 * self.tile0 + self.halves)

    def tile(self, b):
        return b * self.tiles + self.tile0

    def landed(self, b, j):
        return b * (self.unit * self.tiles // RAW_SLOTS) + (self.landed0 + self.unit * (j // RAW_SLOTS + 1))

    def half_rows(self, h):
        rows = self.rows[h // 2]
        first = (rows + 1) // 2
        return (0, self.row0[h // 2], first) if h % 2 == 0 else (first, self.row0[h // 2] + first, rows - first)


def two_blocks(nc, d, out):
    S, D = d["x"].shape[1:]
    T, KC = S // P, D // P
    HC = d["w_ffn_gate"].shape[2] // P
    RC = d["w_conv"].shape[2] // P
    MODS = d["w_ada"].shape[2] // D
    G = d["w_pool"].shape[1]
    HEADS, HD = d["sinks_2"].shape[1], d["q_norm_g_2"].shape[1]
    KV = HEADS // 4
    SH, SG = d["dt_bias_2"].shape[1], 4
    SP = D // SH
    XBC = d["conv_b_2"].shape[1] // P
    PLE = d["p_2"].shape[3]
    O_XBC = D
    O_DT = O_XBC + XBC * P
    O_Q = O_DT + SH
    O_K = O_Q + D
    O_V = O_K + KV * HD
    assert T == 2 and HEADS == SH == 32 and HD == SP == 64 and RC == 8 and G == 4 and KV == 8

    four = [4] * 4
    down_rows = [4] * 8 + [3] * 4
    assert sum(down_rows) == HC and sum(four) == KC
    w_in = Phase(None, 6, four)
    w_out = Phase(w_in, 4, four, first=RC)
    up1 = Phase(w_out, HC // 2, four, dmas=2)
    down1 = Phase(up1, 4, down_rows)
    w_in2 = Phase(down1, 16, four)
    w_out2 = Phase(w_in2, 4, [4] * 8, first=KC)
    up2 = Phase(w_out2, HC // 2, four, dmas=2, lead=LEAD + 1)
    down2 = Phase(up2, 4, down_rows)
    ple_gate = Phase(down2, 4, four)
    w_in_cols = [0, COLS, 2 * RC * P, 2 * RC * P + COLS, RC * P, RC * P + COLS]
    w_in2_cols = [O_Q + COLS * j for j in range(4)] + [O_K, O_V] + [O_XBC + COLS * j for j in range(6)] \
        + [COLS * j for j in range(4)]
    B_K, B_V, B_XBC, B_Z = 4, 5, 6, 12
    K_PLACE, V_PLACE = (B_K - B_XBC) * w_in2.halves, (B_V - B_XBC) * w_in2.halves
    Q_TURN, K_TURN, PAIR_START, PAIR_STEP = V_PLACE + 2, 1, 4, 2
    PAIRS = HEADS // 2
    EXP_LAG, TURN_LAG, VALUE_LAG = 1, 2, 3
    assert PAIR_START + PAIR_STEP * (PAIRS + VALUE_LAG) <= (B_Z - B_XBC) * w_in2.halves
    Z0 = (B_Z - B_XBC) * w_in2.halves
    B_TURN, STATE, FROM_STATE, DECAYS, WITHIN = 5, 10, 12, (14, 23), (21, 30)
    Y_TURN = 4
    MOD_BLOCKS, MOD_M = MODS * D // MOD_COLS, MOD_COLS // P
    MOD_FIRST = 2 * D // MOD_COLS
    mod_places = [2, 1, 1, 1, 2, 1, 1, 1] * 3 + [1, 1, 1, 0, 1, 1, 1, 0] * 3 + [2] * 20 + [1] * 8 + [0] * 4 + [1, 0] * (4 * up1.halves)
    assert MOD_FIRST * KC + sum(mod_places) == MOD_BLOCKS * KC and MOD_FIRST == 4 and MOD_BLOCKS == 12

    def mod_at(place):
        n = MOD_FIRST * KC + sum(mod_places[:place])
        return range(n, n + mod_places[place])

    with ExitStack() as ctx:
        size = 222 * KB
        base = -(-nc.sbuf_base // 64) * 64
        ctx.enter_context(nc.sbuf_tensor("arena", [P, size // 4], F32, align_bytes=64))
        assert nc.sbuf_base == base + size

        def at(name, kb, shape, dtype=F32):
            assert kb * KB + 4 * int(np.prod(shape[1:])) <= size, name
            return nc.alloc_sbuf_tensor_at(name, shape, dtype, offset=base + int(kb * KB))

        def sem(name):
            return ctx.enter_context(nc.semaphore(name))

        raw = at("raw", 0, [P, RAW_SLOTS, 4, COLS])
        w_hi = at("w_hi", 32, [P, HALF_SLOTS, 2, COLS], F32R)
        w_lo = at("w_lo", 48, [P, HALF_SLOTS, 2, COLS], F32R)
        x = at("x_res", 64, [P, T, D])
        a_hi = at("a_hi", 80, [P, KC, S], F32R)
        a_lo = at("a_lo", 96, [P, KC, S], F32R)
        R = 112
        row = at("row", R, [P, D])
        page = at("page", R, [P, D])
        state = at("state", R, [P, SH, SP])
        C = 120
        ident = at("ident", C, [P, P])
        ones = at("ones", C + 0.5, [P, P])
        upper = at("upper", C + 1, [P, P])
        a_mask = at("a_mask", C + 1.5, [P, 3 * P])
        vec = at("vec", C + 3, [P, 7, P])
        mod = at("mod", C + 6.5, [P, MODS * KC])
        pos_i = at("pos_i", C + 6.9375, [P, T], I32)
        rows = at("rows", C + 7, [P, 256])
        keep = at("keep", C + 8, [P, 512])
        F = 130
        xn = at("xn", F, [P, T, D])
        xn_sq = at("xn_sq", F + 32, [P, T, D])
        features_a = at("features_a", 96, [P, KC, S])
        norm_features = [at("features_0", F + 16, [P, KC, S]), features_a, features_a, at("features_3", F + 32, [P, KC, S]), features_a]
        squares_a, diag_a = at("squares_a", 80, [P, T, COLS]), at("diag_a", 84, [P, T, P])
        norm_squares = [None, squares_a, squares_a, at("squares_3", F + 48, [P, T, COLS]), squares_a]
        norm_diag = [None, diag_a, diag_a, at("diag_3", F + 52, [P, T, P]), diag_a]
        c_rows = at("c_rows", F + 48, [P, P])
        vec_rows = at("vec_rows", F + 52, [P, 7, P])
        mod_raw = at("mod_raw", F + 64, [P, MOD_SLOTS, MOD_COLS])
        mod_acc = at("mod_acc", F + 80, [P, 2, MOD_COLS])
        xc = at("xc", F, [P, RC, S])
        lru_a = at("lru_a", F + 8, [P, RC, S])
        lru_u = at("lru_u", F + 16, [P, RC, S])
        lru_hi = at("lru_hi", F + 16, [P, RC, S], F32R)
        lru_lo = at("lru_lo", F + 32, [P, RC, S], F32R)
        pool_hi = at("pool_hi", F + 48, [P, RC, S], F32R)
        pool_lo = at("pool_lo", F + 56, [P, RC, S], F32R)
        y_lru = at("y_lru", F + 24, [P, RC, S])
        lru_m = at("lru_m", F + 32, [P, RC, S])
        xp = at("xp", F + 40, [P, RC, S])
        gates_w = at("gates_w", F + 48, [P, 2, RC, P])
        lru_sq = at("lru_sq", F + 48, [P, RC, S])
        pool_b = at("pool_b", F + 48, [P, RC, S])
        pool_w = at("pool_w", F + 56, [P, 2 * G, 2 * P])
        pool_a = at("pool_a", R, [P, RC, S])
        res_tmp = at("res_tmp", F + 88, [P, T, COLS])
        hid_hi = at("hid_hi", F, [P, HC, S], F32R)
        hid_lo = at("hid_lo", F + 44, [P, HC, S], F32R)
        ff_g = at("ff_g", F + 88, [P, 2, S])
        ff_u = at("ff_u", F + 90, [P, 2, S])
        k_t = at("k_t", F, [P, T, KV, HD])
        k_two = at("k_two", F + 4, [P, T, KV, 2, HD])
        rope = at("rope", F + 16, [P, 4, T, HEADS, HALF_ROPE])
        q_sq = at("q_sq", F + 24, [P, T, HEADS, HD])
        k_sq = at("k_sq", F + 40, [P, T, KV, HD])
        w_dt = at("w_dt", F + 52, [P, KC, SH])
        w_dt_hi = at("w_dt_hi", F + 54, [P, KC, SH], F32R)
        w_dt_lo = at("w_dt_lo", F + 56, [P, KC, SH], F32R)
        q_tr = at("q_tr", F + 24, [P, KC, S])
        k_tr = at("k_tr", F + 40, [P, KV, S])
        v_t = at("v_t", F + 48, [P, T, KV, HD])
        scores = at("scores", F + 52, [P, 4, 2, 3 * P])
        p_tr = at("p_tr", F + 64, [P, 2, 2, 3 * P])
        q_t = at("q_t", F + 72, [P, T, HEADS, HD])
        o_t = at("o_t", F + 72, [P, T, HEADS, HD])
        xbc = at("xbc", F, [P, XBC, S])
        decay = at("decay", F, [P, SH, P])
        xs_t = at("xs_t", F + 24, [P, T, SH, SP])
        xdt = at("xdt", F + 40, [P, T, SH, SP])
        y_t = at("y_t", F + 40, [P, T, SH, SP])
        z_t = at("z_t", F + 56, [P, T, D])
        b_tok = at("b_tok", F + 88, [P, SG, P])
        cb = at("cb", F + 90, [P, SG, P])
        s_hi = at("s_hi", F, [P, KC, S], F32R)
        s_lo = at("s_lo", F + 16, [P, KC, S], F32R)
        g_diag = at("g_diag", F + 56, [P, T * SG, P])
        g_sq = at("g_sq", F + 64, [P, 4, D // SG])
        pe_t = at("pe_t", F + 32, [P, T, D])
        p_t = at("p_t", F + 48, [P, T, PLE])
        p_f = at("p_f", F + 50, [P, PLE // P, S])
        w_ple = at("w_ple", F + 52, [P, PLE // P, D])
        sig = at("sig", F + 68, [P, T, COLS])
        pe_sq = at("pe_sq", F + 72, [P, D])

        pair = ctx.enter_context(nc.psum_tensor("pair", [P, 2, 2, COLS], F32))
        misc = ctx.enter_context(nc.psum_tensor("misc", [P, 4, COLS], F32))

        b_ada, g_mix, g_ffn = vec[:, 0, 0:96], vec[:, 0, 96:112], vec[:, 0, 112:128]
        cw1, cb1 = vec[:, 1, 0:32], vec[:, 1, 32:40]
        b_ra, b_ri, lam, ls_pool = (vec[:, 1, 40 + 8 * n:48 + 8 * n] for n in range(4))
        g_att, g_fin, g_ssm = (vec[:, 1, 72 + 16 * n:88 + 16 * n] for n in range(3))
        cw2, g_ffn2, g_ple = vec[:, 2, 0:96], vec[:, 2, 96:112], vec[:, 2, 112:128]
        cb2, cb3, g_post = vec[:, 3, 0:24], vec[:, 3, 24:112], vec[:, 3, 112:128]

        def by_chunk(a):
            return a.rearrange("(n p) -> n p", p=P)

        vec_loads = [
            (0, 0, by_chunk(d["b_ada"][0])), (0, 96, by_chunk(d["g_norm_mix"][0])), (0, 112, by_chunk(d["g_norm_ffn"][0])),
            *[(1, RC * j, by_chunk(d["w_conv"][0, j])) for j in range(CONV)],
            (1, 32, by_chunk(d["b_conv"][0])), (1, 40, by_chunk(d["b_rg_a"][0])), (1, 48, by_chunk(d["b_rg_i"][0])),
            (1, 56, by_chunk(d["lru_lambda"][0])), (1, 64, d["ls_pool"][0].rearrange("g (n p) -> (g n) p", p=P)),
            (1, 72, by_chunk(d["attn_norm_g_2"][0])), (1, 88, by_chunk(d["g_norm_final"])),
            (1, 104, by_chunk(d["ssm_norm_g_2"][0])),
            *[(2, XBC * j, by_chunk(d["conv_w_2"][0, j])) for j in range(CONV)],
            (2, 96, by_chunk(d["ffn_norm_g_2"][0])), (2, 112, by_chunk(d["ple_norm_g_2"][0])),
            (3, 0, by_chunk(d["conv_b_2"][0])), (3, 24, by_chunk(d["ffn_conv_b_2"][0])), (3, 112, by_chunk(d["ple_post_g_2"][0])),
            *[(4 + j, 0, by_chunk(d["ffn_conv_w_2"][0, j])) for j in range(FFN_CONV)],
        ]
        dt_bias, a_log, d_skip, sinks = (rows[:, 32 * n:32 * n + 32] for n in range(4))
        q_g, k_g = rows[:, 128:192], rows[:, 192:256]
        row_loads = [(dt_bias, d["dt_bias_2"]), (a_log, d["a_log_2"]), (d_skip, d["d_skip_2"]), (sinks, d["sinks_2"]),
                     (q_g, d["q_norm_g_2"]), (k_g, d["k_norm_g_2"])]

        def columns(tile, widths):
            ends = np.cumsum(widths)
            assert ends[-1] <= tile.shape[1]
            return [tile[:, int(e) - w:int(e)] for e, w in zip(ends, widths)]

        ssq, var, std, rstd, c_silu, g_mod, ls8, nls8, window_inv, ssq_parts, scale, squared = columns(
            keep, [T, T, T, T, KC, KC, RC, RC, 16, T * 4, T, T])
        g_both, g_weigh = mod[:, 2 * KC:3 * KC], mod[:, 0:2 * KC].rearrange("p (m n) -> p m n", n=2)
        dt, a_dt, a_cs, a_neg, to_last, from_start, a_last, cos_t, sin_t = columns(
            keep[:, 96:512], [T * SH, T * SH, T * SH, SH, SH, SH, SH, T * HALF_ROPE, T * HALF_ROPE])
        g_ssq, g_var, g_std, g_rstd = columns(keep[:, 450:512], [T * SG] * 4)
        l_abs, l_exp, l_den, l_s, l_s2, l_p, l_max = columns(page, [RC] * 7)
        freq, pos_f, ang, turns, ang_r, half_sin = columns(page[:, 64:512], [HALF_ROPE, T] + [T * HALF_ROPE] * 4)
        hn_ssq, hn_var, hn_std, hn_r = columns(page[:, 512:1024], [T * (HEADS + KV)] * 4)
        d_x, d_abs, d_exp, d_den, d_s, d_s2, d_p, d_max = columns(page[:, 1024:1536], [T * SH] * 8)
        m_max, m_all, m_neg, m_sink, e_sink, e_sum, e_den, e_inv = columns(page[:, 1536:2048], [2 * HEADS] * 8)

        mod_landed = [sem(f"mod_landed{n}") for n in range(MOD_SLOTS)]
        landed = [sem(f"raw_landed{n}") for n in range(RAW_SLOTS)]
        hi_ready, lo_ready, w_used = sem("hi_ready"), sem("lo_ready"), sem("w_used")
        x_landed, vec_landed, rows_landed, mixw_landed = (sem(n) for n in ("x_landed", "vec_landed", "rows_landed", "mixw_landed"))
        dt_landed, ple_landed, stored = sem("dt_landed"), sem("ple_landed"), sem("stored")
        vec_zero, gates_zero, consts = sem("vec_zero"), sem("gates_zero"), sem("consts")
        pool_step, act_step, dve_step = sem("pool_step"), sem("act_step"), sem("dve_step")
        vec_turned, vec_ready, c_ready = sem("vec_turned"), sem("vec_ready"), sem("c_ready")
        c_landed, c_turned, n_rstd = sem("c_landed"), sem("c_turned"), sem("norm_rstd")
        prep_in, prep_exp = sem("prep_in"), sem("prep_exp")
        mod_step, mod_mm, mod_ready = sem("mod_step"), sem("mod_mm"), sem("mod_ready")
        n_ssq, n_var, n_std, n_xn, n_turned, n_f, n_hi, n_lo, n_gain, n_sq, n_sums, n_diag, n_row, n_scaled = (
            sem("norm_" + n) for n in ("ssq", "var", "std", "xn", "turned", "f", "hi", "lo", "gain", "sq", "sums", "diag", "row", "scaled"))
        x_new = sem("x_new")
        c1_bias, c1_tap, gate_mm, gate_ev, xp_ev, ge_ev = (sem(n) for n in ("c1_bias", "c1_tap", "gate_mm", "gate_ev", "xp_ev", "ge_ev"))
        lru_s = sem("lru_s")
        lru_t, lru_e, lru_q, lru_r, pooled, pool_mm, pool_hi_ev, pool_lo_ev, lru_y, lru_hi_ev, lru_lo_ev = (
            sem(n) for n in ("lru_t", "lru_e", "lru_q", "lru_r", "pooled", "pool_mm", "pool_hi_ev", "pool_lo_ev", "lru_y", "lru_hi_ev",
                             "lru_lo_ev"))
        row_mm, row_ready, fin_mm, fin_x = (sem(n) for n in ("row_mm", "row_ready", "fin_mm", "fin_x"))
        ff_sig, ff_prod, h_hi, h_lo, c3_bias, c3_tap = (sem(n) for n in ("ff_sig", "ff_prod", "h_hi", "h_lo", "c3_bias", "c3_tap"))
        qkv_ev, dt_hi, dt_lo, dt_mm, dt_x, dt_exp, hn_v, hn_s, k_ready, q_ready, qk_turned, qk_ev = (
            sem(n) for n in ("qkv_ev", "dt_hi", "dt_lo", "dt_mm", "dt_x", "dt_exp", "hn_v", "hn_s", "k_ready", "q_ready",
                             "qk_turned", "qk_ev"))
        sc_mm, sc_ev, sc_max, sink_exp, sc_exp, p_turned, p_ev, pv_mm, o_ev = (
            sem(n) for n in ("sc_mm", "sc_ev", "sc_max", "sink_exp", "sc_exp", "p_turned", "p_ev", "pv_mm", "o_ev"))
        c2_bias, c2_tap, xbc_ev, z_ev, a_ready, cs_mm, cs_ev, end_ev, xs_turned, xs_ev, b_turned, b_ev = (
            sem(n) for n in ("c2_bias", "c2_tap", "xbc_ev", "z_ev", "a_ready", "cs_mm", "cs_ev", "end_ev", "xs_turned", "xs_ev",
                             "b_turned", "b_ev"))
        xdt_ready, cb_mm, cb_ev, seg_mm, seg_ev, seg_min, seg_exp, decay_ready, yd_mm, yd_ev, st_in, st_mm, st_ev, yo_mm, yo_ev = (
            sem(n) for n in ("xdt_ready", "cb_mm", "cb_ev", "seg_mm", "seg_ev", "seg_min", "seg_exp", "decay_ready", "yd_mm", "yd_ev",
                             "st_in", "st_mm", "st_ev", "yo_mm", "yo_ev"))
        gated, g_sums, g_v, g_s, ys_ready, ys_turned, ys_hi, ys_lo, yo_turned, ya_hi, ya_lo = (
            sem(n) for n in ("gated", "g_sums", "g_v", "g_s", "ys_ready", "ys_turned", "ys_hi", "ys_lo", "yo_turned", "ya_hi", "ya_lo"))
        pt_turned, pt_ev, pe_mm, pe_ev, pe_ssq, pe_v, pe_s, post_mm, pe_ready, gate_sig, x_out = (
            sem(n) for n in ("pt_turned", "pt_ev", "pe_mm", "pe_ev", "pe_ssq", "pe_v", "pe_s", "post_mm", "pe_ready", "gate_sig",
                             "x_out"))

        class Steps:

            def __init__(self, eng, steps):
                self.eng, self.steps, self.n = eng, steps, 0

            def __call__(self, ins):
                ins.then_inc(self.steps, 1)
                self.n += 1
                return self.n

            def wait(self, n=None):
                self.eng.wait_ge(self.steps, self.n if n is None else n)

        X_BEFORE = [0, 0, w_out.blocks, w_out.blocks + down1.blocks, w_out.blocks + down1.blocks + w_out2.blocks]
        XB = D // COLS
        XG = KC // 2
        SSQ_DONE, ROOTS = [T, T + T * XB, None, T + 2 * T * XB, T + 3 * T * XB], [1, 2, (3, 4), 5, 6]

        def flat(a):
            return a.rearrange("p a b -> p (a b)")

        def flat3(a):
            return a.rearrange("p a b c -> p (a b c)")

        def q_part(a):
            return a.rearrange("p (t h) -> p t h", t=T)[:, :, 0:HEADS]

        def k_part(a):
            return a.rearrange("p (t h) -> p t h", t=T)[:, :, HEADS:]

        def by_block(a):
            return a.rearrange("p (b h) -> p b h", b=2)

        end_in, dt_raw, res_ready = sem("end_in"), sem("dt_raw"), sem("res_ready")
        block = ctx.enter_context(nc.Block())

        @block.gpsimd
        def _(pool):
            done = Steps(pool, pool_step)
            done(pool.memset(ident[:], 0.0))
            done.wait()
            pool.affine_select(out=ident[:], in_=ident[:], compare_op=ALU.not_equal, fill=1.0, base=0,
                               pattern=[[-1, P]], channel_multiplier=1).then_inc(consts, 1)
            pool.memset(vec_rows[:], 0.0).then_inc(vec_zero, 1)
            done(pool.memset(upper[:], 1.0))
            done(pool.memset(a_mask[:], 0.0))
            pool.memset(ones[:], 1.0).then_inc(consts, 1)
            done.wait()
            pool.affine_select(out=upper[:], in_=upper[:], compare_op=ALU.is_ge, fill=0.0, base=0,
                               pattern=[[1, P]], channel_multiplier=-1).then_inc(consts, 1)
            done(pool.affine_select(out=a_mask[:, 0:S], in_=a_mask[:, 0:S], compare_op=ALU.is_ge, fill=MASKED, base=-1,
                                    pattern=[[1, S]], channel_multiplier=-1))
            done.wait()
            pool.affine_select(out=a_mask[:, 0:S], in_=a_mask[:, 0:S], compare_op=ALU.is_ge, fill=MASKED, base=P,
                               pattern=[[-1, S]], channel_multiplier=1).then_inc(consts, 1)
            pool.affine_select(out=a_mask[:, S:3 * P], in_=a_mask[:, S:3 * P], compare_op=ALU.is_ge, fill=MASKED, base=0,
                               pattern=[[-1, P]], channel_multiplier=1).then_inc(consts, 1)
            pool.iota(window_inv, [[1, 16]], base=1, channel_multiplier=0,
                      allow_small_or_imprecise_dtypes=True).then_inc(consts, 1)
            for n in range(HALF_ROPE):
                pool.memset(freq[:, n:n + 1], float(np.float32(ROPE_THETA) ** np.float32(-n / HALF_ROPE))).then_inc(consts, 1)
            pool.wait_ge(mod_mm, MOD_FIRST)
            pool.memset(gates_w[:], 0.0).then_inc(gates_zero, 1)

        CONSTS = 6 + HALF_ROPE

        @block.sync
        def _(sp):
            ada = d["w_ada"][0].rearrange("(k p) n -> p k n", p=P)

            def load_mod(a, k, first=False):
                if not first:
                    sp.wait_ge(mod_step, a * KC + (k + 1 - MOD_SLOTS))
                sp.dma_start(mod_raw[:, k % MOD_SLOTS, :], ada[:, k, bass.ds(a * MOD_COLS, MOD_COLS)]).then_inc(mod_landed[k % MOD_SLOTS], 16)

            small_loads = [(vec_rows[r0:r0 + src.shape[0], n, :], src, vec_landed) for n, r0, src in vec_loads] \
                + [(dst, src.to_broadcast([P, src.shape[1]]), rows_landed) for dst, src in row_loads]

            def load_tile(ph, b, j, sources):
                if not isinstance(b, int) or ph.tile(b) + j >= RAW_SLOTS:
                    sp.wait_ge(lo_ready, 2 * ph.tile(b) + (2 * j - 2 * RAW_SLOTS + 2))
                k0, n = ph.row0[j], ph.rows[j]
                for c0, src in sources(k0, k0 + n):
                    sp.dma_start(raw[:, j % RAW_SLOTS, 0:n, c0:c0 + src.shape[2]], src).then_inc(landed[j % RAW_SLOTS], 16)

            def load(ph, b, sources):
                for j in range(ph.tiles):
                    load_tile(ph, b, j, sources)

            def load_beside(ph, b, sources):
                for j in range(ph.tiles):
                    load_tile(ph, b, j, sources)
                    mods_beside(ph, b, j)

            def mods_beside(ph, b, j):
                for place in (2 * (ph.tile(b) + j - 2) - LEAD, 2 * (ph.tile(b) + j - 2) - LEAD + 1):
                    load_mods(place)

            def load_mods(place):
                if 0 <= place < len(mod_places):
                    for n in mod_at(place):
                        load_mod(n // KC, n % KC)

            def plain(w, cols):
                w = w.rearrange("(k p) n -> p k n", p=P)
                return lambda k0, k1: [(0, w[:, k0:k1, cols])]

            def twin(w, col, v, col2):
                w, v = (a.rearrange("(k p) n -> p k n", p=P) for a in (w, v))
                return lambda k0, k1: [(0, w[:, k0:k1, bass.ds(col, COLS // 2)]), (COLS // 2, v[:, k0:k1, bass.ds(col2, COLS // 2)])]

            def load_all(ph, w):
                with sp.Fori(0, ph.blocks) as b:
                    load(ph, b, plain(w, bass.ds(b * COLS, COLS)))

            sp.dma_start(c_rows[0:KC, :], by_chunk(d["c"][0])).then_inc(c_landed, 16)
            sp.dma_start(pos_i[:], d["positions_2"][0].rearrange("(t p) -> p t", p=P),
                         allow_slow_non_contiguous=True).then_inc(rows_landed, 16)
            for a in range(MOD_FIRST):
                for k in range(KC):
                    load_mod(a, k, first=(a == 0 and k < MOD_SLOTS))
                    if (a, k) == (0, MOD_SLOTS - 1):
                        sp.wait_ge(vec_zero, 1)
                    if a == 0 and k >= MOD_SLOTS - 1:
                        for dst, src, signal in small_loads[3 * (k - MOD_SLOTS + 1):3 * (k - MOD_SLOTS + 2)]:
                            sp.dma_start(dst, src).then_inc(signal, 16)
                    if (a, k) in ((0, KC // 2 + 1), (0, KC // 2 + 2)):
                        t = k - KC // 2 - 1
                        sp.dma_start(x[:, t, :], d["x"][0, t * P:(t + 1) * P, :]).then_inc(x_landed, 16)
                    if k == KC // 2:
                        load_tile(w_in, 0, a, plain(d["w_in"][0], bass.ds(w_in_cols[0], COLS)))
            for j in range(w_in.tiles):
                mods_beside(w_in, 0, j)
            sp.wait_ge(gates_zero, 1)
            for n, w in enumerate((d["w_rg_a"][0], d["w_rg_i"][0])):
                for e in range(2):
                    sp.dma_start(gates_w[64 * e:64 * e + 64, n, :, 64 * e:64 * e + 64],
                                 w.rearrange("(m e) i j -> e i m j", e=2)[e]).then_inc(mixw_landed, 16)
            sp.dma_start(pool_w[:], d["w_pool"][0].rearrange("g (k p) n -> p (g k) n", p=P)).then_inc(mixw_landed, 16)
            for b in range(1, w_in.blocks):
                load_beside(w_in, b, plain(d["w_in"][0], bass.ds(w_in_cols[b], COLS)))
            for b in range(w_out.blocks):
                load_beside(w_out, b, plain(d["w_out"][0], bass.ds(b * COLS, COLS)))

            def load_up1(b, how):
                how(up1, b, twin(d["w_ffn_gate"][0], b * (COLS // 2), d["w_ffn_up"][0], b * (COLS // 2)))

            UP1_BESIDE = 10
            for b in range(UP1_BESIDE):
                load_up1(b, load_beside)
            with sp.Fori(UP1_BESIDE, up1.blocks) as b:
                load_up1(b, load)
            load_all(down1, d["w_ffn_down"][0])
            load(w_in2, 0, plain(d["w_in_2"][0], bass.ds(w_in2_cols[0], COLS)))
            sp.wait_ge(w_used, down1.end(down1.blocks - 1))
            sp.dma_start(w_dt[:], d["w_in_2"][0].rearrange("(k p) n -> p k n", p=P)[:, :, O_DT:O_DT + SH]).then_inc(dt_landed, 16)
            for b in range(1, w_in2.blocks):
                load(w_in2, b, plain(d["w_in_2"][0], bass.ds(w_in2_cols[b], COLS)))
            for b in range(w_out2.blocks):
                load(w_out2, b, plain(d["w_out_2"][0], bass.ds(b * COLS, COLS)))
            with sp.Fori(0, up2.blocks) as b:
                load(up2, b, twin(d["w_up_2"][0], b * (COLS // 2), d["w_up_2"][0], b * (COLS // 2) + HC * P))
            load_all(down2, d["w_down_2"][0])
            load(ple_gate, 0, plain(d["w_ple_gate_2"][0], bass.ds(0, COLS)))
            sp.wait_ge(w_used, down2.end(down2.blocks - 1))
            sp.dma_start(p_t[:], d["p_2"][0, 0].rearrange("(t p) n -> p t n", p=P)).then_inc(ple_landed, 16)
            sp.dma_start(w_ple[:], d["w_ple_proj_2"][0].rearrange("(k p) n -> p k n", p=P)).then_inc(ple_landed, 16)
            for b in range(1, ple_gate.blocks):
                load(ple_gate, b, plain(d["w_ple_gate_2"][0], bass.ds(b * COLS, COLS)))
            result = out[0].rearrange("(t p) n -> p t n", p=P)
            for b in range(ple_gate.blocks):
                sp.wait_ge(x_out, b + 1)
                sp.dma_start(result[:, :, b * COLS:(b + 1) * COLS], x[:, :, b * COLS:(b + 1) * COLS]).then_inc(stored, 16)
            sp.wait_ge(stored, 16 * ple_gate.blocks)

        @block.scalar
        def _(act):
            done = Steps(act, act_step)
            run = nc.scalar.activation

            def split_hi(ph, b, halves):
                for h in halves:
                    at0, _, n = ph.half_rows(h)
                    if h % 2 == 0:
                        act.wait_ge(landed[h // 2 % RAW_SLOTS], ph.landed(b, h // 2))
                    if not isinstance(b, int) or ph.half(b) + h >= HALF_SLOTS:
                        act.wait_ge(w_used, ph.half(b) + (h - HALF_SLOTS + 1))
                    run(w_hi[:, h % HALF_SLOTS, 0:n, :], raw[:, h // 2 % RAW_SLOTS, at0:at0 + n, :],
                        ACT.Copy).then_inc(hi_ready, 1)

            def stream(ph, finish, nxt, peel=0, beside=None):
                def one(b, c, more):
                    split_hi(ph, b, range(ph.lead, ph.halves))
                    if more:
                        split_hi(ph, b + 1, range(ph.lead))
                    elif nxt:
                        split_hi(nxt, 0, range(nxt.lead))
                    act.wait_ge(w_used, ph.end(b))
                    finish(b, c)

                if ph.blocks == XB:
                    for b in range(ph.blocks):
                        more = b + 1 < ph.blocks
                        for n in range(ph.halves):
                            h = ph.lead + n
                            if h < ph.halves:
                                split_hi(ph, b, [h])
                            elif more:
                                split_hi(ph, b + 1, [h - ph.halves])
                            if beside and b == 0:
                                beside(n)
                        if not more:
                            split_hi(nxt, 0, range(LEAD))
                        act.wait_ge(w_used, ph.end(b))
                        finish(b, b % 2)
                    split_hi(nxt, 0, range(LEAD, nxt.lead))
                    return
                for b in range(2 * peel):
                    one(b, b % 2, True)
                with act.Fori(peel, ph.blocks // 2 - 1) as i:
                    one(i * 2, 0, True)
                    one(i * 2 + 1, 1, True)
                one(ph.blocks - 2, 0, True)
                one(ph.blocks - 1, 1, False)

            def root(k):
                act.wait_ge(n_var, k)
                run(std, var, ACT.Sqrt).then_inc(n_std, 1)

            def norm_sums(n, b):
                act.wait_ge(x_new, X_BEFORE[n] + b + 1)
                if b:
                    act.wait_ge(n_ssq, SSQ_DONE[n] - T * (XB - b))
                for t in range(T):
                    run(norm_squares[n][:, t, :], x[:, t, b * COLS:(b + 1) * COLS], ACT.Square,
                        accum_out=ssq_parts[:, t * XB + b:t * XB + b + 1]).then_inc(n_ssq, 1)

            def norm_turned(n, b, gain=None):
                act.wait_ge(n_turned, XB * n + b + 1)
                of, dst = flat(misc[:, 0:2, :]), norm_features[n]
                if n == 2:
                    if b:
                        act.wait_ge(n_sums, b)
                    run(flat(norm_squares[n][:]), of, ACT.Square).then_inc(n_sq, 1)
                if gain is None:
                    run(flat(dst[:, 4 * b:4 * b + 4, :]), of, ACT.Copy).then_inc(n_f, 1)
                else:
                    for m in range(4 * b, 4 * b + 4):
                        ins = run(dst[:, m, :], misc[:, m % 4 // 2, (m % 2) * S:(m % 2 + 1) * S], ACT.Copy, scale=gain[:, m:m + 1])
                    ins.then_inc(n_f, 1)

            def norm_high(n, q, shift=None):
                act.wait_ge(n_scaled, XG * n + q + 1)
                two = slice(2 * q, 2 * q + 2)
                if shift is None:
                    run(flat(a_hi[:, two, :]), flat(norm_features[n][:, two, :]), ACT.Copy).then_inc(n_hi, 1)
                else:
                    for m in (2 * q, 2 * q + 1):
                        ins = run(a_hi[:, m, :], norm_features[n][:, m, :], ACT.Identity, bias=shift[:, m:m + 1])
                    ins.then_inc(n_hi, 1)

            def norm_beside(n, gain=None):
                def finish(b, c):
                    if b:
                        if n != 2:
                            norm_sums(n, b - 1)
                        norm_turned(n, b - 1, gain)
                return finish

            def norm_end(n, gain=None, shift=None):
                if n == 2:
                    norm_turned(n, XB - 1, gain)
                    for k in ROOTS[n]:
                        root(k)
                else:
                    norm_sums(n, XB - 1)
                    root(ROOTS[n])
                    norm_turned(n, XB - 1, gain)
                for q in range(XG):
                    norm_high(n, q, shift)

            def conv_bias(c, m0, tap, bias, dst, signal):
                for m in range(4):
                    run(dst[:, m0 + m, :], pair[:, c, m // 2, (m % 2) * S:(m % 2 + 1) * S], ACT.Identity,
                        scale=tap[:, m0 + m:m0 + m + 1], bias=bias[:, m0 + m:m0 + m + 1]).then_inc(signal, 1)

            act.wait_ge(c_turned, 1)
            run(c_silu, misc[:, 2, 0:KC], ACT.Silu).then_inc(c_ready, 1)
            act.wait_ge(vec_turned, 1)
            run(flat(vec[:, 0:4, :]), misc[:, 0, :], ACT.Copy).then_inc(vec_ready, 1)
            run(flat(vec[:, 4:7, :]), misc[:, 1, 0:3 * P], ACT.Copy).then_inc(vec_ready, 1)
            act.wait_ge(prep_in, 1)
            run(l_exp, l_abs, ACT.Exp, scale=-1.0).then_inc(prep_exp, 1)
            act.wait_ge(rows_landed, 16 * (len(row_loads) + 1))
            run(a_neg, a_log, ACT.Exp).then_inc(prep_exp, 1)
            act.wait_ge(prep_in, 2)
            run(half_sin, ang_r, ACT.Sin, scale=0.5).then_inc(prep_exp, 1)
            run(sin_t, ang_r, ACT.Sin).then_inc(prep_exp, 1)

            act.wait_ge(x_landed, 16 * T)
            for t in range(T):
                run(xn_sq[:, t, :], x[:, t, :], ACT.Square, accum_out=ssq[:, t:t + 1]).then_inc(n_ssq, 1)
            root(ROOTS[0])
            act.wait_ge(n_rstd, 1)
            for t in range(T):
                run(xn[:, t, :], x[:, t, :], ACT.Copy, scale=rstd[:, t:t + 1]).then_inc(n_xn, 1)
            for b in range(XB):
                norm_turned(0, b)
            for q in range(XG):
                norm_high(0, q)
                if q < LEAD:
                    split_hi(w_in, 0, [q])

            def mixer(b):
                for n in range(w_in.halves):
                    h = LEAD + n
                    ph, b1 = (w_in, b) if h < w_in.halves else (w_in, b + 1) if b + 1 < w_in.blocks else (w_out, 0)
                    split_hi(ph, b1, [h % w_in.halves])
                    beside(b, n)
                act.wait_ge(w_used, w_in.end(b))

            def beside(b, n):
                if (b, n) == (3, 1):
                    act.wait_ge(gate_ev, 2 * RC)
                    act.wait_ge(prep_in, 4)
                    for m in range(RC):
                        run(lru_m[:, m, :], lru_a[:, m, :], ACT.Tanh, scale=nls8[:, m:m + 1]).then_inc(lru_t, 1)
                elif (b, n) == (3, 3):
                    act.wait_ge(lru_t, RC)
                    for m in range(RC):
                        run(lru_a[:, m, :], lru_a[:, m, :], ACT.Exp, scale=ls8[:, m:m + 1]).then_inc(lru_e, 1)
                elif (b, n) == (3, 4):
                    act.wait_ge(lru_e, RC)
                    run(flat(lru_sq[:]), flat(lru_a[:]), ACT.Square).then_inc(lru_s, 1)
                elif (b, n) == (4, 0):
                    act.wait_ge(lru_q, 1)
                    run(flat(lru_m[:]), flat(lru_m[:]), ACT.Sqrt).then_inc(lru_r, 1)
                elif (b, n) == (5, 4):
                    pooled_out(range(6))
                elif (b, n) == (5, 5):
                    lru_out(0)
                elif (b, n) == (5, 7):
                    pooled_out(range(6, 2 * G))

            def pooled_out(chunks):
                for m in chunks:
                    act.wait_ge(pool_mm, m // 2 * 2 + 2)
                    run(pool_hi[:, m, :], misc[:, m // 2 % 3, (m % 2) * S:(m % 2 + 1) * S], ACT.Copy,
                        scale=ls_pool[:, m:m + 1]).then_inc(pool_hi_ev, 1)

            def lru_out(e):
                act.wait_ge(lru_y, e + 1)
                run(flat(lru_hi[:, 4 * e:4 * e + 4, :]), flat(y_lru[:, 4 * e:4 * e + 4, :]), ACT.Copy).then_inc(lru_hi_ev, 1)

            for b in range(2):
                mixer(b)
                conv_bias(b % 2, 4 * b, cw1[:, (CONV - 1) * RC:], cb1, xc, c1_bias)
            mixer(2)
            run(flat(xp[:, 0:4, :]), flat(pair[:, 0]), ACT.Copy).then_inc(xp_ev, 1)
            for m in range(RC):
                act.wait_ge(gate_mm, m + 1)
                run(lru_a[:, m, :], misc[:, m % 3, 0:S], ACT.Sigmoid, bias=b_ra[:, m:m + 1]).then_inc(gate_ev, 1)
                run(lru_u[:, m, :], misc[:, m % 3, S:2 * S], ACT.Sigmoid, bias=b_ri[:, m:m + 1]).then_inc(gate_ev, 1)
            mixer(3)
            run(flat(xp[:, 4:8, :]), flat(pair[:, 1]), ACT.Copy).then_inc(xp_ev, 1)
            mixer(4)
            run(flat(y_lru[:, 0:4, :]), flat(pair[:, 0]), ACT.Gelu_apprx_tanh).then_inc(ge_ev, 1)
            mixer(5)
            run(flat(y_lru[:, 4:8, :]), flat(pair[:, 1]), ACT.Gelu_apprx_tanh).then_inc(ge_ev, 1)
            lru_out(1)
            act.wait_ge(row_mm, 1)
            run(row[:], flat(misc[:]), ACT.Copy).then_inc(row_ready, 1)

            stream(w_out, norm_beside(1), up1)
            norm_end(1, shift=mod[:, 3 * KC:4 * KC])

            def finish_up1(b, c):
                if not isinstance(b, int) or b:
                    act.wait_ge(ff_prod, b)
                run(flat(ff_g[:]), pair[:, c, 0, :], ACT.Silu).then_inc(ff_sig, 1)

            stream(up1, finish_up1, down1, peel=1)
            act.wait_ge(row_mm, 2)
            run(row[:], flat(misc[:]), ACT.Copy).then_inc(row_ready, 1)
            act.wait_ge(n_gain, 1)
            stream(down1, norm_beside(2, g_both), w_in2)

            norm_end(2, g_both)

            def mixer2(b, beside=None):
                for n in range(w_in2.halves):
                    h = LEAD + n
                    ph, b1 = (w_in2, b) if h < w_in2.halves else (w_in2, b + 1) if b + 1 < w_in2.blocks else (w_out2, 0)
                    split_hi(ph, b1, [h % w_in2.halves])
                    if beside:
                        beside((b - B_XBC) * w_in2.halves + n)
                act.wait_ge(w_used, w_in2.end(b))

            for b in range(B_K):
                mixer2(b)
                run(q_t[:, :, 8 * b:8 * b + 8, :].rearrange("p t h e -> p t (h e)"), pair[:, b % 2], ACT.Copy).then_inc(qkv_ev, 1)
                if b == 0:
                    act.wait_ge(dt_landed, 16)
                    run(flat(w_dt_hi[:]), flat(w_dt[:]), ACT.Copy).then_inc(dt_hi, 1)
                if b == 3:
                    act.wait_ge(dt_x, 1)
                    run(d_exp, d_abs, ACT.Exp, scale=-1.0).then_inc(dt_exp, 1)

            def turned(f):
                act.wait_ge(qk_turned, f + 1)
                dst = q_tr[:, 2 * f:2 * f + 2, :] if f < KC // 2 else k_tr[:, 2 * f - KC:2 * f - KC + 2, :]
                run(flat(dst), misc[:, f % 4, :], ACT.Copy).then_inc(qk_ev, 1)

            def exponentials(i):
                act.wait_ge(sc_max, i + 1)
                two = slice(2 * i, 2 * i + 2)
                run(by_block(e_sink)[:, :, two], by_block(m_sink)[:, :, two], ACT.Exp).then_inc(sink_exp, 1)
                for e in range(2):
                    for blk, keys in ((1, slice(0, S)), (0, slice(S, 3 * P))):
                        n = blk * HEADS + 2 * i + e
                        run(scores[:, i % 4, e, keys], scores[:, i % 4, e, keys], ACT.Exp, bias=m_neg[:, n:n + 1],
                            accum_out=e_sum[:, n:n + 1]).then_inc(sc_exp, 1)

            def attention(place):
                if place == K_PLACE:
                    act.wait_ge(hn_v, 1)
                    run(q_part(hn_std), q_part(hn_var), ACT.Sqrt).then_inc(hn_s, 1)
                elif place == V_PLACE:
                    act.wait_ge(hn_v, 2)
                    run(k_part(hn_std), k_part(hn_var), ACT.Sqrt).then_inc(hn_s, 1)
                elif Q_TURN < place <= Q_TURN + KC // 4:
                    for e in range(2):
                        turned(2 * (place - Q_TURN - 1) + e)
                elif K_TURN < place <= K_TURN + KV // 4:
                    for e in range(2):
                        turned(KC // 2 + 2 * (place - K_TURN - 1) + e)
                elif place >= PAIR_START:
                    i, late = divmod(place - PAIR_START, PAIR_STEP)
                    if not late and 0 <= i - EXP_LAG < PAIRS:
                        exponentials(i - EXP_LAG)
                    if late and 0 <= i - TURN_LAG < PAIRS:
                        j = i - TURN_LAG
                        act.wait_ge(p_turned, j + 1)
                        if j >= 2:
                            act.wait_ge(pv_mm, j - 1)
                        run(p_tr[:, j % 2], misc[:, 2:4, 0:3 * P], ACT.Copy).then_inc(p_ev, 1)

            for b, kv in ((B_K, k_t), (B_V, v_t)):
                mixer2(b, attention)
                run(kv.rearrange("p t h e -> p t (h e)"), pair[:, b % 2], ACT.Copy).then_inc(qkv_ev, 1)

            for b in range(B_XBC, B_Z):
                j = b - B_XBC
                mixer2(b, attention)
                conv_bias(b % 2, 4 * j, cw2[:, (CONV - 1) * XBC:], cb2, xbc, c2_bias)
                if j:
                    act.wait_ge(c2_tap, 12 * j)
                    run(flat(xbc[:, 4 * j - 4:4 * j, :]), flat(xbc[:, 4 * j - 4:4 * j, :]), ACT.Silu).then_inc(xbc_ev, 1)
            def states(place):
                place -= Z0
                if 1 <= place <= 4:
                    for i in (2 * place - 2, 2 * place - 1):
                        act.wait_ge(xs_turned, i + 1)
                        t, f = i // 4, i % 4
                        run(xs_t[:, t, 8 * f:8 * f + 8, :].rearrange("p h e -> p (h e)"), misc[:, i % 4, :], ACT.Copy).then_inc(xs_ev, 1)
                elif place == B_TURN + 1:
                    act.wait_ge(b_turned, 1)
                    run(flat(b_tok[:]), misc[:, 0, :], ACT.Copy).then_inc(b_ev, 1)
                    act.wait_ge(cs_mm, 1)
                    run(a_cs, misc[:, 1, 0:T * SH], ACT.Copy).then_inc(cs_ev, 1)
                    run(a_last, misc[:, 1, T * SH:T * SH + SH], ACT.Copy).then_inc(cs_ev, 1)
                    act.wait_ge(cs_ev, 2)
                    run(from_start, a_cs[:, SH:2 * SH], ACT.Exp).then_inc(end_ev, 1)
                elif place == B_TURN + 2:
                    act.wait_ge(c2_tap, 72)
                    run(flat(xbc[:, 20:24, :]), flat(xbc[:, 20:24, :]), ACT.Silu).then_inc(xbc_ev, 1)
                elif place == B_TURN + 3:
                    act.wait_ge(end_in, 1)
                    run(to_last, to_last, ACT.Exp).then_inc(end_ev, 1)
                elif place == STATE + 1:
                    act.wait_ge(st_mm, 1)
                    run(state.rearrange("p h e -> p (h e)"), flat(misc[:]), ACT.Copy).then_inc(st_ev, 1)
                for c in range(T):
                    g = place - DECAYS[c] - 2
                    if 0 <= g < SG:
                        act.wait_ge(seg_min, SG * c + g + 1)
                        run(flat(decay[:, 8 * g:8 * g + 8, :]), flat(decay[:, 8 * g:8 * g + 8, :]), ACT.Exp).then_inc(seg_exp, 1)

            for b in range(B_Z, w_in2.blocks):
                j = b - B_Z
                mixer2(b, states)
                run(z_t[:, :, COLS * j:COLS * (j + 1)], pair[:, b % 2], ACT.Silu).then_inc(z_ev, 1)

            for f in range(KC // 2):
                act.wait_ge(yo_turned, f + 1)
                run(flat(a_hi[:, 2 * f:2 * f + 2, :]), misc[:, f % 4, :], ACT.Copy).then_inc(ya_hi, 1)

            def state_output(place):
                if place == 0:
                    act.wait_ge(gated, 4)
                    for n in range(T * SG):
                        t, g = n // SG, n % SG
                        if n >= 4:
                            act.wait_ge(g_sums, n - 3)
                        run(g_sq[:, n % 4, :], flat(y_t[:, t])[:, g * COLS:(g + 1) * COLS], ACT.Square,
                            accum_out=g_ssq[:, n:n + 1]).then_inc(g_sums, 1)
                elif place == 1:
                    act.wait_ge(g_v, 1)
                    run(g_std, g_var, ACT.Sqrt).then_inc(g_s, 1)
                elif Y_TURN < place <= Y_TURN + 4:
                    for f in (2 * (place - Y_TURN) - 2, 2 * (place - Y_TURN) - 1):
                        act.wait_ge(ys_turned, f + 1)
                        for m in (2 * f, 2 * f + 1):
                            run(s_hi[:, m, :], misc[:, f % 4, m % 2 * S:(m % 2 + 1) * S], ACT.Copy, scale=g_ssm[:, m:m + 1]).then_inc(ys_hi, 1)

            stream(w_out2, norm_beside(3, g_ffn2), up2, beside=state_output)
            norm_end(3, g_ffn2)

            def finish_up2(b, c):
                act.wait_ge(h_lo, b + up1.blocks)
                for m in range(4):
                    dst, m0 = ((ff_g, 0), (ff_u, HC))[m // 2]
                    ch = bass.ds(b * 2 + (m0 + m % 2), 1)
                    run(dst[:, m % 2, :], pair[:, c, m // 2, (m % 2) * S:(m % 2 + 1) * S], ACT.Identity,
                        scale=vec[:, 4 + FFN_CONV - 1, ch], bias=cb3[:, ch]).then_inc(c3_bias, 1)
                act.wait_ge(c3_tap, b * 8 + 8)
                run(flat(ff_g[:]), flat(ff_g[:]), ACT.Silu).then_inc(ff_sig, 1)

            stream(up2, finish_up2, down2)
            stream(down2, norm_beside(4, g_ple), ple_gate)
            norm_end(4, g_ple)

            def embedding(place):
                if place == 2:
                    act.wait_ge(pt_turned, 1)
                    run(flat(p_f[:]), misc[:, 0, :], ACT.Copy).then_inc(pt_ev, 1)
                elif place in (4, 6):
                    t = place // 2 - 2
                    act.wait_ge(pe_mm, t + 1)
                    run(pe_t[:, t, :], flat(misc[:]), ACT.Copy).then_inc(pe_ev, 1)
                    act.wait_ge(pe_ev, t + 1)
                    if t:
                        act.wait_ge(pe_ssq, t)
                    run(pe_sq[:], pe_t[:, t, :], ACT.Square, accum_out=ssq[:, t:t + 1]).then_inc(pe_ssq, 1)
                elif place == 7:
                    act.wait_ge(pe_v, 1)
                    run(std, var, ACT.Sqrt).then_inc(pe_s, 1)

            for b in range(ple_gate.blocks):
                for n in range(ple_gate.halves):
                    h, more = (LEAD + n) % ple_gate.halves, LEAD + n >= ple_gate.halves
                    if b + more < ple_gate.blocks:
                        split_hi(ple_gate, b + more, [h])
                    if b == 0:
                        embedding(n)
                act.wait_ge(w_used, ple_gate.end(b))
                if b:
                    act.wait_ge(x_out, b)
                run(flat(sig[:]), flat(pair[:, b % 2]), ACT.Sigmoid).then_inc(gate_sig, 1)

        @block.tensor
        def _(pe):
            def features(ph, b, c, hi, lo, beside=None, before=None):
                for h in range(ph.halves):
                    pe.wait_ge(lo_ready, ph.half(b) + (h + 1))
                    if before:
                        before(h)
                    slot = h % HALF_SLOTS
                    _, k0, n = ph.half_rows(h)
                    for kk in range(n):
                        k = k0 + kk
                        for m in range(4):
                            o = pair[:, c, m // 2, (m % 2) * S:(m % 2 + 1) * S]
                            wh, wl = (w[:, slot, kk, m * P:(m + 1) * P] for w in (w_hi, w_lo))
                            pe.matmul(o, wh, hi[:, k, :], start=(h == kk == 0 and m % 2 == 0), stop=False, skip_group_check=True)
                            pe.matmul(o, wh, lo[:, k, :], start=False, stop=False, skip_group_check=True)
                            mm = pe.matmul(o, wl, hi[:, k, :], start=False, stop=(h == ph.halves - 1 and kk == n - 1), skip_group_check=True)
                    mm.then_inc(w_used, 1)
                    if beside:
                        beside(h)

            def tokens(ph, b, c, operand, beside=None, before=None):
                for h in range(ph.halves):
                    pe.wait_ge(lo_ready, ph.half(b) + (h + 1))
                    if before:
                        before(h)
                    slot = h % HALF_SLOTS
                    _, k0, n = ph.half_rows(h)
                    for kk in range(n):
                        k = k0 + kk
                        hi, lo = operand(k)
                        for t in range(T):
                            o, own = pair[:, c, t, :], slice(t * P, (t + 1) * P)
                            pe.matmul(o, hi[:, own], w_hi[:, slot, kk, :], start=(h == kk == 0), stop=False)
                            pe.matmul(o, hi[:, own], w_lo[:, slot, kk, :], start=False, stop=False)
                            mm = pe.matmul(o, lo[:, own], w_hi[:, slot, kk, :], start=False, stop=(h == ph.halves - 1 and kk == n - 1))
                    mm.then_inc(w_used, 1)
                    if beside:
                        beside(h)

            def normed(k):
                return a_hi[:, k, :], a_lo[:, k, :]

            def hidden(k):
                return hid_hi[:, k, :], hid_lo[:, k, :]

            def turn_block(n, b):
                if n == 0:
                    pe.wait_ge(n_xn, T)
                else:
                    pe.wait_ge(x_new, X_BEFORE[n] + b + 1)
                if b:
                    pe.wait_ge(n_f, XB * n + b)
                src = xn if n == 0 else x
                for m in range(4 * b, 4 * b + 4):
                    for t in range(T):
                        mm = pe.transpose(misc[:, m % 4 // 2, m % 2 * S + t * P:m % 2 * S + (t + 1) * P], src[:, t, m * P:(m + 1) * P], ident[:])
                mm.then_inc(n_turned, 1)

            def weigh_squares(b):
                pe.wait_ge(n_sq, b + 1)
                for m in range(4 * b, 4 * b + 4):
                    for t in range(T):
                        at0 = m % 4 * S + t * P
                        mm = pe.matmul(misc[:, 3, 2 * t:2 * t + 2], flat(squares_a[:])[:, at0:at0 + P], g_weigh[:, m, :],
                                       start=(m == t == 0), stop=(m == KC - 1), skip_group_check=True)
                mm.then_inc(n_sums, 1)

            def spread(n):
                pe.wait_ge(n_diag, T * n)
                for t in range(T):
                    mm = pe.matmul(misc[:, 2, t * P:(t + 1) * P], ones[:], norm_diag[n][:, t, :], start=True, stop=True, skip_group_check=True)
                mm.then_inc(n_row, 1)

            def norm_beside(n, b, other=None):
                def beside(h):
                    if other:
                        other(h)
                    if h == 2 and b:
                        if n == 2 and b == 1:
                            pe.wait_ge(row_ready, 2)
                            pe.wait_ge(n_gain, 1)
                        turn_block(n, b - 1)
                        if n == 2 and b > 1:
                            weigh_squares(b - 2)
                return beside

            def norm_end(n):
                if n == 2:
                    weigh_squares(XB - 2)
                turn_block(n, XB - 1)
                if n == 2:
                    weigh_squares(XB - 1)
                spread(n)

            def normed_yet(n):
                def before(h):
                    pe.wait_ge(n_lo, XG * n + h + 1)
                return before

            def rows_of(col, signal):
                for m in range(KC):
                    mm = pe.matmul(misc[:, m // 4, (m % 4) * P:(m % 4 + 1) * P], col[:, m:m + 1].to_broadcast([P, P]), ident[:],
                                   start=True, stop=True, skip_group_check=True)
                mm.then_inc(signal, 1)

            pe.wait_ge(consts, 1)
            pe.wait_ge(c_landed, 16)
            pe.transpose(misc[:, 2, 0:KC], c_rows[0:KC, :], ident[0:KC, 0:KC]).then_inc(c_turned, 1)
            pe.wait_ge(consts, CONSTS)
            pe.wait_ge(vec_landed, 16 * len(vec_loads))
            for n in range(7):
                mm = pe.transpose(misc[:, n // 4, (n % 4) * P:(n % 4 + 1) * P], vec_rows[:, n, :], ident[:])
            mm.then_inc(vec_turned, 1)

            def mod_sums(a, c, read=None):
                pe.wait_ge(mod_step, a * KC + KC)
                if read:
                    pe.wait_ge(mod_ready, read)
                for m in range(MOD_M):
                    mm = pe.matmul(misc[:, 3, bass.ds(a * MOD_M + m, 1)], mod_acc[:, c, m * P:(m + 1) * P], ones[:, 0:1],
                                   start=True, stop=True, skip_group_check=True)
                mm.then_inc(mod_mm, 1)

            for a in range(MOD_FIRST):
                mod_sums(a, a % 2, read=a)
                if a == 0:
                    for b in range(XB):
                        turn_block(0, b)

            pe.wait_ge(mod_ready, MOD_FIRST)

            def pools(h):
                if h == 3:
                    pe.wait_ge(pooled, 4)
                    pe.wait_ge(gate_ev, 2 * RC)
                if h == 6:
                    pe.wait_ge(pool_lo_ev, 2)
                for m in range(6) if h == 3 else range(6, 2 * G) if h == 6 else ():
                    g, e = m // 2, m % 2
                    for kk in range(2):
                        mm = pe.matmul(misc[:, g % 3, e * S:(e + 1) * S], pool_w[:, 2 * g + kk, e * P:(e + 1) * P], xp[:, 2 * g + kk, :],
                                       start=(kk == 0), stop=(kk == 1), skip_group_check=True)
                    mm.then_inc(pool_mm, 1)

            for b in range(w_in.blocks):
                if 2 <= b < 4:
                    pe.wait_ge(c1_tap, 12 * (b - 1))
                elif b >= 4:
                    pe.wait_ge(xp_ev, b - 3)
                features(w_in, b, b % 2, a_hi, a_lo, pools if b == 5 else None, normed_yet(0) if b == 0 else None)
                if b in (2, 4):
                    mod_sums(4 + (b - 2) // 2, b // 2 - 1, read=4 + (b - 2) // 2)
                if b == 2:
                    pe.wait_ge(c1_tap, 24)
                    pe.wait_ge(mixw_landed, 5 * 16)
                    for m in range(RC):
                        if m >= 3:
                            pe.wait_ge(gate_ev, 2 * (m - 3) + 2)
                        for n in range(2):
                            mm = pe.matmul(misc[:, m % 3, n * S:(n + 1) * S], gates_w[:, n, m, :], xc[:, m, :],
                                           start=True, stop=True, skip_group_check=True)
                        mm.then_inc(gate_mm, 1)
            pe.wait_ge(pool_lo_ev, 2 * G)
            pe.wait_ge(mod_ready, 6)
            rows_of(mod[:, 2 * KC:3 * KC], row_mm)

            def mixed_first(k):
                return (lru_hi[:, k, :], lru_lo[:, k, :]) if k < RC else (pool_hi[:, k - RC, :], pool_lo[:, k - RC, :])

            def lru_ready(h):
                if h == 3:
                    pe.wait_ge(lru_lo_ev, 2)

            for b in range(w_out.blocks):
                if b < 2:
                    pe.wait_ge(ge_ev, b + 1)
                else:
                    pe.wait_ge(x_new, b - 1)
                tokens(w_out, b, b % 2, mixed_first, norm_beside(1, b, lru_ready))
                if b == 0:
                    pe.wait_ge(row_ready, 1)
                if b < 2:
                    mod_sums(6 + b, b, read=6 + b)
            mod_sums(8, 0, read=8)
            mod_sums(9, 1)

            norm_end(1)
            for b in range(2):
                features(up1, b, b, a_hi, a_lo, None, normed_yet(1) if b == 0 else None)

            def up1_pair(i, beside=None):
                for c in range(2):
                    pe.wait_ge(ff_prod, i * 2 + (c - 1))
                    features(up1, i * 2 + c, c, a_hi, a_lo, beside if c == 0 else None)

            for i in range(1, 5):
                up1_pair(i, lambda h: mod_sums(9 + i // 2, 1 - i // 2 % 2) if h == 3 and i % 2 == 0 else None)
            with pe.Fori(5, up1.blocks // 2) as i:
                up1_pair(i)
            pe.wait_ge(mod_ready, 10)
            rows_of(mod[:, 5 * KC:6 * KC], row_mm)

            def last_hidden(ph, count):
                def wait(h):
                    if h == ph.halves - 3:
                        pe.wait_ge(h_lo, count)
                return wait

            pe.wait_ge(h_lo, up1.blocks - 1)
            for b in range(down1.blocks):
                if b >= 2:
                    pe.wait_ge(x_new, X_BEFORE[2] + b - 1)
                tokens(down1, b, b % 2, hidden, norm_beside(2, b, last_hidden(down1, up1.blocks)))

            norm_end(2)
            def turn_qk(f):
                if f >= 4:
                    pe.wait_ge(qk_ev, f - 3)
                for e in range(2):
                    for t in range(T):
                        if f < KC // 2:
                            m = 2 * f + e
                            src = q_t[:, t, 2 * m:2 * m + 2, :].rearrange("p a b -> p (a b)")
                        else:
                            src = k_two[:, t, 2 * f - KC + e].rearrange("p a b -> p (a b)")
                        mm = pe.transpose(misc[:, f % 4, e * S + t * P:e * S + (t + 1) * P], src, ident[:])
                mm.then_inc(qk_turned, 1)

            def scores_of(i):
                for e in range(2):
                    half = slice(HD * e, HD * e + HD)
                    pe.matmul(misc[:, e, 0:S], q_tr[half, i, P:S], k_tr[half, i // 2, :], start=True, stop=True, skip_group_check=True)
                    mm = pe.matmul(misc[:, e, S:3 * P], q_tr[half, i, 0:P], k_tr[half, i // 2, 0:P], start=True, stop=True, skip_group_check=True)
                mm.then_inc(sc_mm, 1)

            def turn_probs(i):
                pe.wait_ge(sc_exp, 4 * i + 4)
                if i:
                    pe.wait_ge(p_ev, i)
                for e in range(2):
                    for n in range(3):
                        mm = pe.transpose(misc[:, 2 + e, n * P:(n + 1) * P], scores[:, i % 4, e, n * P:(n + 1) * P], ident[:])
                mm.then_inc(p_turned, 1)

            def values(i):
                pe.wait_ge(p_ev, i + 1)
                n = i // 2
                for e in range(2):
                    own = slice(3 * P + HD * e, 3 * P + HD * (e + 1))
                    pe.matmul(misc[:, 0, own], p_tr[:, i % 2, e, S:3 * P], v_t[:, 0, n, :], start=True, stop=True, skip_group_check=True)
                    pe.matmul(misc[:, 1, own], p_tr[:, i % 2, e, 0:P], v_t[:, 0, n, :], start=True, stop=False, skip_group_check=True)
                    mm = pe.matmul(misc[:, 1, own], p_tr[:, i % 2, e, P:S], v_t[:, 1, n, :], start=False, stop=True, skip_group_check=True)
                mm.then_inc(pv_mm, 1)

            def attention(place):
                if Q_TURN <= place < Q_TURN + KC // 4:
                    if place == Q_TURN:
                        pe.wait_ge(dt_x, 1)
                        pe.wait_ge(q_ready, 1)
                    for e in range(2):
                        turn_qk(2 * (place - Q_TURN) + e)
                elif K_TURN <= place < K_TURN + KV // 4:
                    if place == K_TURN:
                        pe.wait_ge(k_ready, 1)
                    for e in range(2):
                        turn_qk(KC // 2 + 2 * (place - K_TURN) + e)
                elif place >= PAIR_START:
                    i, late = divmod(place - PAIR_START, PAIR_STEP)
                    if late:
                        if 0 <= i - TURN_LAG < PAIRS:
                            turn_probs(i - TURN_LAG)
                        return
                    if i == 0:
                        pe.wait_ge(qkv_ev, B_XBC)
                        pe.wait_ge(qk_ev, KV // 2 + KC // 2)
                    elif i <= PAIRS:
                        pe.wait_ge(sc_ev, i)
                    if 0 < i - VALUE_LAG <= PAIRS:
                        pe.wait_ge(o_ev, i - VALUE_LAG)
                    if 0 <= i - VALUE_LAG < PAIRS:
                        values(i - VALUE_LAG)
                    if i < PAIRS:
                        scores_of(i)

            def beside_v(h):
                attention(V_PLACE + h)

            for b in range(B_XBC):
                if b >= 2:
                    pe.wait_ge(qkv_ev, b - 1)
                tokens(w_in2, b, b % 2, normed, beside_v if b == B_V else None, normed_yet(2) if b == 0 else None)
                if b == 0:
                    rows_of(g_fin, fin_mm)
                if b == 1:
                    pe.wait_ge(dt_lo, 1)
                    pe.wait_ge(fin_x, T)
                    for t in range(T):
                        own = slice(t * P, (t + 1) * P)
                        for k in range(KC):
                            o = misc[:, 0, t * SH:(t + 1) * SH]
                            pe.matmul(o, a_hi[:, k, own], w_dt_hi[:, k, :], start=(k == 0), stop=False, skip_group_check=True)
                            pe.matmul(o, a_hi[:, k, own], w_dt_lo[:, k, :], start=False, stop=False, skip_group_check=True)
                            mm = pe.matmul(o, a_lo[:, k, own], w_dt_hi[:, k, :], start=False, stop=(k == KC - 1), skip_group_check=True)
                    mm.then_inc(dt_mm, 1)
            pe.wait_ge(dt_x, 1)

            for b in range(B_XBC, B_Z):
                j = b - B_XBC
                if j < 2:
                    pe.wait_ge(qkv_ev, 5 + j)
                else:
                    pe.wait_ge(c2_tap, 12 * (j - 1))
                features(w_in2, b, b % 2, a_hi, a_lo, lambda h: attention(j * w_in2.halves + h))
            def states(place):
                if place < 4:
                    for i in (2 * place, 2 * place + 1):
                        t, f = i // 4, i % 4
                        if i == 0:
                            pe.wait_ge(xbc_ev, 4)
                            pe.wait_ge(o_ev, PAIRS)
                        if i >= 4:
                            pe.wait_ge(xs_ev, i - 3)
                        for e in range(4):
                            mm = pe.transpose(misc[:, i % 4, e * P:(e + 1) * P], xbc[:, 4 * f + e, t * P:(t + 1) * P], ident[:])
                        mm.then_inc(xs_turned, 1)
                elif place == B_TURN:
                    pe.wait_ge(xbc_ev, 5)
                    pe.wait_ge(xs_ev, 5)
                    for g in range(SG):
                        mm = pe.transpose(misc[:, 0, g * P:(g + 1) * P], xbc[:, KC + g, 0:P], ident[:])
                    mm.then_inc(b_turned, 1)
                    pe.wait_ge(xs_ev, 6)
                    pe.wait_ge(a_ready, 1)
                    for c in range(T):
                        pe.matmul(misc[:, 1, c * SH:(c + 1) * SH], upper[:], a_dt[:, c * SH:(c + 1) * SH], start=True, stop=True, skip_group_check=True)
                    pe.matmul(misc[:, 1, T * SH:T * SH + SH], ones[:], a_dt[:, 0:SH], start=True, stop=True, skip_group_check=True).then_inc(cs_mm, 1)
                elif place == STATE:
                    pe.wait_ge(st_in, 1)
                    pe.wait_ge(b_ev, 1)
                    pe.wait_ge(cs_ev, 2)
                    pe.wait_ge(xs_ev, 8)
                    for g in range(SG):
                        mm = pe.matmul(misc[:, g, :], b_tok[:, g, :], state[:, 8 * g:8 * g + 8, :].rearrange("p h e -> p (h e)"), start=True, stop=True)
                    mm.then_inc(st_mm, 1)
                elif place == FROM_STATE:
                    pe.wait_ge(st_ev, 1)
                    pe.wait_ge(xbc_ev, 6)
                    for g in range(SG):
                        mm = pe.matmul(misc[:, g, :], xbc[:, KC + SG + g, P:S], state[:, 8 * g:8 * g + 8, :].rearrange("p h e -> p (h e)"), start=True, stop=True)
                    mm.then_inc(yo_mm, 1)
                for c in range(T):
                    if DECAYS[c] <= place < DECAYS[c] + 4:
                        decays(c, place - DECAYS[c])
                    elif place == WITHIN[c]:
                        within(c)

            def decays(c, step):
                if step == 0:
                    if c == 0:
                        pe.wait_ge(yo_ev, 1)
                    else:
                        pe.wait_ge(yd_ev, c)
                    own = slice(c * P, (c + 1) * P)
                    for g in range(SG):
                        mm = pe.matmul(misc[:, 0, g * P:(g + 1) * P], xbc[:, KC + g, own], xbc[:, KC + SG + g, own], start=True, stop=True, skip_group_check=True)
                    mm.then_inc(cb_mm, 1)
                for n in (2 * step, 2 * step + 1):
                    if n >= 3:
                        pe.wait_ge(seg_ev, 8 * c + n - 2)
                    for e in range(4):
                        h = c * SH + 4 * n + e
                        mm = pe.matmul(misc[:, 1 + n % 3, e * P:(e + 1) * P], a_dt[:, h:h + 1].to_broadcast([P, P]), upper[:], start=True, stop=True, skip_group_check=True)
                    mm.then_inc(seg_mm, 1)

            def within(c):
                pe.wait_ge(cb_ev, c + 1)
                pe.wait_ge(seg_ev, 8 * c + 8)
                for h in range(SH):
                    if h % 8 == 0:
                        pe.wait_ge(decay_ready, SG * c + h // 8 + 1)
                    mm = pe.matmul(misc[:, h // 8, (h % 8) * SP:(h % 8 + 1) * SP], decay[:, h, :], xdt[:, c, h, :], start=True, stop=True, skip_group_check=True)
                mm.then_inc(yd_mm, 1)

            for b in range(B_Z, w_in2.blocks):
                j = b - B_Z
                if j < 2:
                    pe.wait_ge(c2_tap, 60 + 12 * j)
                else:
                    pe.wait_ge(z_ev, j - 1)
                tokens(w_in2, b, b % 2, normed, lambda h: states(j * w_in2.halves + h))

            pe.wait_ge(yd_ev, T)
            for f in range(KC // 2):
                if f >= 4:
                    pe.wait_ge(ya_lo, f - 3)
                for e in range(2):
                    m = 2 * f + e
                    for t in range(T):
                        mm = pe.transpose(misc[:, f % 4, e * S + t * P:e * S + (t + 1) * P],
                                          o_t[:, t, 2 * m:2 * m + 2, :].rearrange("p a b -> p (a b)"), ident[:])
                mm.then_inc(yo_turned, 1)

            def state_output(h):
                if Y_TURN <= h < Y_TURN + 4:
                    for f in (2 * (h - Y_TURN), 2 * (h - Y_TURN) + 1):
                        if f < 4:
                            pe.wait_ge(ya_lo, f + 5)
                        else:
                            pe.wait_ge(ys_lo, 2 * (f - 4) + 2)
                        for m in (2 * f, 2 * f + 1):
                            for t in range(T):
                                n = t * SG + m // 4
                                pe.wait_ge(ys_ready, n + 1)
                                mm = pe.matmul(misc[:, f % 4, m % 2 * S + t * P:m % 2 * S + (t + 1) * P],
                                               y_t[:, t, 2 * m:2 * m + 2, :].rearrange("p a b -> p (a b)"), g_diag[:, n, :],
                                               start=True, stop=True, skip_group_check=True)
                        mm.then_inc(ys_turned, 1)

            def mixed_yet(h):
                if h < 8:
                    pe.wait_ge(ya_lo, h + 1)
                else:
                    pe.wait_ge(ys_lo, 2 * (h - 8) + 2)

            def mixed(k):
                return (s_hi[:, k, :], s_lo[:, k, :]) if k < KC else (a_hi[:, k - KC, :], a_lo[:, k - KC, :])

            for b in range(w_out2.blocks):
                if b < 2:
                    pe.wait_ge(z_ev, b + 3)
                else:
                    pe.wait_ge(x_new, X_BEFORE[3] + b - 1)
                tokens(w_out2, b, b % 2, mixed, state_output if b == 0 else norm_beside(3, b), mixed_yet if b == 0 else None)

            norm_end(3)
            for b in range(2):
                features(up2, b, b, a_hi, a_lo, None, normed_yet(3) if b == 0 else None)
            with pe.Fori(1, up2.blocks // 2) as i:
                for c in range(2):
                    pe.wait_ge(ff_prod, i * 2 + (up1.blocks + c - 1))
                    features(up2, i * 2 + c, c, a_hi, a_lo)
            pe.wait_ge(h_lo, up1.blocks + up2.blocks - 1)
            for b in range(down2.blocks):
                if b >= 2:
                    pe.wait_ge(x_new, X_BEFORE[4] + b - 1)
                tokens(down2, b, b % 2, hidden, norm_beside(4, b, last_hidden(down2, up1.blocks + up2.blocks)))

            norm_end(4)

            def embedding(h):
                if h == 1:
                    pe.wait_ge(ple_landed, 32)
                    for k in range(PLE // P):
                        for t in range(T):
                            mm = pe.transpose(misc[:, 0, k * S + t * P:k * S + (t + 1) * P], p_t[:, t, k * P:(k + 1) * P], ident[:])
                    mm.then_inc(pt_turned, 1)
                elif h in (3, 5):
                    t = h // 2 - 1
                    if t == 0:
                        pe.wait_ge(n_lo, 5 * XG)
                        pe.wait_ge(pt_ev, 1)
                    else:
                        pe.wait_ge(pe_ev, t)
                    for j in range(D // COLS):
                        for k in range(PLE // P):
                            mm = pe.matmul(misc[:, j, :], p_f[:, k, t * P:(t + 1) * P], w_ple[:, k, j * COLS:(j + 1) * COLS],
                                           start=(k == 0), stop=(k == PLE // P - 1))
                    mm.then_inc(pe_mm, 1)
                elif h == 7:
                    pe.wait_ge(pe_ev, T)
                    rows_of(g_post, post_mm)

            for b in range(ple_gate.blocks):
                if b >= 2:
                    pe.wait_ge(gate_sig, b - 1)
                tokens(ple_gate, b, b % 2, normed, embedding if b == 0 else None, normed_yet(4) if b == 0 else None)

        @block.vector
        def _(dve):
            done = Steps(dve, dve_step)

            def split_lo(ph, b, halves, beside=None):
                for h in halves:
                    at0, _, n = ph.half_rows(h)
                    dve.wait_ge(hi_ready, ph.half(b) + (h + 1))
                    slot = h % HALF_SLOTS
                    dve.tensor_tensor(w_lo[:, slot, 0:n, :], raw[:, h // 2 % RAW_SLOTS, at0:at0 + n, :],
                                      w_hi[:, slot, 0:n, :].bitcast(F32), ALU.subtract).then_inc(lo_ready, 1)
                    if beside:
                        beside(h)

            def stream(ph, finish, nxt, mod_pairs=0, beside=None):
                def one(b, c, more, a=None):
                    def beside(h):
                        place = (b % 4) * ph.halves + (h - ph.lead) % ph.halves
                        if place % 2 == 0:
                            mod_product(a, place // 2, a % 2, read=a - 1)

                    beside = None if a is None else beside
                    split_lo(ph, b, range(ph.lead, ph.halves), beside)
                    if more:
                        split_lo(ph, b + 1, range(ph.lead), beside)
                    elif nxt:
                        split_lo(nxt, 0, range(nxt.lead))
                    dve.wait_ge(w_used, ph.end(b))
                    finish(b, c)

                if ph.blocks == XB:
                    for b in range(ph.blocks):
                        more = b + 1 < ph.blocks
                        for n in range(ph.halves):
                            h = ph.lead + n
                            if h < ph.halves:
                                split_lo(ph, b, [h])
                            elif more:
                                split_lo(ph, b + 1, [h - ph.halves])
                            if beside and b == 0:
                                beside(n)
                        if not more:
                            split_lo(nxt, 0, range(LEAD))
                        dve.wait_ge(w_used, ph.end(b))
                        finish(b, b % 2)
                    split_lo(nxt, 0, range(LEAD, nxt.lead))
                    return
                if mod_pairs:
                    for i in range(mod_pairs):
                        for c in range(2):
                            one(i * 2 + c, c, True, i // 2 + (MOD_BLOCKS - mod_pairs // 2))
                with dve.Fori(mod_pairs, ph.blocks // 2 - 1) as i:
                    one(i * 2, 0, True)
                    one(i * 2 + 1, 1, True)
                if mod_pairs:
                    mod_result(MOD_BLOCKS - mod_pairs // 2, mod_pairs // 2)
                one(ph.blocks - 2, 0, True)
                one(ph.blocks - 1, 1, False)

            def inverse_root(squares, out_, var_signal, std_signal, k, meanwhile=None, signal=None):
                dve.tensor_scalar(var, squares, 1.0 / D, EPS, ALU.mult, ALU.add).then_inc(var_signal, 1)
                if meanwhile:
                    meanwhile()
                dve.wait_ge(std_signal, k)
                ins = dve.reciprocal(out_, std)
                if signal:
                    ins.then_inc(signal, 1)
                else:
                    done(ins)
                    done.wait()

            def norm_low(n, q, shift=None):
                dve.wait_ge(n_hi, XG * n + q + 1)
                two = slice(2 * q, 2 * q + 2)
                if shift is None:
                    dve.tensor_tensor(flat(a_lo[:, two, :]), flat(norm_features[n][:, two, :]), flat(a_hi[:, two, :]).bitcast(F32),
                                      ALU.subtract).then_inc(n_lo, 1)
                else:
                    for m in (2 * q, 2 * q + 1):
                        ins = dve.scalar_tensor_tensor(out=a_lo[:, m, :], in0=norm_features[n][:, m, :], scalar=shift[:, m:m + 1],
                                                       in1=a_hi[:, m, :].bitcast(F32), op0=ALU.add, op1=ALU.subtract)
                    ins.then_inc(n_lo, 1)

            def norm_end(n, gain=None, shift=None, meanwhile=None):
                if n == 2:
                    dve.wait_ge(n_sums, XB)
                    sums = misc[:, 3, 0:2 * T].rearrange("p (t n) -> p t n", n=2)
                    inverse_root(sums[:, :, 1], rstd, n_var, n_std, ROOTS[n][0])
                    done(dve.tensor_tensor(squared, rstd, rstd, ALU.mult))
                    done.wait()
                    done(dve.tensor_tensor(squared, squared, sums[:, :, 0], ALU.mult))
                    done.wait()
                    inverse_root(squared, scale, n_var, n_std, ROOTS[n][1])
                    done(dve.tensor_tensor(scale, scale, rstd, ALU.mult))
                    done.wait()
                else:
                    dve.wait_ge(n_ssq, SSQ_DONE[n])
                    done(dve.tensor_reduce(ssq, ssq_parts.rearrange("p (t b) -> p t b", t=T), AX.X, ALU.add))
                    done.wait()
                    inverse_root(ssq, scale, n_var, n_std, ROOTS[n], meanwhile)
                for t in range(T):
                    dve.tensor_scalar(norm_diag[n][:, t, :], ident[:], scale[:, t:t + 1], None, ALU.mult).then_inc(n_diag, 1)
                dve.wait_ge(n_row, n)
                by = misc[:, 2, 0:S]
                for q in range(XG):
                    dve.wait_ge(n_f, XB * n + q // 2 + 1)
                    two = norm_features[n][:, 2 * q:2 * q + 2, :]
                    if gain is None:
                        dve.tensor_tensor(two, two, by[:, None, :].to_broadcast([P, 2, S]), ALU.mult).then_inc(n_scaled, 1)
                    else:
                        for m in range(2):
                            ins = dve.scalar_tensor_tensor(out=two[:, m, :], in0=two[:, m, :], scalar=gain[:, 2 * q + m:2 * q + m + 1],
                                                           in1=by, op0=ALU.mult, op1=ALU.mult)
                        ins.then_inc(n_scaled, 1)
                    if q:
                        norm_low(n, q - 1, shift)
                norm_low(n, XG - 1, shift)

            def log1p(e, den, s, s2, p):
                done(dve.tensor_scalar(den, e, 2.0, None, ALU.add))
                done.wait()
                done(dve.reciprocal(den, den))
                done.wait()
                done(dve.tensor_tensor(s, e, den, ALU.mult))
                done.wait()
                done(dve.tensor_tensor(s2, s, s, ALU.mult))
                done.wait()
                done(dve.tensor_scalar(p, s2, 1.0 / 19, None, ALU.mult))
                done.wait()
                for n in range(17, 1, -2):
                    done(dve.scalar_tensor_tensor(out=p, in0=p, scalar=1.0 / n, in1=s2, op0=ALU.add, op1=ALU.mult))
                    done.wait()
                done(dve.tensor_scalar(p, p, 1.0, 2.0, ALU.add, ALU.mult))
                done.wait()
                done(dve.tensor_tensor(p, p, s, ALU.mult))
                done.wait()

            def conv_taps(place, c, m0, taps, n_taps, width, dst, bias_signal, tap_signal, before):
                if place >= 2 * (n_taps - 1):
                    return
                j = place // 2 + 1
                for m in (2 * (place % 2), 2 * (place % 2) + 1):
                    if j == 1:
                        dve.wait_ge(bias_signal, m0 + m // 2 * 2 + 2)
                    else:
                        dve.wait_ge(tap_signal, before + 4 * (j - 2) + m + 1)
                    col = (n_taps - 1 - j) * width + m0 + m
                    dve.scalar_tensor_tensor(
                        out=dst[:, m0 + m, j:S], in0=pair[:, c, m // 2, (m % 2) * S:(m % 2 + 1) * S - j],
                        scalar=taps[:, col:col + 1], in1=dst[:, m0 + m, j:S], op0=ALU.mult, op1=ALU.add).then_inc(tap_signal, 1)

            def prepare():
                dve.wait_ge(vec_ready, 2)
                dve.wait_ge(consts, CONSTS)
                dve.wait_ge(rows_landed, 16 * (len(row_loads) + 1))
                dve.scalar_tensor_tensor(out=l_abs, in0=lam, scalar=-1.0, in1=lam, op0=ALU.mult, op1=ALU.max).then_inc(prep_in, 1)
                done(dve.tensor_copy(pos_f, pos_i[:]))
                done.wait()
                for t in range(T):
                    done(dve.tensor_scalar(ang[:, t * HALF_ROPE:(t + 1) * HALF_ROPE], freq, pos_f[:, t:t + 1], None, ALU.mult))
                done.wait()
                done(dve.tensor_scalar(turns, ang, float(1 / (2 * np.pi)), ROUND, ALU.mult, ALU.add))
                done.wait()
                done(dve.tensor_scalar(turns, turns, ROUND, None, ALU.subtract))
                done.wait()
                for n, part in enumerate((TWO_PI_1, TWO_PI_2, TWO_PI_3)):
                    done(dve.scalar_tensor_tensor(out=ang_r, in0=turns, scalar=-part, in1=ang if n == 0 else ang_r, op0=ALU.mult, op1=ALU.add))
                    done.wait()
                dve.tensor_scalar(ang_r, ang_r, 3.1415925, -3.1415925, ALU.min, ALU.max).then_inc(prep_in, 1)
                dve.wait_ge(prep_exp, 1)
                log1p(l_exp, l_den, l_s, l_s2, l_p)
                done(dve.tensor_scalar(l_max, lam, -1.0, 0.0, ALU.mult, ALU.max))
                done.wait()
                done(dve.tensor_tensor(l_p, l_p, l_max, ALU.add))
                done.wait()
                dve.tensor_scalar(ls8, l_p, -LRU_C, None, ALU.mult).then_inc(prep_in, 1)
                dve.tensor_scalar(nls8, l_p, LRU_C, None, ALU.mult).then_inc(prep_in, 1)
                dve.wait_ge(prep_exp, 4)
                done(dve.tensor_tensor(half_sin, half_sin, half_sin, ALU.mult))
                done.wait()
                done(dve.tensor_scalar(cos_t, half_sin, -2.0, 1.0, ALU.mult, ALU.add))
                done(dve.reciprocal(window_inv, window_inv))

            dve.wait_ge(c_ready, 1)

            def mod_product(a, k, c, read=None):
                dve.wait_ge(mod_landed[k % MOD_SLOTS], a * (16 * KC // MOD_SLOTS) + 16 * (k // MOD_SLOTS + 1))
                of, by, acc = mod_raw[:, k % MOD_SLOTS, :], c_silu[:, k:k + 1], mod_acc[:, c, :]
                if k == 0:
                    if read is not None:
                        dve.wait_ge(mod_mm, read)
                    dve.tensor_scalar(acc, of, by, None, ALU.mult).then_inc(mod_step, 1)
                else:
                    dve.wait_ge(mod_step, a * KC + k)
                    dve.scalar_tensor_tensor(out=acc, in0=of, scalar=by, in1=acc, op0=ALU.mult, op1=ALU.add).then_inc(mod_step, 1)

            def mod_result(a, blocks=1):
                own = slice(a * MOD_M, (a + blocks) * MOD_M)
                dve.wait_ge(mod_mm, a + blocks)
                dve.tensor_tensor(mod[:, own], misc[:, 3, own], b_ada[:, own], ALU.add).then_inc(mod_ready, 1)

            def mod_beside(place):
                for n in mod_at(place):
                    mod_product(n // KC, n % KC, n // KC % 2, read=n // KC - 1)

            for a in range(MOD_FIRST):
                for k in range(KC):
                    mod_product(a, k, a % 2, read=a - 1 if a >= 2 else None)
                    if a and k == 2:
                        mod_result(a - 1)
                    if (a, k) == (1, 4):
                        dve.wait_ge(n_ssq, T)
                        inverse_root(ssq, rstd, n_var, n_std, ROOTS[0], signal=n_rstd)
                if a == 0:
                    prepare()
            mod_result(MOD_FIRST - 1)
            dve.wait_ge(mod_ready, MOD_FIRST)

            def modulated_gain(scale, g):
                done(dve.scalar_tensor_tensor(out=g_mod, in0=scale, scalar=1.0, in1=g, op0=ALU.add, op1=ALU.mult))
                done.wait()

            modulated_gain(mod[:, KC:2 * KC], g_mix)

            for q in range(XG):
                dve.wait_ge(n_f, q // 2 + 1)
                for m in (2 * q, 2 * q + 1):
                    of = norm_features[0][:, m, :]
                    ins = dve.tensor_scalar(of, of, g_mod[:, m:m + 1], mod[:, m:m + 1], ALU.mult, ALU.add)
                ins.then_inc(n_scaled, 1)
                if q:
                    norm_low(0, q - 1)
                    if q <= LEAD:
                        split_lo(w_in, 0, [q - 1])
            norm_low(0, XG - 1)

            def mixer(b):
                for n in range(w_in.halves):
                    h = LEAD + n
                    ph, b1 = (w_in, b) if h < w_in.halves else (w_in, b + 1) if b + 1 < w_in.blocks else (w_out, 0)
                    split_lo(ph, b1, [h % w_in.halves])
                    beside(b, n)
                    mod_beside(b * w_in.halves + n)
                    if b in (3, 5) and n == 3:
                        mod_result(4 + (b - 3) // 2)

            def window(g):
                w, dst, src = POOL_WINDOWS[g], (pool_a, pool_b)[g % 2], (pool_a, pool_b)[1 - g % 2] if g else xp
                if g:
                    done.wait()
                done(dve.tensor_copy(dst[:, 2 * g:, 0:w // 2], src[:, 2 * g:, 0:w // 2]))
                done(dve.tensor_tensor(dst[:, 2 * g:, w // 2:], src[:, 2 * g:, w // 2:], src[:, 2 * g:, 0:S - w // 2], ALU.add))

            def beside(b, n):
                if b in (1, 2):
                    conv_taps(n, (b - 1) % 2, 4 * (b - 1), cw1, CONV, RC, xc, c1_bias, c1_tap, 12 * (b - 1))
                if (b, n) == (3, 2):
                    dve.wait_ge(gate_ev, 2 * RC)
                    dve.wait_ge(c1_tap, 24)
                    done(dve.tensor_tensor(flat(lru_u[:]), flat(lru_u[:]), flat(xc[:]), ALU.mult))
                elif (b, n) == (3, 6):
                    dve.wait_ge(lru_t, RC)
                    dve.wait_ge(lru_s, 1)
                    dve.scalar_tensor_tensor(out=flat(lru_m[:]), in0=flat(lru_sq[:]), scalar=1.0, in1=flat(lru_m[:]),
                                             op0=ALU.add, op1=ALU.mult).then_inc(lru_q, 1)
                elif (b, n) == (4, 1):
                    dve.wait_ge(lru_e, RC)
                    dve.wait_ge(lru_r, 1)
                    done(dve.tensor_tensor(flat(lru_u[:]), flat(lru_u[:]), flat(lru_m[:]), ALU.mult))
                    done(dve.memset(lru_a[:, :, 0:1], 0.0))
                elif (b, n) == (4, 2):
                    done.wait()
                    done(dve.tensor_tensor_scan(flat(xc[:]), flat(lru_a[:]), flat(lru_u[:]), 0.0, ALU.mult, ALU.add))
                elif b == 4 and n in (3, 4, 5):
                    if n == 3:
                        dve.wait_ge(xp_ev, 2)
                    for g in ((0,), (1,), (2, 3))[n - 3]:
                        window(g)
                elif (b, n) == (4, 6):
                    done.wait()
                    for g, w in enumerate(POOL_WINDOWS):
                        sums, two = (pool_a, pool_b)[g % 2], slice(2 * g, 2 * g + 2)
                        done(dve.scalar_tensor_tensor(out=sums[:, two, 0:w - 1], in0=sums[:, two, 0:w - 1], scalar=float(w),
                                                      in1=window_inv[:, None, 0:w - 1].to_broadcast([P, 2, w - 1]), op0=ALU.mult, op1=ALU.mult))
                elif (b, n) == (4, 7):
                    done.wait()
                    for g, w in enumerate(POOL_WINDOWS):
                        sums, two = (pool_a, pool_b)[g % 2], slice(2 * g, 2 * g + 2)
                        dve.scalar_tensor_tensor(out=xp[:, two, :], in0=sums[:, two, :], scalar=1.0 / w, in1=xp[:, two, :],
                                                 op0=ALU.mult, op1=ALU.subtract).then_inc(pooled, 1)
                elif (b, n) == (5, 2):
                    lru_out(0)
                elif (b, n) == (5, 5):
                    pooled_out(range(3))
                elif (b, n) == (5, 6):
                    pooled_out(range(3, 6))

            def lru_out(e):
                dve.wait_ge(ge_ev, e + 1)
                done.wait()
                half = slice(4 * e, 4 * e + 4)
                dve.tensor_tensor(flat(y_lru[:, half, :]), flat(y_lru[:, half, :]), flat(xc[:, half, :]), ALU.mult).then_inc(lru_y, 1)

            def lru_rest(e):
                half = slice(4 * e, 4 * e + 4)
                dve.wait_ge(lru_hi_ev, e + 1)
                dve.tensor_tensor(flat(lru_lo[:, half, :]), flat(y_lru[:, half, :]), flat(lru_hi[:, half, :]).bitcast(F32),
                                  ALU.subtract).then_inc(lru_lo_ev, 1)

            def pooled_out(chunks):
                for m in chunks:
                    dve.wait_ge(pool_hi_ev, m // 2 * 2 + 2)
                    dve.scalar_tensor_tensor(out=pool_lo[:, m, :], in0=misc[:, m // 2 % 3, (m % 2) * S:(m % 2 + 1) * S],
                                             scalar=ls_pool[:, m:m + 1], in1=pool_hi[:, m, :].bitcast(F32),
                                             op0=ALU.mult, op1=ALU.subtract).then_inc(pool_lo_ev, 1)

            for b in range(w_in.blocks):
                mixer(b)
            pooled_out(range(6, 2 * G))
            lru_rest(0)
            lru_out(1)
            lru_rest(1)

            def add_gated(x0):
                def finish(b, c):
                    cols = bass.ds(b * COLS, COLS)
                    dve.tensor_tensor(res_tmp[:], pair[:, c], row[:, None, cols].to_broadcast([P, T, COLS]), ALU.mult).then_inc(res_ready, 1)
                    dve.wait_ge(res_ready, b + (x0 + 1))
                    dve.tensor_tensor(x[:, :, cols], x[:, :, cols], res_tmp[:], ALU.add).then_inc(x_new, 1)
                return finish

            def add_plain(b, c):
                cols = bass.ds(b * COLS, COLS)
                dve.tensor_tensor(x[:, :, cols], x[:, :, cols], pair[:, c], ALU.add).then_inc(x_new, 1)

            for b in range(w_out.blocks):
                def beside(h):
                    mod_beside(w_out.half(b) + (h - LEAD) % w_out.halves)
                    if b in (1, 2) and h == w_out.halves - 1:
                        mod_result(5 + b)

                split_lo(w_out, b, range(LEAD, w_out.halves), beside)
                nxt, b1 = (w_out, b + 1) if b + 1 < w_out.blocks else (up1, 0)
                split_lo(nxt, b1, range(LEAD), beside)
                dve.wait_ge(w_used, w_out.end(b))
                dve.wait_ge(row_ready, 1)
                add_gated(0)(b, b % 2)

            def last_results():
                mod_result(8, 2)
                dve.wait_ge(mod_ready, 9)
                modulated_gain(mod[:, 4 * KC:5 * KC], g_ffn)

            norm_end(1, g_mod, mod[:, 3 * KC:4 * KC], last_results)

            def hidden(b, c, source, blocks0):
                dve.wait_ge(ff_sig, b + (blocks0 + 1))
                dve.tensor_tensor(flat(ff_u[:]), flat(ff_g[:]), source, ALU.mult).then_inc(ff_prod, 1)
                dve.wait_ge(ff_prod, b + (blocks0 + 1))
                two = bass.ds(b * 2, 2)
                dve.tensor_copy(hid_hi[:, two, :], ff_u[:]).then_inc(h_hi, 1)
                dve.wait_ge(h_hi, b + (blocks0 + 1))
                dve.tensor_tensor(hid_lo[:, two, :], ff_u[:], hid_hi[:, two, :].bitcast(F32), ALU.subtract).then_inc(h_lo, 1)

            stream(up1, lambda b, c: hidden(b, c, pair[:, c, 1, :], 0), down1, mod_pairs=4)
            dve.wait_ge(row_ready, 2)
            dve.tensor_tensor(g_both, g_fin, g_att, ALU.mult)
            dve.tensor_tensor(g_weigh[:, :, 0], g_fin, g_fin, ALU.mult)
            dve.memset(g_weigh[:, :, 1], 1.0).then_inc(n_gain, 1)
            stream(down1, add_gated(w_out.blocks), w_in2)

            norm_end(2)

            def mixer2(b, beside=None):
                for n in range(w_in2.halves):
                    h = LEAD + n
                    ph, b1 = (w_in2, b) if h < w_in2.halves else (w_in2, b + 1) if b + 1 < w_in2.blocks else (w_out2, 0)
                    split_lo(ph, b1, [h % w_in2.halves])
                    if beside:
                        beside((b - B_XBC) * w_in2.halves + n)

            def hn(a, t, h0, n):
                return a.rearrange("p (t h) -> p t h", t=T)[:, t, h0:h0 + n]

            def over_tiles(a):
                return a.rearrange("p (t h) -> p t h", t=T)

            for b in range(B_K):
                mixer2(b)
                dve.wait_ge(qkv_ev, b + 1)
                eight = slice(8 * b, 8 * b + 8)
                done(dve.tensor_tensor(q_sq[:, :, eight, :].rearrange("p t h e -> p t (h e)"), q_t[:, :, eight, :].rearrange("p t h e -> p t (h e)"),
                                       q_t[:, :, eight, :].rearrange("p t h e -> p t (h e)"), ALU.mult))
                done.wait()
                done(dve.tensor_reduce(over_tiles(hn_ssq)[:, :, eight], q_sq[:, :, eight, :], AX.X, ALU.add))
                if b == 0:
                    dve.wait_ge(fin_mm, 1)
                    for t in range(T):
                        dve.scalar_tensor_tensor(out=x[:, t, :], in0=x[:, t, :], scalar=rstd[:, t:t + 1], in1=flat(misc[:]),
                                                 op0=ALU.mult, op1=ALU.mult).then_inc(fin_x, 1)
                    dve.wait_ge(dt_hi, 1)
                    dve.tensor_tensor(flat(w_dt_lo[:]), flat(w_dt[:]), flat(w_dt_hi[:]).bitcast(F32), ALU.subtract).then_inc(dt_lo, 1)
                if b == 2:
                    dve.wait_ge(dt_mm, 1)
                    dve.tensor_tensor(over_tiles(d_x), misc[:, 0, 0:T * SH].rearrange("p (t h) -> p t h", t=T),
                                      dt_bias[:, None, :].to_broadcast([P, T, SH]), ALU.add).then_inc(dt_raw, 1)
                    dve.wait_ge(dt_raw, 1)
                    dve.scalar_tensor_tensor(out=d_abs, in0=d_x, scalar=-1.0, in1=d_x, op0=ALU.mult, op1=ALU.max).then_inc(dt_x, 1)
            def scale_heads(a, t, h0, n):
                done(dve.tensor_tensor(a[:, t], a[:, t], hn(hn_r, t, h0, n)[:, :, None].to_broadcast([P, n, HD]), ALU.mult))

            def gain_heads(a, t, g, n):
                done(dve.tensor_tensor(a[:, t], a[:, t], g[:, None, :].to_broadcast([P, n, HD]), ALU.mult))

            def rotate(a, n):
                for t in range(T):
                    one, two = a[:, t, :, 0:HALF_ROPE], a[:, t, :, HALF_ROPE:2 * HALF_ROPE]
                    cos, sin = (v[:, None, t * HALF_ROPE:(t + 1) * HALF_ROPE].to_broadcast([P, n, HALF_ROPE]) for v in (cos_t, sin_t))
                    for i, (of, by) in enumerate(((one, cos), (two, sin), (two, cos), (one, sin))):
                        done(dve.tensor_tensor(rope[:, i, t, 0:n, :], of, by, ALU.mult))
                done.wait()
                for t in range(T):
                    done(dve.tensor_tensor(a[:, t, :, 0:HALF_ROPE], rope[:, 0, t, 0:n, :], rope[:, 1, t, 0:n, :], ALU.subtract))
                    last = dve.tensor_tensor(a[:, t, :, HALF_ROPE:2 * HALF_ROPE], rope[:, 2, t, 0:n, :], rope[:, 3, t, 0:n, :], ALU.add)
                    if a is q_t and t == T - 1:
                        last.then_inc(q_ready, 1)
                    else:
                        done(last)

            def pair_of(a, i):
                return by_block(a)[:, :, 2 * i:2 * i + 2]

            def masked(i):
                dve.wait_ge(sc_mm, i + 1)
                if i >= 4:
                    dve.wait_ge(p_turned, i - 3)
                dve.scalar_tensor_tensor(out=scores[:, i % 4], in0=misc[:, 0:2, 0:3 * P], scalar=float(HD) ** -0.5,
                                         in1=a_mask[:, None, :].to_broadcast([P, 2, 3 * P]), op0=ALU.mult, op1=ALU.add).then_inc(sc_ev, 1)

            def maxima(i):
                dve.wait_ge(sc_ev, i + 1)
                done(dve.tensor_reduce(pair_of(m_max, i)[:, 1], scores[:, i % 4, :, 0:S], AX.X, ALU.max))
                done(dve.tensor_reduce(pair_of(m_max, i)[:, 0], scores[:, i % 4, :, S:3 * P], AX.X, ALU.max))
                done.wait()
                sink = sinks[:, None, 2 * i:2 * i + 2].to_broadcast([P, 2, 2])
                done(dve.tensor_tensor(pair_of(m_all, i), pair_of(m_max, i), sink, ALU.max))
                done.wait()
                done(dve.tensor_scalar(pair_of(m_neg, i), pair_of(m_all, i), -1.0, None, ALU.mult))
                done.wait()
                dve.tensor_tensor(pair_of(m_sink, i), pair_of(m_neg, i), sink, ALU.add).then_inc(sc_max, 1)

            def inverses(i):
                dve.wait_ge(sink_exp, i + 1)
                dve.wait_ge(sc_exp, 4 * i + 4)
                done(dve.tensor_tensor(pair_of(e_den, i), pair_of(e_sum, i), pair_of(e_sink, i), ALU.add))
                done.wait()
                done(dve.reciprocal(pair_of(e_inv, i), pair_of(e_den, i)))

            def weighted(i):
                dve.wait_ge(pv_mm, i + 1)
                done.wait()
                for blk in range(2):
                    ins = dve.tensor_tensor(o_t[:, blk, 2 * i:2 * i + 2, :], misc[:, blk, 3 * P:].rearrange("p (h e) -> p h e", h=2),
                                            pair_of(e_inv, i)[:, blk][:, :, None].to_broadcast([P, 2, HD]), ALU.mult)
                    if blk:
                        ins.then_inc(o_ev, 1)

            def attention(place):
                q, k = place - K_PLACE, place - V_PLACE
                if q == 1:
                    dve.wait_ge(hn_s, 1)
                    done(dve.reciprocal(q_part(hn_r), q_part(hn_std)))
                elif q in (2, 3):
                    done.wait()
                    scale_heads(q_t, q - 2, 0, HEADS)
                elif q in (4, 5):
                    done.wait()
                    gain_heads(q_t, q - 4, q_g, HEADS)
                elif q == 6:
                    done.wait()
                    rotate(q_t, HEADS)
                elif k == 1:
                    dve.wait_ge(hn_s, 2)
                    done(dve.reciprocal(k_part(hn_r), k_part(hn_std)))
                    done.wait()
                    for t in range(T):
                        scale_heads(k_t, t, HEADS, KV)
                elif k == 2:
                    done.wait()
                    for t in range(T):
                        gain_heads(k_t, t, k_g, KV)
                elif k == 3:
                    dve.wait_ge(q_ready, 1)
                    done.wait()
                    rotate(k_t, KV)
                elif k == 4:
                    done.wait()
                    for t in range(T):
                        done(dve.tensor_copy(k_two[:, t, :, 0, :], k_t[:, t]))
                        last = dve.tensor_copy(k_two[:, t, :, 1, :], k_t[:, t])
                        if t == T - 1:
                            last.then_inc(k_ready, 1)
                        else:
                            done(last)
                elif place >= PAIR_START:
                    i, late = divmod(place - PAIR_START, PAIR_STEP)
                    if not late:
                        return
                    if i < PAIRS:
                        masked(i)
                    if 0 <= i - VALUE_LAG < PAIRS:
                        weighted(i - VALUE_LAG)
                    if i < PAIRS:
                        maxima(i)
                    if 0 <= i - EXP_LAG < PAIRS:
                        inverses(i - EXP_LAG)

            done.wait()
            dve.tensor_scalar(q_part(hn_var), q_part(hn_ssq), 1.0 / HD, EPS, ALU.mult, ALU.add).then_inc(hn_v, 1)
            mixer2(B_K, attention)
            dve.wait_ge(qkv_ev, B_K + 1)
            done(dve.tensor_tensor(flat3(k_sq[:]), flat3(k_t[:]), flat3(k_t[:]), ALU.mult))
            done.wait()
            done(dve.tensor_reduce(over_tiles(hn_ssq)[:, :, HEADS:], k_sq[:], AX.X, ALU.add))
            done.wait()
            dve.tensor_scalar(k_part(hn_var), k_part(hn_ssq), 1.0 / HD, EPS, ALU.mult, ALU.add).then_inc(hn_v, 1)
            mixer2(B_V, attention)
            dve.wait_ge(dt_exp, 1)
            log1p(d_exp, d_den, d_s, d_s2, d_p)
            done(dve.tensor_scalar(d_max, d_x, 0.0, None, ALU.max))
            done.wait()
            done(dve.tensor_tensor(dt, d_p, d_max, ALU.add))
            done.wait()
            dve.scalar_tensor_tensor(out=over_tiles(a_dt), in0=over_tiles(dt), scalar=-1.0, in1=a_neg[:, None, :].to_broadcast([P, T, SH]),
                                     op0=ALU.mult, op1=ALU.mult).then_inc(a_ready, 1)

            def convolution(place):
                j = place // w_in2.halves - 1
                if j >= 0:
                    conv_taps(place % w_in2.halves, (B_XBC + j) % 2, 4 * j, cw2, CONV, XBC, xbc, c2_bias, c2_tap, 12 * j)

            def attention_beside(place):
                attention(place)
                convolution(place)

            for b in range(B_XBC, B_Z):
                mixer2(b, attention_beside)
            def heads(a, t):
                return a[:, t * SH:(t + 1) * SH][:, :, None].to_broadcast([P, SH, SP])

            def states(place):
                if place < Z0 + w_in2.halves:
                    convolution(place)
                place -= Z0
                if place in (4, 6):
                    t = place // 2 - 2
                    dve.wait_ge(a_ready, 1)
                    dve.wait_ge(xs_ev, 4 * (t + 1))
                    dve.tensor_tensor(xdt[:, t], xs_t[:, t], heads(dt, t), ALU.mult).then_inc(xdt_ready, 1)
                elif place == B_TURN + 2:
                    dve.wait_ge(cs_ev, 2)
                    dve.tensor_tensor(to_last, a_last, a_cs[:, 0:SH], ALU.subtract).then_inc(end_in, 1)
                elif place == B_TURN + 4:
                    dve.wait_ge(end_ev, 2)
                    dve.wait_ge(xdt_ready, 2)
                    dve.tensor_tensor(state[:], xdt[:, 0], heads(to_last, 0), ALU.mult).then_inc(st_in, 1)
                elif place == FROM_STATE + 1:
                    dve.wait_ge(yo_mm, 1)
                    dve.tensor_tensor(state[:], misc.rearrange("p a (h e) -> p (a h) e", e=SP), heads(from_start, 0), ALU.mult).then_inc(yo_ev, 1)
                for c in range(T):
                    step = place - DECAYS[c] - 1
                    if 0 <= step < SG:
                        decays(c, step)
                    if 2 <= step < SG + 2:
                        g = step - 2
                        dve.wait_ge(cb_ev, c + 1)
                        dve.wait_ge(seg_exp, SG * c + g + 1)
                        dve.tensor_tensor(decay[:, 8 * g:8 * g + 8, :], decay[:, 8 * g:8 * g + 8, :], cb[:, g:g + 1, :].to_broadcast([P, 8, P]),
                                          ALU.mult).then_inc(decay_ready, 1)
                    if place == WITHIN[0] - 1 + c:
                        done(dve.tensor_tensor(xs_t[:, c], xs_t[:, c], heads(d_skip, 0), ALU.mult))
                    if place == WITHIN[c] + 1:
                        done.wait()
                        dve.wait_ge(yd_mm, c + 1)
                        dve.tensor_tensor(flat(y_t[:, c]), flat(xs_t[:, c]), flat(misc[:]), ALU.add).then_inc(yd_ev, 1)
                if place == 28:
                    gate(0, 0, 2)
                elif place == 30:
                    gate(0, 2, 3)

            def decays(c, g):
                if g == 0:
                    dve.wait_ge(cb_mm, c + 1)
                    dve.tensor_tensor(cb[:], misc[:, 0, :].rearrange("p (g l) -> p g l", g=SG), upper[:, None, :].to_broadcast([P, SG, P]),
                                      ALU.mult).then_inc(cb_ev, 1)
                    if c:
                        dve.wait_ge(yd_mm, c)
                for n in (2 * g, 2 * g + 1):
                    dve.wait_ge(seg_mm, 8 * c + n + 1)
                    h = slice(c * SH + 4 * n, c * SH + 4 * n + 4)
                    dve.tensor_tensor(decay[:, 4 * n:4 * n + 4, :], misc[:, 1 + n % 3, :].rearrange("p (h l) -> p h l", h=4),
                                      a_cs[:, h][:, :, None].to_broadcast([P, 4, P]), ALU.subtract).then_inc(seg_ev, 1)
                dve.wait_ge(seg_ev, 8 * c + 2 * g + 2)
                part = flat(decay[:, 8 * g:8 * g + 8, :])
                dve.tensor_scalar(part, part, 0.0, None, ALU.min).then_inc(seg_min, 1)

            def gate(t, j0, j1):
                dve.wait_ge(z_ev, j1)
                own = slice(j0 * COLS, j1 * COLS)
                dve.tensor_tensor(flat(y_t[:, t])[:, own], flat(y_t[:, t])[:, own], z_t[:, t, own], ALU.mult).then_inc(gated, 1)

            for b in range(B_Z, w_in2.blocks):
                mixer2(b, states)
            dve.wait_ge(yd_ev, T)
            done(dve.tensor_tensor(flat(y_t[:, 1]), flat(y_t[:, 1]), flat(state[:]), ALU.add))
            done.wait()
            for f in range(KC // 2):
                two = slice(2 * f, 2 * f + 2)
                dve.wait_ge(ya_hi, f + 1)
                dve.tensor_tensor(flat(a_lo[:, two, :]), misc[:, f % 4, :], flat(a_hi[:, two, :]).bitcast(F32), ALU.subtract).then_inc(ya_lo, 1)

            gate(0, 3, 4)
            gate(1, 0, 4)

            def state_output(place):
                if place == 1:
                    dve.wait_ge(g_sums, T * SG)
                    dve.tensor_scalar(g_var, g_ssq, SG / D, EPS, ALU.mult, ALU.add).then_inc(g_v, 1)
                elif place == 2:
                    dve.wait_ge(g_s, 1)
                    done(dve.reciprocal(g_rstd, g_std))
                    done.wait()
                    for n in range(T * SG):
                        dve.tensor_scalar(g_diag[:, n, :], ident[:], g_rstd[:, n:n + 1], None, ALU.mult).then_inc(ys_ready, 1)
                elif Y_TURN < place <= Y_TURN + 4:
                    for m in range(4 * (place - Y_TURN) - 4, 4 * (place - Y_TURN)):
                        dve.wait_ge(ys_hi, m // 2 * 2 + 2)
                        dve.scalar_tensor_tensor(out=s_lo[:, m, :], in0=misc[:, m // 2 % 4, m % 2 * S:(m % 2 + 1) * S], scalar=g_ssm[:, m:m + 1],
                                                 in1=s_hi[:, m, :].bitcast(F32), op0=ALU.mult, op1=ALU.subtract).then_inc(ys_lo, 1)

            stream(w_out2, add_plain, up2, beside=state_output)
            norm_end(3)

            def finish_up2(b, c):
                for j in range(1, FFN_CONV):
                    for m in range(4):
                        if j == 1:
                            dve.wait_ge(c3_bias, b * 4 + (m // 2 * 2 + 2))
                        else:
                            dve.wait_ge(c3_tap, b * 8 + (m + 1))
                        dst, m0 = ((ff_g, 0), (ff_u, HC))[m // 2]
                        dve.scalar_tensor_tensor(
                            out=dst[:, m % 2, j:S], in0=pair[:, c, m // 2, (m % 2) * S:(m % 2 + 1) * S - j],
                            scalar=vec[:, 4 + FFN_CONV - 1 - j, bass.ds(b * 2 + (m0 + m % 2), 1)], in1=dst[:, m % 2, j:S],
                            op0=ALU.mult, op1=ALU.add).then_inc(c3_tap, 1)
                hidden(b, c, flat(ff_u[:]), up1.blocks)

            stream(up2, finish_up2, down2)
            stream(down2, add_plain, ple_gate)

            norm_end(4)
            for b in range(ple_gate.blocks):
                for n in range(ple_gate.halves):
                    h, more = (LEAD + n) % ple_gate.halves, LEAD + n >= ple_gate.halves
                    if b + more < ple_gate.blocks:
                        split_lo(ple_gate, b + more, [h])
                    if (b, n) == (0, 7):
                        dve.wait_ge(pe_ssq, T)
                        inverse_root(ssq, rstd, pe_v, pe_s, 1)
                if b == 0:
                    dve.wait_ge(post_mm, 1)
                    for t in range(T):
                        dve.scalar_tensor_tensor(out=pe_t[:, t, :], in0=pe_t[:, t, :], scalar=rstd[:, t:t + 1], in1=flat(misc[:]),
                                                 op0=ALU.mult, op1=ALU.mult).then_inc(pe_ready, 1)
                    dve.wait_ge(pe_ready, T)
                cols = slice(b * COLS, (b + 1) * COLS)
                dve.wait_ge(gate_sig, b + 1)
                done(dve.tensor_tensor(sig[:], sig[:], pe_t[:, :, cols], ALU.mult))
                done.wait()
                dve.tensor_tensor(x[:, :, cols], x[:, :, cols], sig[:], ALU.add).then_inc(x_out, 1)


NAMES = ["x", "c", "w_ada", "b_ada", "g_norm_mix", "w_in", "w_conv", "b_conv", "w_rg_a", "b_rg_a", "w_rg_i", "b_rg_i",
         "lru_lambda", "w_pool", "ls_pool", "w_out", "g_norm_ffn", "w_ffn_gate", "w_ffn_up", "w_ffn_down",
         "g_norm_final", "p_2", "positions_2", "attn_norm_g_2", "w_in_2", "conv_w_2", "conv_b_2", "dt_bias_2",
         "a_log_2", "d_skip_2", "ssm_norm_g_2", "q_norm_g_2", "k_norm_g_2", "sinks_2", "w_out_2", "ffn_norm_g_2",
         "w_up_2", "ffn_conv_w_2", "ffn_conv_b_2", "w_down_2", "ple_norm_g_2", "w_ple_gate_2", "w_ple_proj_2",
         "ple_post_g_2"]


def kernel(**inputs):
    from concourse import bacc
    from concourse.bass_utils import run_bass_kernel_spmd

    nc = bacc.Bacc("TRN2", target_bir_lowering=False, num_devices=1, dynamic_dma_scratch_size=1024)
    arrays = {f"in_{name}": np.ascontiguousarray(inputs[name]) for name in NAMES}
    d = {name: nc.dram_tensor(f"in_{name}", a.shape, mybir.dt.from_np(a.dtype), kind="ExternalInput").ap()
         for name, a in zip(NAMES, arrays.values())}
    out = nc.dram_tensor("out", arrays["in_x"].shape, F32, kind="ExternalOutput").ap()
    two_blocks(nc, d, out)
    return run_bass_kernel_spmd(nc, [arrays], core_ids=[0]).results[0]["out"]
```
